# Optimizing a Trainium2 kernel written in Bass

```python
import math
import jax, jax.numpy as jnp
from jax import lax
import numpy as np

D_MODEL = 1024
BATCH = 1
SEQ = 256
DEPTH = 1

CHUNK = 64
D_MIX = D_MODEL
D_CONV = D_MIX // 2
CONV_K = 3
D_SSM = D_MIX - D_CONV
SSM_HEADDIM = 64
SSM_HEADS = D_SSM // SSM_HEADDIM
SSM_GROUPS = 2
SSM_STATE = 128
SSM_CONV_K = 4
D_XBC = D_SSM + 2 * SSM_GROUPS * SSM_STATE
D_IN_PROJ = 3 * D_CONV + D_SSM + D_XBC + SSM_HEADS
N_EXPERTS = 64
TOP_K = 8
N_EXPERT_GROUPS = 8
TOPK_GROUPS = 4
D_EXPERT = 256
D_SHARED = 256
ROUTED_SCALE = 2.5
EPS = 1e-6

kernel_name = "hybrid_conv_ssd_moe_adaln_block"

def rms_norm(x, g):
    xf = x.astype(jnp.float32)
    y = xf * lax.rsqrt(jnp.mean(xf * xf, axis=-1, keepdims=True) + EPS)
    return (y * g.astype(jnp.float32)).astype(x.dtype)

def modulate(h, shift, scale):
    return h * (1 + scale[:, None, :]) + shift[:, None, :]

def causal_dwconv(u, w):
    k, ch = w.shape
    return lax.conv_general_dilated(
        u, w[:, None, :].astype(u.dtype), window_strides=(1,), padding=[(k - 1, 0)],
        dimension_numbers=("NWC", "WIO", "NWC"), feature_group_count=ch)

def segsum(a):
    cs = jnp.cumsum(a, axis=-1)
    n = a.shape[-1]
    diff = cs[..., :, None] - cs[..., None, :]
    return jnp.where(jnp.tril(jnp.ones((n, n), dtype=bool)), diff, -jnp.inf)

def ssd_chunked(xh, dt, A, Bm, Cm):
    b, s, h, p = xh.shape
    g, n = Bm.shape[-2:]
    r = h // g
    nc = s // CHUNK
    x = xh.reshape(b, nc, CHUNK, g, r, p)
    dtc = dt.reshape(b, nc, CHUNK, g, r)
    Bc = Bm.reshape(b, nc, CHUNK, g, n)
    Cc = Cm.reshape(b, nc, CHUNK, g, n)
    a = jnp.moveaxis(dtc * A.reshape(g, r), 2, -1)
    a_cs = jnp.cumsum(a, axis=-1)
    dtx = x * dtc[..., None]
    cb = jnp.einsum("bclgn,bcsgn->bcgls", Cc, Bc)
    wts = cb[:, :, :, None] * jnp.exp(segsum(a))
    y_diag = jnp.einsum("bcgrls,bcsgrp->bclgrp", wts, dtx)
    decay_l = jnp.moveaxis(jnp.exp(a_cs[..., -1:] - a_cs), -1, 2)
    states = jnp.einsum("bclgn,bclgrp->bcgrpn", Bc, dtx * decay_l[..., None])
    chunk_decay = jnp.exp(a_cs[..., -1])

    def step(prev, inp):
        st, dec = inp
        return prev * dec[..., None, None] + st, prev

    init = jnp.zeros((b, g, r, p, n), jnp.float32)
    _, prev_states = lax.scan(step, init, (jnp.moveaxis(states, 1, 0), jnp.moveaxis(chunk_decay, 1, 0)))
    prev_states = jnp.moveaxis(prev_states, 0, 1)
    out_decay = jnp.moveaxis(jnp.exp(a_cs), -1, 2)
    y_off = jnp.einsum("bclgn,bcgrpn->bclgrp", Cc, prev_states) * out_decay[..., None]
    return (y_diag + y_off).reshape(b, s, h, p)

def short_conv_mixer(gate_b, gate_c, u, w):
    return gate_b * causal_dwconv(gate_c * u, w)

def ssd_mixer(z, xbc, dt_raw, conv_w, conv_b, dt_bias, a_log, d_skip, norm_g):
    b, s, _ = z.shape
    xbc = jax.nn.silu(causal_dwconv(xbc, conv_w) + conv_b.astype(xbc.dtype))
    gn = SSM_GROUPS * SSM_STATE
    xs, Bm, Cm = jnp.split(xbc.astype(jnp.float32), [D_SSM, D_SSM + gn], axis=-1)
    dt = jax.nn.softplus(dt_raw.astype(jnp.float32) + dt_bias.astype(jnp.float32))
    A = -jnp.exp(a_log.astype(jnp.float32))
    xh = xs.reshape(b, s, SSM_HEADS, SSM_HEADDIM)
    y = ssd_chunked(xh, dt, A, Bm.reshape(b, s, SSM_GROUPS, SSM_STATE), Cm.reshape(b, s, SSM_GROUPS, SSM_STATE))
    y = y + d_skip.astype(jnp.float32)[:, None] * xh
    y = y.reshape(b, s, D_SSM) * jax.nn.silu(z.astype(jnp.float32))
    return rms_norm(y, norm_g).astype(z.dtype)

def moe_ffn(h, w_router, router_bias, we_gate, we_up, we_down, ws_gate, ws_up, ws_down):
    b, s, d = h.shape
    t = h.reshape(b * s, d)
    scores = jax.nn.sigmoid(jnp.dot(t.astype(jnp.float32), w_router.astype(jnp.float32)))
    sel = scores + router_bias.astype(jnp.float32)
    grp = sel.reshape(-1, N_EXPERT_GROUPS, N_EXPERTS // N_EXPERT_GROUPS)
    grp_score = jnp.sum(lax.top_k(grp, 2)[0], axis=-1)
    _, grp_idx = lax.top_k(grp_score, TOPK_GROUPS)
    grp_mask = jnp.any(grp_idx[..., None] == jnp.arange(N_EXPERT_GROUPS), axis=-2)
    exp_mask = jnp.repeat(grp_mask, N_EXPERTS // N_EXPERT_GROUPS, axis=-1)
    _, idx = lax.top_k(jnp.where(exp_mask, sel, -jnp.inf), TOP_K)
    w = jnp.take_along_axis(scores, idx, axis=-1)
    w = w / jnp.sum(w, axis=-1, keepdims=True) * ROUTED_SCALE
    gates = jnp.sum(jax.nn.one_hot(idx, N_EXPERTS, dtype=jnp.float32) * w[..., None], axis=1).astype(t.dtype)
    out = (jax.nn.silu(t @ ws_gate) * (t @ ws_up)) @ ws_down
    for e in range(N_EXPERTS):
        hid = jax.nn.silu(t @ we_gate[e]) * (t @ we_up[e])
        out = out + gates[:, e:e + 1] * (hid @ we_down[e])
    return out.reshape(b, s, d)

def setup_inputs(seed: int = 0) -> dict:
    key = jax.random.key(seed)
    ks = iter(jax.random.split(key, 32))
    L = DEPTH

    def nrm(shape, scale):
        return jax.random.normal(next(ks), shape, jnp.float32) * scale

    x = nrm((BATCH, SEQ, D_MODEL), 1.0)
    c = nrm((BATCH, D_MODEL), 1.0)
    w_ada = nrm((L, D_MODEL, 6 * D_MODEL), 0.5 * D_MODEL ** -0.5)
    b_ada = nrm((L, 6 * D_MODEL), 0.02)
    norm_mix_g = 1.0 + nrm((L, D_MODEL), 0.02)
    w_in = nrm((L, D_MODEL, D_IN_PROJ), D_MODEL ** -0.5)
    conv_a_w = nrm((L, CONV_K, D_CONV), CONV_K ** -0.5)
    ssm_conv_w = nrm((L, SSM_CONV_K, D_XBC), SSM_CONV_K ** -0.5)
    ssm_conv_b = nrm((L, D_XBC), 0.02)
    dt0 = jnp.exp(jax.random.uniform(next(ks), (L, SSM_HEADS), jnp.float32, math.log(1e-3), math.log(1e-1)))
    ssm_dt_bias = dt0 + jnp.log(-jnp.expm1(-dt0))
    ssm_a_log = jnp.log(jax.random.uniform(next(ks), (L, SSM_HEADS), jnp.float32, 1.0, 16.0))
    ssm_d = 1.0 + nrm((L, SSM_HEADS), 0.1)
    ssm_norm_g = 1.0 + nrm((L, D_SSM), 0.02)
    w_out = nrm((L, D_MIX, D_MODEL), D_MIX ** -0.5)
    norm_ffn_g = 1.0 + nrm((L, D_MODEL), 0.02)
    w_router = nrm((L, D_MODEL, N_EXPERTS), D_MODEL ** -0.5)
    router_bias = nrm((L, N_EXPERTS), 0.01)
    we_gate = nrm((L, N_EXPERTS, D_MODEL, D_EXPERT), D_MODEL ** -0.5)
    we_up = nrm((L, N_EXPERTS, D_MODEL, D_EXPERT), D_MODEL ** -0.5)
    we_down = nrm((L, N_EXPERTS, D_EXPERT, D_MODEL), D_EXPERT ** -0.5)
    ws_gate = nrm((L, D_MODEL, D_SHARED), D_MODEL ** -0.5)
    ws_up = nrm((L, D_MODEL, D_SHARED), D_MODEL ** -0.5)
    ws_down = nrm((L, D_SHARED, D_MODEL), D_SHARED ** -0.5)
    norm_final_g = 1.0 + nrm((D_MODEL,), 0.02)
    return {"x": x, "c": c, "w_ada": w_ada, "b_ada": b_ada, "norm_mix_g": norm_mix_g,
            "w_in": w_in, "conv_a_w": conv_a_w, "ssm_conv_w": ssm_conv_w, "ssm_conv_b": ssm_conv_b,
            "ssm_dt_bias": ssm_dt_bias, "ssm_a_log": ssm_a_log, "ssm_d": ssm_d, "ssm_norm_g": ssm_norm_g,
            "w_out": w_out, "norm_ffn_g": norm_ffn_g, "w_router": w_router, "router_bias": router_bias,
            "we_gate": we_gate, "we_up": we_up, "we_down": we_down,
            "ws_gate": ws_gate, "ws_up": ws_up, "ws_down": ws_down, "norm_final_g": norm_final_g}

def reference(x, c, w_ada, b_ada, norm_mix_g, w_in, conv_a_w, ssm_conv_w, ssm_conv_b,
              ssm_dt_bias, ssm_a_log, ssm_d, ssm_norm_g, w_out, norm_ffn_g, w_router, router_bias,
              we_gate, we_up, we_down, ws_gate, ws_up, ws_down, norm_final_g):
    gn = SSM_GROUPS * SSM_STATE
    cuts = [D_CONV, 2 * D_CONV, 3 * D_CONV, 3 * D_CONV + D_SSM, 3 * D_CONV + D_SSM + D_XBC]
    for l in range(DEPTH):
        mod = (jnp.dot(c.astype(jnp.float32), w_ada[l].astype(jnp.float32)) + b_ada[l].astype(jnp.float32)).astype(x.dtype)
        sh1, sc1, g1, sh2, sc2, g2 = jnp.split(mod, 6, axis=-1)
        h = modulate(rms_norm(x, norm_mix_g[l]), sh1, sc1)
        proj = h @ w_in[l]
        cb, cc, cu, z, xbc, dt_raw = jnp.split(proj, cuts, axis=-1)
        y_a = short_conv_mixer(cb, cc, cu, conv_a_w[l])
        y_b = ssd_mixer(z, xbc, dt_raw, ssm_conv_w[l], ssm_conv_b[l], ssm_dt_bias[l],
                        ssm_a_log[l], ssm_d[l], ssm_norm_g[l])
        x = x + g1[:, None, :] * (jnp.concatenate([y_a, y_b], axis=-1) @ w_out[l])
        h = modulate(rms_norm(x, norm_ffn_g[l]), sh2, sc2)
        x = x + g2[:, None, :] * moe_ffn(h, w_router[l], router_bias[l], we_gate[l], we_up[l], we_down[l],
                                         ws_gate[l], ws_up[l], ws_down[l])
    return rms_norm(x, norm_final_g)


_drawn_inputs = setup_inputs


def setup_inputs(seed=0):
    import zlib

    import numpy as np

    out = dict(_drawn_inputs(seed))
    spreads = {}
    factors = {}
    for name, (base, spread) in spreads.items():
        noise = np.random.default_rng([zlib.crc32(name.encode()), seed]).standard_normal(out[name].shape)
        drawn = base * np.exp(spread * noise) if base else spread * noise
        out[name] = __import__('jax').numpy.asarray(drawn.astype(out[name].dtype))
    for name, factor in factors.items():
        out[name] = (out[name] * factor).astype(out[name].dtype)
    return out
```

```python
from contextlib import ExitStack

import concourse.bass as bass
from concourse import mybir

P = 128
F32 = mybir.dt.float32
BF16 = mybir.dt.bfloat16
U32 = mybir.dt.uint32
ALU = mybir.AluOpType
ACT = mybir.ActivationFunctionType
AX = mybir.AxisListType

D = 1024
KD = D // P
TT = 2
TOK = TT * P
DC = 512
DS = 512
NH = 8
HD = 64
NG = 2
HPG = NH // NG
CBLK = DC // P
XB = (DS + 2 * NG * P) // P
CK = 3
SK = 4
EPS = 1e-6
NE = 64
TOPK = 8
NGR = 8
TOPG = 4
FE = 256
FT = FE // P
ROUTED_SCALE = 2.5

NSLOT = 4
PIECE = 768
LASTP = 776
SLOTW = KD * LASTP
GU = 2 * KD * FE
NADA = 6 * D // PIECE
AHEAD = 2
GRP = 4
NGRP = NE // GRP
TG = NGRP + AHEAD
TE = TG * GRP
NCOL = 5
PASS_GROUPS = NGRP + AHEAD

R_CA, R_CS, R_CB, R_NG, R_NM = 0, CK * CBLK, CK * CBLK + SK * XB, CK * CBLK + SK * XB + XB, 56
R_END = R_NM + KD

A, I, O, S = "ada", "in", "out", "shared"
LOADS = [(A, 0), (A, 1), (A, 2), (I, 3), (I, 2), (A, 3), (I, 1), (A, 4), (I, 0), (A, 5), (A, 6), (A, 7),
         (O, 0), (O, 1), (S, 0)]
E0 = len(LOADS)
OUT_K = [(0, 6), (6, 8)]
ORDER = [18, 19, 20, 21, 22, 23, 12, 13, 14, 15, 16, 17, 6, 7, 8, 9, 10, 11, 0, 1, 2, 3, 4, 5]
NQ = len(ORDER)
QB = 5


def n_dmas(what):
    return 3 if what == S else 1


def slot_of(n):
    return n % NSLOT


def loaded_count(n):
    return 16 * sum(n_dmas(LOADS[m][0]) for m in range(n + 1) if slot_of(m) == slot_of(n))


def slot_base(s):
    return 16 * sum(n_dmas(LOADS[m][0]) for m in range(E0) if slot_of(m) == s)


def build(nc, x, c, w_ada, b_ada, norm_mix_g, w_in, conv_a_w, ssm_conv_w, ssm_conv_b, ssm_dt_bias,
          ssm_a_log, ssm_d, ssm_norm_g, w_out, norm_ffn_g, w_router, router_bias, we_gate, we_up,
          we_down, ws_gate, ws_up, ws_down, norm_final_g, out):
    with ExitStack() as ctx:
        def sb(name, shape, dt=F32):
            return ctx.enter_context(nc.sbuf_tensor(name, shape, dt))

        def sem(name):
            return ctx.enter_context(nc.semaphore(name))

        h2_dram = nc.dram_tensor("h2_rows", [TOK, D], F32, kind="Internal").ap()
        y_dram = nc.dram_tensor("expert_rows", [TOK * TOPK, D], F32, kind="Internal").ap()

        ring = sb("ring", [P, NSLOT, SLOTW])
        X = sb("X", [P, TT, D])
        hT = sb("hT", [P, KD, TOK])
        MOD = sb("MOD", [P, 6 * D])
        gffn = sb("gffn", [P, D])
        gfin = sb("gfin", [P, D])
        arena = sb("arena", [P, 13352])
        ident = sb("ident", [P, P])
        tri = sb("tri", [P, P])
        ones = sb("ones", [P, P])
        trib = sb("trib", [P, P], BF16)
        onesb = sb("onesb", [P, P], BF16)
        slots = sb("slots", [P, 2, P])
        WR = sb("WR", [P, KD, NE])
        prm = sb("prm", [R_END, P])
        COL = sb("COL", [P, R_END])
        ccol = sb("ccol", [P, KD])
        rbias = sb("rbias", [P, NE])
        hrow = sb("hrow", [P, 2, NH])
        dskip = sb("dskip", [P, CBLK])
        small = sb("small", [P, 16])
        dtv = sb("dtv", [P, 10, TT * NH])
        csv = sb("csv", [P, 4 * NH])
        AB1 = sb("AB1", [P, 2 * KD])
        lower = sb("lower", [P, NGR, NGR])
        tokid = sb("tokid", [P, TT])
        rankm = sb("rankm", [P, TT, TE])
        RT = sb("RT", [P, TT, TE, NCOL], BF16)
        gidx = sb("gidx", [P, TE], U32)
        sidx = sb("sidx", [P, TE], U32)
        gate = sb("gate", [P, TE])
        gi = sb("gi", [P, 2, 1], U32)
        si = sb("si", [P, 2, 1], U32)
        spare = sb("spare", [P, 2])
        oflag = sb("oflag", [P, 1], U32)
        PS = ctx.enter_context(nc.psum_tensor("PS", [P, 8, 512], F32))

        o = [0]

        def part(n):
            o[0] += n
            return arena[:, o[0] - n:o[0]]

        XPf = part(XB * 260)
        XP = XPf.rearrange("p (b n) -> p b n", b=XB)
        CU = XPf[:, 0:CBLK * TOK].rearrange("p (b n) -> p b n", b=CBLK)
        CB = XPf[:, CBLK * TOK:2 * CBLK * TOK].rearrange("p (b n) -> p b n", b=CBLK)
        XC = part(XB * TOK).rearrange("p (b n) -> p b n", b=XB)
        SZ = part(CBLK * TOK).rearrange("p (b n) -> p b n", b=CBLK)
        CC = part(CBLK * 258).rearrange("p (b n) -> p b n", b=CBLK)
        DTX = part(TT * DS).rearrange("p (t n) -> p t n", t=TT)
        Ef = part(3 * NH * P)
        E = Ef.rearrange("p (v h n) -> p v h n", v=3, h=NH)
        YC = part(KD * TOK).rearrange("p (b n) -> p b n", b=KD)
        CBT = part(3 * NG * P).rearrange("p (v g n) -> p v g n", v=3, g=NG)
        XN = YC.rearrange("p b n -> p (b n)").rearrange("p (t n) -> p t n", t=TT)
        T1 = Ef[:, 0:2 * D].rearrange("p (t n) -> p t n", t=TT)
        SQ = Ef[:, 0:CBLK * TOK].rearrange("p (b n) -> p b n", b=CBLK)
        RSB = Ef[:, CBLK * TOK:CBLK * TOK + 2 * TOK].rearrange("p (b n) -> p b n", b=2)
        AB = MOD[:, 0:TT * NH * P].rearrange("p (t h n) -> p t h n", t=TT, h=NH)
        o[0] = 0
        HG = part(2 * D).rearrange("p (b n) -> p b n", b=2)
        XT = part(2 * D).rearrange("p (b k n) -> p b k n", b=2, k=KD)
        YS = part(2 * D).rearrange("p (b n) -> p b n", b=2)
        HID = part(2 * FE).rearrange("p (b n) -> p b n", b=2)
        HTT = part(FE).rearrange("p (c n) -> p c n", c=FT)
        SG = part(2 * FE).rearrange("p (b n) -> p b n", b=2)
        o[0] = 9256
        H2P = part(2 * D).rearrange("p (t n) -> p t n", t=TT)
        SH = part(2 * D).rearrange("p (t n) -> p t n", t=TT)
        o2 = [0]

        def mpart(n):
            o2[0] += n
            return MOD[:, o2[0] - n:o2[0]]

        W64 = TT * NE
        score = mpart(W64).rearrange("p (t e) -> p t e", t=TT)
        sel = mpart(W64).rearrange("p (t e) -> p t e", t=TT)
        msel = mpart(W64).rearrange("p (t e) -> p t e", t=TT)
        maskf = mpart(W64).rearrange("p (t e) -> p t e", t=TT)
        gates = mpart(W64).rearrange("p (t e) -> p t e", t=TT)
        cumA = mpart(TT * 96).rearrange("p (t e) -> p t e", t=TT)
        cumB = mpart(TT * 96).rearrange("p (t e) -> p t e", t=TT)
        top8 = mpart(TT * NGR * 8).rearrange("p (t g j) -> p t g j", t=TT, g=NGR)
        gs = mpart(TT * NGR).rearrange("p (t g) -> p t g", t=TT)
        grank = mpart(TT * NGR).rearrange("p (t g) -> p t g", t=TT)
        gpair = mpart(TT * NGR * NGR).rearrange("p (t g j) -> p t g j", t=TT, g=NGR)
        gpair2 = mpart(TT * NGR * NGR).rearrange("p (t g j) -> p t g j", t=TT, g=NGR)
        m8 = mpart(TT * 8).rearrange("p (t j) -> p t j", t=TT)
        maskb = sb("maskb", [P, TT, NE], BF16)
        rcur = sb("rcur", [P, TT, GRP])
        onehot = mpart(TT * GRP * P // 2).bitcast(BF16).rearrange("p (t e n) -> p t e n", t=TT, e=GRP)
        rtcur = sb("rtcur", [P, TT, GRP, NCOL], BF16)
        dec = sb("dec", [P, 2, GRP])

        loaded = [sem(f"loaded{s}") for s in range(NSLOT)]
        x_in = sem("x_in")
        bada_in = sem("bada_in")
        small_in = sem("small_in")
        params_in = sem("params_in")
        gains_in = sem("gains_in")
        mod_zero = sem("mod_zero")
        consts = sem("consts")
        ss_ready = sem("ss_ready")
        ms_ready = sem("ms_ready")
        std_ready = sem("std_ready")
        rstd_ready = sem("rstd_ready")
        xn_ready = sem("xn_ready")
        xnT_ps = sem("xnT_ps")
        xnT_ready = sem("xnT_ready")
        prm_ps = sem("prm_ps")
        col_ready = sem("col_ready")
        ada_acc = sem("ada_acc")
        modcol_ps = sem("modcol_ps")
        modrow_ps = sem("modrow_ps")
        modrow_ready = sem("modrow_ready")
        h1_ready = sem("h1_ready")
        dt_ps = sem("dt_ps")
        exp_in = sem("exp_in")
        exp_out = sem("exp_out")
        a_ready = sem("a_ready")
        cs_ps = sem("cs_ps")
        cs_ready = sem("cs_ready")
        csrow_ps = sem("csrow_ps")
        csrow_used = sem("csrow_used")
        decay_in = sem("decay_in")
        decay_ready = sem("decay_ready")
        proj_mm = sem("proj_mm")
        proj_evac = sem("proj_evac")
        conv_ready = sem("conv_ready")
        xbc_ready = sem("xbc_ready")
        xsT_ps = sem("xsT_ps")
        dtx_ready = sem("dtx_ready")
        cb_ps = sem("cb_ps")
        cb_used = sem("cb_used")
        wts_ready = sem("wts_ready")
        y_ps = sem("y_ps")
        y_used = sem("y_used")
        sq_ready = sem("sq_ready")
        yss_ps = sem("yss_ps")
        yms_ready = sem("yms_ready")
        ystd_ready = sem("ystd_ready")
        yb_ready = sem("yb_ready")
        ya_ready = sem("ya_ready")
        mix_ps = sem("mix_ps")
        wout_used = sem("wout_used")
        x2_ready = sem("x2_ready")
        h2_ready = sem("h2_ready")
        h2_stored = sem("h2_stored")
        h2T_ps = sem("h2T_ps")
        h2T_ready = sem("h2T_ready")
        logit_ps = sem("logit_ps")
        score_ready = sem("score_ready")
        mask_ready = sem("mask_ready")
        rank_ps = sem("rank_ps")
        table_ready = sem("table_ready")
        sgu_ps = sem("sgu_ps")
        ssg_ready = sem("ssg_ready")
        shid_ready = sem("shid_ready")
        shT_ps = sem("shT_ps")
        shT_ready = sem("shT_ready")
        sy_ps = sem("sy_ps")
        sh_ready = sem("sh_ready")
        cur_copied = sem("cur_copied")
        onehot_ready = sem("onehot_ready")
        slot_ps = sem("slot_ps")
        dec_step = sem("dec_step")
        slot_ready = sem("slot_ready")
        gi_ready = sem("gi_ready")
        si_ready = sem("si_ready")
        gathered = [sem(f"gathered{b}") for b in range(2)]
        xT_ps = sem("xT_ps")
        xT_ready = sem("xT_ready")
        gu_ps = sem("gu_ps")
        sg_ready = sem("sg_ready")
        hg_ready = sem("hg_ready")
        hid_ready = sem("hid_ready")
        hidT_ps = sem("hidT_ps")
        hidT_ready = sem("hidT_ready")
        expert_done = sem("expert_done")
        y_ready = sem("y_ready")
        scattered = [sem(f"scattered{b}") for b in range(2)]
        moe_done = sem("moe_done")
        y_loaded = [sem(f"y_loaded{s}") for s in range(4)]
        fin_ss = sem("fin_ss")
        fin_ms = sem("fin_ms")
        fin_std = sem("fin_std")
        out_ready = sem("out_ready")
        stored = sem("stored")
        act_step = sem("act_step")
        dve_step = sem("dve_step")
        pool_step = sem("pool_step")

        block = ctx.enter_context(nc.Block())

        def bank(b):
            return PS[:, b, :]

        def ada_w(n):
            return ring[:, slot_of(n), 0:KD * PIECE].rearrange("p (k n) -> p k n", k=KD)

        def load_no(what, j):
            return LOADS.index((what, j))

        def gu_w(s):
            return ring[:, s, 0:GU].rearrange("p (a k n) -> p a k n", a=2, k=KD)

        def down_w(s):
            return ring[:, s, GU:GU + FT * D].rearrange("p (c n) -> p c n", c=FT)

        def e_slot(u):
            return (E0 + u) % NSLOT

        def number(pas, i, u):
            return i * GRP + (NE * pas + u)

        @block.sync
        def _(sp):
            def load_expert(s, wg, wu, wd):
                sp.dma_start(ring[:, s, 0:GU // 2], wg.rearrange("(p k) n -> p (k n)", p=P)).then_inc(loaded[s], 16)
                sp.dma_start(ring[:, s, GU // 2:GU], wu.rearrange("(p k) n -> p (k n)", p=P)).then_inc(loaded[s], 16)
                sp.dma_start(ring[:, s, GU:GU + FT * D],
                             wd.rearrange("(p c) n -> p (c n)", p=P)).then_inc(loaded[s], 16)

            sp.dma_start(X[:], x[0].rearrange("(t p) d -> p t d", p=P)).then_inc(x_in, 16)
            ada_order = [j for w, j in LOADS if w == A]
            freed = {}
            nin = 0
            for n, (what, j) in enumerate(LOADS):
                if what == A:
                    freed[n] = (ada_acc, ada_order.index(j) + 1)
                elif what == I:
                    nin += 1
                    freed[n] = (proj_mm, 6 * nin)
                elif what == O:
                    freed[n] = (wout_used, 1) if j == 0 else (mix_ps, 2 * TT)
            for n, (what, j) in enumerate(LOADS):
                s = slot_of(n)
                if n >= NSLOT:
                    sp.wait_ge(*freed[n - NSLOT])
                if what == A:
                    sp.dma_start(ada_w(n), w_ada[0, :, PIECE * j:PIECE * j + PIECE]
                                 .rearrange("(p k) n -> p k n", p=P)).then_inc(loaded[s], 16)
                elif what == I:
                    w = LASTP if j == 3 else PIECE
                    sp.dma_start(ring[:, s, 0:KD * w].rearrange("p (k n) -> p k n", k=KD),
                                 w_in[0, :, PIECE * j:PIECE * j + w]
                                 .rearrange("(k p) n -> p k n", p=P)).then_inc(loaded[s], 16)
                elif what == O:
                    k0, k1 = OUT_K[j]
                    sp.dma_start(ring[:, s, 0:(k1 - k0) * D].rearrange("p (k n) -> p k n", n=D),
                                 w_out[0, k0 * P:k1 * P, :].rearrange("(k p) n -> p k n", p=P)
                                 ).then_inc(loaded[s], 16)
                else:
                    load_expert(s, ws_gate[0], ws_up[0], ws_down[0])
            for u in range(GRP):
                n = E0 + u
                if LOADS[n - NSLOT][0] == S:
                    sp.wait_ge(sy_ps, TT)
                else:
                    sp.wait_ge(*freed[n - NSLOT])
                load_expert(e_slot(u), we_gate[0, u], we_up[0, u], we_down[0, u])

            def load_group(pas, i, first):
                for u in range(GRP):
                    sp.wait_ge(expert_done, number(pas, i, u) - (NSLOT - 1))
                    e = i * GRP + u
                    load_expert(e_slot(u), we_gate[0, e], we_up[0, e], we_down[0, e])

            with sp.Fori(1, NGRP) as i:
                load_group(0, i, False)
            sp.wait_ge(table_ready, 1)
            over = sp.value_load(oflag[0:1, 0:1], min_val=0, max_val=1)
            with sp.If(over > 0):
                load_group(1, 0, True)
                with sp.Fori(1, NGRP) as i:
                    load_group(1, i, False)
            with sp.Else():
                sp.nop()
            sp.wait_ge(moe_done, 1)
            for t in range(TT):
                for h in range(2):
                    s = 2 * t + h
                    sp.dma_start(ring[:, s, 0:4 * D],
                                 y_dram.rearrange("(t p j) d -> t p j d", t=TT, p=P)[t, :, 4 * h:4 * h + 4, :]
                                 .rearrange("p j d -> p (j d)")).then_inc(y_loaded[s], 16)
            for t in range(TT):
                sp.wait_ge(out_ready, t + 1)
                sp.dma_start(out[0, t * P:(t + 1) * P, :], X[:, t, :]).then_inc(stored, 16)
            sp.wait_ge(stored, 16 * TT)

        @block.gpsimd
        def _(pool):
            count = [0]

            def link(ins):
                count[0] += 1
                ins.then_inc(pool_step, 1)
                pool.wait_ge(pool_step, count[0])

            pool.memset(MOD[:], 0.0).then_inc(mod_zero, 1)
            link(pool.memset(ident[:], 0.0))
            link(pool.affine_select(out=ident[:], in_=ident[:], compare_op=ALU.not_equal, fill=1.0, base=0,
                                    pattern=[[-1, P]], channel_multiplier=1))
            link(pool.memset(ones[:], 1.0))
            link(pool.affine_select(out=tri[:], in_=ones[:], compare_op=ALU.is_ge, fill=0.0, base=0,
                                    pattern=[[1, P]], channel_multiplier=-1))
            link(pool.memset(onesb[:], 1.0))
            link(pool.affine_select(out=trib[:], in_=onesb[:], compare_op=ALU.is_ge, fill=0.0, base=-1,
                                    pattern=[[1, P]], channel_multiplier=-1))
            link(pool.memset(lower[:], 1.0))
            link(pool.affine_select(out=lower[:], in_=lower[:], compare_op=ALU.is_ge, fill=0.0, base=-1,
                                    pattern=[[1, NGR], [-1, NGR]], channel_multiplier=0))
            link(pool.iota(slots[:], pattern=[[P, 2], [1, P]], base=0, channel_multiplier=0,
                           allow_small_or_imprecise_dtypes=True))
            link(pool.iota(tokid[:], pattern=[[P, TT]], base=-TOK, channel_multiplier=1,
                           allow_small_or_imprecise_dtypes=True))
            link(pool.memset(spare[:], 0.0))
            link(pool.memset(rankm[:], -1.0))
            link(pool.memset(RT[:], 0.0))
            link(pool.memset(XPf, 0.0))
            pool.memset(CC, 0.0).then_inc(consts, 1)

            pool.wait_ge(table_ready, 2)
            pool.wait_ge(h2T_ready, 4)
            pool.wait_ge(h2_stored, 16)
            link(pool.memset(HG, 0.0))

            last_token = pool.to_reg(TOK - 1)
            last_row = pool.to_reg(TOK * TOPK - 1)

            def carry_wait():
                pool.tensor_tensor(spare[:, 1:2], spare[:, 0:1], spare[:, 0:1], ALU.add)

            def stage_group(pas, g, first):
                n = g + PASS_GROUPS * pas
                if not first:
                    pool.wait_ge(slot_ps, n)
                cols = bass.ds(g * GRP, GRP)
                pool.tensor_copy(rcur[:], rankm[:, :, cols]).then_inc(cur_copied, 1)
                pool.tensor_copy(rtcur[:], RT[:, :, cols, :]).then_inc(cur_copied, 1)

            def gather(pas, i, u, first=False):
                n = number(pas, i, u)
                b = u % 2
                if u % GRP == 0 or first:
                    pool.wait_ge(slot_ready, (i + (PASS_GROUPS * pas + u // GRP + 1)) * 3)
                if not first:
                    pool.wait_ge(xT_ps, n - 1)
                pool.tensor_copy(gi[:, b, :], gidx[:, bass.ds(i * GRP + u, 1)]).then_inc(gi_ready, 1)
                pool.wait_ge(gi_ready, n + 1)
                carry_wait()
                pool.indirect_dma_start(out=HG[:, b, :], out_offset=None, in_=h2_dram[:],
                                        in_offset=bass.IndirectOffsetOnAxis(ap=gi[:, b, :], axis=0),
                                        bounds_check=last_token, oob_is_err=False).then_inc(gathered[b], 16)

            def scatter(pas, i, u):
                n = number(pas, i, u)
                b = u % 2
                pool.wait_ge(y_ready, n * 2 + 2)
                pool.tensor_copy(si[:, b, :], sidx[:, bass.ds(i * GRP + u, 1)]).then_inc(si_ready, 1)
                pool.wait_ge(si_ready, n + 1)
                carry_wait()
                pool.indirect_dma_start(out=y_dram[:], out_offset=bass.IndirectOffsetOnAxis(ap=si[:, b, :], axis=0),
                                        in_=YS[:, b, :], in_offset=None, bounds_check=last_row,
                                        oob_is_err=False).then_inc(scattered[b], 16)

            def group(pas, i, last=False):
                for u in range(GRP):
                    if u == 1 and not last:
                        stage_group(pas, i + AHEAD, False)
                    if not (last and u + 3 >= GRP):
                        gather(pas, i, u + 3)
                    if u < 2:
                        if pas == 0 and isinstance(i, int) and i == 0:
                            pass
                        else:
                            pool.wait_ge(scattered[u % 2], (i * 2 + 32 * pas) * 16)
                    else:
                        pool.wait_ge(scattered[u % 2], (i * 2 + (32 * pas + 1)) * 16)
                    scatter(pas, i, u)

            def run_pass(pas):
                stage_group(pas, 0, pas == 0)
                stage_group(pas, 1, False)
                for u in range(2):
                    gather(pas, 0, u, first=True)
                gather(pas, 0, 2)
                group(pas, 0)
                with pool.Fori(1, NGRP - 1) as i:
                    group(pas, i)
                group(pas, NGRP - 1, last=True)
                for b in range(2):
                    pool.wait_ge(scattered[b], 16 * 32 * (pas + 1))

            run_pass(0)
            over = pool.value_load(oflag[0:1, 0:1], min_val=0, max_val=1)
            with pool.If(over > 0):
                run_pass(1)
            with pool.Else():
                pool.nop()
            pool.memset(rcur[:], 0.0).then_inc(moe_done, 1)

        @block.scalar
        def _(act):
            count = [0]

            def link(ins):
                count[0] += 1
                ins.then_inc(act_step, 1)
                act.wait_ge(act_step, count[0])

            act.dma_start(ccol[:], c[0].rearrange("(p k) -> p k", p=P)).then_inc(small_in, 16)
            act.dma_start(prm[R_CA:R_CS, :], conv_a_w[0].rearrange("k (b q) -> (k b) q", q=P)).then_inc(params_in, 16)
            act.dma_start(prm[R_CS:R_CB, :], ssm_conv_w[0].rearrange("k (b q) -> (k b) q", q=P)).then_inc(params_in, 16)
            act.dma_start(prm[R_CB:R_NG, :], ssm_conv_b[0].rearrange("(b q) -> b q", q=P)).then_inc(params_in, 16)
            act.dma_start(prm[R_NG:R_NM, :], ssm_norm_g[0].rearrange("(b q) -> b q", q=P)).then_inc(params_in, 16)
            act.dma_start(prm[R_NM:R_END, :], norm_mix_g[0].rearrange("(b q) -> b q", q=P)).then_inc(params_in, 16)
            act.wait_ge(mod_zero, 1)
            act.dma_start(MOD[0:1, :], b_ada[0:1, :]).then_inc(bada_in, 16)
            act.dma_start(hrow[:, 0, :], ssm_dt_bias[0].partition_broadcast(P)).then_inc(small_in, 16)
            act.dma_start(hrow[:, 1, :], ssm_a_log[0].partition_broadcast(P)).then_inc(small_in, 16)
            for half in range(2):
                act.dma_start(dskip[HD * half:HD * half + HD, :],
                              ssm_d[0].rearrange("(b q) -> q b", q=2)[half].partition_broadcast(HD),
                              allow_slow_non_contiguous=True).then_inc(small_in, 16)
            act.dma_start(rbias[:], router_bias[0].partition_broadcast(P)).then_inc(small_in, 16)
            act.dma_start(WR[:], w_router[0].rearrange("(p k) n -> p k n", p=P)).then_inc(gains_in, 16)
            act.dma_start(gffn[:], norm_ffn_g[0].partition_broadcast(P)).then_inc(gains_in, 16)
            act.dma_start(gfin[:], norm_final_g.partition_broadcast(P)).then_inc(gains_in, 16)

            act.wait_ge(x_in, 16)
            for t in range(TT):
                act.activation(XN[:, t, :], X[:, t, :], ACT.Square, accum_out=small[:, t:t + 1]).then_inc(ss_ready, 1)
            act.wait_ge(ms_ready, 1)
            act.activation(small[:, 4:6], small[:, 2:4], ACT.Sqrt).then_inc(std_ready, 1)
            act.wait_ge(rstd_ready, 1)
            act.wait_ge(ss_ready, TT)
            for t in range(TT):
                act.activation(XN[:, t, :], X[:, t, :], ACT.Copy, scale=small[:, 6 + t:7 + t]).then_inc(xn_ready, 1)
            act.wait_ge(prm_ps, 1)
            act.copy(COL[:], PS[:, 7, 0:R_END]).then_inc(col_ready, 1)
            act.wait_ge(xnT_ps, 1)
            for b in range(4):
                act.copy(hT[:, 2 * b:2 * b + 2, :].rearrange("p k n -> p (k n)"), bank(2 + b)).then_inc(xnT_ready, 1)

            def exp_step(n, dst, src):
                act.wait_ge(exp_in, n)
                act.activation(dst, src, ACT.Exp).then_inc(exp_out, 1)

            act.wait_ge(small_in, 16 * 6)
            act.activation(dtv[:, 8, 0:NH], hrow[:, 1, :], ACT.Exp).then_inc(exp_out, 1)
            exp_step(1, dtv[:, 2, :], dtv[:, 1, :])

            nconv = [0]

            def silu_conv(b):
                nconv[0] += 1
                act.wait_ge(conv_ready, nconv[0])
                act.activation(XC[:, b, :], XC[:, b, :], ACT.Silu,
                               bias=COL[:, R_CB + b:R_CB + b + 1]).then_inc(xbc_ready, 1)

            act.wait_ge(consts, 1)
            for q, m in enumerate(ORDER):
                if m < 4 or (8 <= m < 12):
                    act.wait_ge(conv_ready, XB)
                act.wait_ge(proj_mm, q + 1)
                src = PS[:, 2 + q % QB, 0:TOK]
                if m >= 16:
                    act.copy(XP[:, m - 16, SK - 1:SK - 1 + TOK], src).then_inc(proj_evac, 1)
                elif m >= 12:
                    act.activation(SZ[:, m - 12, :], src, ACT.Silu).then_inc(proj_evac, 1)
                elif m >= 8:
                    act.copy(CU[:, m - 8, :], src).then_inc(proj_evac, 1)
                elif m >= 4:
                    act.copy(CC[:, m - 4, CK - 1:CK - 1 + TOK], src).then_inc(proj_evac, 1)
                else:
                    act.copy(CB[:, m, :], src).then_inc(proj_evac, 1)
                if q == 9:
                    for b in range(2, 8):
                        silu_conv(b)
                if q == 11:
                    for b in range(2):
                        silu_conv(b)
                if q == 14:
                    for v in range(3):
                        act.wait_ge(decay_in, v + 1)
                        act.activation(E[:, v, :, :], E[:, v, :, :], ACT.Exp).then_inc(decay_ready, 1)
            act.wait_ge(yms_ready, 1)
            act.activation(RSB[:, 0, :], RSB[:, 0, :], ACT.Sqrt).then_inc(ystd_ready, 1)
            for r in range(8):
                act.wait_ge(modrow_ps, r + 1)
                act.copy(MOD[:, 2 * D + 512 * r:2 * D + 512 * r + 512], bank(r % 2)).then_inc(modrow_ready, 1)
            for t in range(TT):
                act.wait_ge(x2_ready, 2 * t + 2)
                act.activation(T1[:, t, :], X[:, t, :], ACT.Square,
                               accum_out=small[:, t:t + 1]).then_inc(ss_ready, 1)
            act.wait_ge(ms_ready, 2)
            act.activation(small[:, 4:6], small[:, 2:4], ACT.Sqrt).then_inc(std_ready, 1)
            act.wait_ge(h2_ready, TT)
            act.dma_start(h2_dram.rearrange("(t p) d -> p t d", p=P), H2P).then_inc(h2_stored, 16)
            for b in range(4):
                act.wait_ge(h2T_ps, b + 1)
                act.copy(hT[:, 2 * b:2 * b + 2, :].rearrange("p k n -> p (k n)"), bank(2 + b)).then_inc(h2T_ready, 1)
            act.wait_ge(logit_ps, 1)
            act.activation(score, PS[:, 7, 0:TT * NE].rearrange("p (t e) -> p t e", t=TT),
                           ACT.Sigmoid).then_inc(score_ready, 1)
            for t in range(TT):
                act.wait_ge(sgu_ps, t + 1)
                act.activation(SG[:, t, :], PS[:, 2 + t, 0:FE], ACT.Silu).then_inc(ssg_ready, 1)
            for t in range(TT):
                act.wait_ge(shT_ps, t + 1)
                act.copy(HTT.rearrange("p c n -> p (c n)"), PS[:, 6, 0:FE]).then_inc(shT_ready, 1)
                act.wait_ge(sy_ps, t + 1)
                act.copy(SH[:, t, :].rearrange("p (a n) -> p a n", a=2), PS[:, 4:6, :]).then_inc(sh_ready, 1)

            def copy_xT(n, u):
                act.wait_ge(xT_ps, n + 1)
                act.copy(XT[:, u % 2, 0:4, :].rearrange("p k n -> p (k n)"), bank(0)).then_inc(xT_ready, 1)

            def silu_gate(n, u):
                act.wait_ge(gu_ps, n + 1)
                act.activation(SG[:, u % 2, :], PS[:, 2 + u % 2, 0:FE], ACT.Silu).then_inc(sg_ready, 1)

            def group(pas, i, last=False):
                for u in range(GRP):
                    n = number(pas, i, u)
                    if not (last and u == 3):
                        act.wait_ge(hid_ready, n)
                        silu_gate(n + 1, u + 1)
                    act.wait_ge(hidT_ps, n + 1)
                    act.copy(HTT.rearrange("p c n -> p (c n)"), PS[:, 6, 0:FE]).then_inc(hidT_ready, 1)
                    if not (last and u >= 2):
                        copy_xT(n + 2, u)
                    act.wait_ge(expert_done, n + 1)
                    if u >= 2:
                        act.wait_ge(scattered[u % 2], (i * 2 + (32 * pas + 1)) * 16)
                    elif not (isinstance(i, int) and i == 0 and pas == 0):
                        act.wait_ge(scattered[u % 2], (i * 2 + 32 * pas) * 16)
                    act.copy(YS[:, u % 2, 0:512], bank(4)).then_inc(y_ready, 1)

            def run_pass(pas):
                n = NE * pas
                copy_xT(n, 0)
                silu_gate(n, 0)
                copy_xT(n + 1, 1)
                group_first(pas)
                with act.Fori(1, NGRP - 1) as i:
                    group(pas, i)
                group(pas, NGRP - 1, last=True)

            def group_first(pas):
                group(pas, 0)

            run_pass(0)
            over = act.value_load(oflag[0:1, 0:1], min_val=0, max_val=1)
            with act.If(over > 0):
                run_pass(1)
            with act.Else():
                act.nop()
            for t in range(TT):
                act.wait_ge(fin_ss, t + 1)
                act.activation(SH[:, t, :], X[:, t, :], ACT.Square, accum_out=small[:, t:t + 1]).then_inc(ss_ready, 1)
                act.wait_ge(fin_ms, t + 1)
                act.activation(small[:, 4 + t:5 + t], small[:, 2 + t:3 + t], ACT.Sqrt).then_inc(fin_std, 1)

        @block.vector
        def _(dve):
            counts = {}

            def signal(ins, s):
                ins.then_inc(s, 1)
                counts[id(s)] = counts.get(id(s), 0) + 1
                return counts[id(s)]

            def link(ins, s=None):
                s = dve_step if s is None else s
                dve.wait_ge(s, signal(ins, s))

            def rstd(col, n):
                dve.wait_ge(ss_ready, TT * n)
                link(dve.tensor_scalar(small[:, 2:4], small[:, 0:2], 1.0 / D, EPS, ALU.mult, ALU.add), ms_ready)
                dve.wait_ge(std_ready, n)
                link(dve.reciprocal(small[:, col:col + 2], small[:, 4:6]), rstd_ready)

            rstd(6, 1)

            def ada(j):
                n = load_no(A, j)
                w = ada_w(n)
                dve.wait_ge(loaded[slot_of(n)], loaded_count(n))
                dst = MOD[:, PIECE * j:PIECE * j + PIECE]
                for k in range(KD):
                    ins = dve.scalar_tensor_tensor(out=dst, in0=w[:, k, :], scalar=ccol[:, k:k + 1], in1=dst,
                                                   op0=ALU.mult, op1=ALU.add)
                    link(ins, ada_acc if k == KD - 1 else None)

            dve.wait_ge(bada_in, 16)
            dve.wait_ge(small_in, 16 * 6)
            for j in range(3):
                ada(j)
            dve.wait_ge(modcol_ps, 1)
            dve.wait_ge(col_ready, 1)
            link(dve.scalar_tensor_tensor(out=AB1[:, 0:KD], in0=PS[:, 0, KD:2 * KD], scalar=1.0,
                                          in1=COL[:, R_NM:R_END], op0=ALU.add, op1=ALU.mult))
            link(dve.tensor_copy(AB1[:, KD:2 * KD], PS[:, 0, 0:KD]))
            dve.wait_ge(xnT_ready, 4)
            for k in range(KD):
                signal(dve.tensor_scalar(hT[:, k, :], hT[:, k, :], AB1[:, k:k + 1], AB1[:, KD + k:KD + k + 1],
                                         ALU.mult, ALU.add), h1_ready)

            s_, n_, u_, w_, z_, z2_, p_, dt_, a_ = (dtv[:, i, :] for i in (0, 1, 2, 3, 4, 5, 6, 7, 9))
            dve.wait_ge(dt_ps, 1)
            link(dve.tensor_tensor(s_.rearrange("p (t h) -> p t h", t=TT),
                                   PS[:, 7, 0:TT * NH].rearrange("p (t h) -> p t h", t=TT),
                                   hrow[:, 0, :].unsqueeze(1).to_broadcast([P, TT, NH]), ALU.add))
            link(dve.tensor_scalar(n_, s_, -1.0, None, ALU.mult))
            link(dve.tensor_tensor(n_, n_, s_, ALU.min), exp_in)
            link(dve.tensor_scalar(s_, s_, 0.0, None, ALU.max))
            dve.wait_ge(exp_out, 2)
            link(dve.tensor_scalar(w_, u_, 2.0, None, ALU.add))
            link(dve.reciprocal(w_, w_))
            link(dve.tensor_tensor(z_, u_, w_, ALU.mult))
            link(dve.tensor_tensor(z2_, z_, z_, ALU.mult))
            link(dve.tensor_scalar(p_, z2_, 1.0 / 17, None, ALU.mult))
            for c_ in (15, 13, 11, 9, 7, 5, 3):
                link(dve.scalar_tensor_tensor(out=p_, in0=p_, scalar=1.0 / c_, in1=z2_, op0=ALU.add, op1=ALU.mult))
            link(dve.scalar_tensor_tensor(out=p_, in0=p_, scalar=1.0, in1=z_, op0=ALU.add, op1=ALU.mult))
            link(dve.scalar_tensor_tensor(out=dt_, in0=p_, scalar=2.0, in1=s_, op0=ALU.mult, op1=ALU.add))
            link(dve.scalar_tensor_tensor(out=a_.rearrange("p (t h) -> p t h", t=TT),
                                          in0=dt_.rearrange("p (t h) -> p t h", t=TT), scalar=-1.0,
                                          in1=dtv[:, 8, 0:NH].unsqueeze(1).to_broadcast([P, TT, NH]),
                                          op0=ALU.mult, op1=ALU.mult))
            link(dve.tensor_copy(AB.rearrange("p t h n -> p (t h) n"),
                                 a_.unsqueeze(2).to_broadcast([P, TT * NH, P])), a_ready)

            evac = {m: q + 1 for q, m in enumerate(ORDER)}

            def conv(b):
                dve.wait_ge(proj_evac, evac[16 + b])
                w = [COL[:, R_CS + k * XB + b:R_CS + k * XB + b + 1] for k in range(SK)]
                link(dve.tensor_scalar(XC[:, b, :], XP[:, b, 0:TOK], w[0], None, ALU.mult))
                for k in range(1, SK):
                    link(dve.scalar_tensor_tensor(out=XC[:, b, :], in0=XP[:, b, k:k + TOK], scalar=w[k],
                                                  in1=XC[:, b, :], op0=ALU.mult, op1=ALU.add),
                         conv_ready if k == SK - 1 else None)

            for b in range(2, 8):
                conv(b)
            dve.wait_ge(cs_ps, 1)
            link(dve.tensor_copy(csv[:, 0:3 * NH], PS[:, 7, 32:32 + 3 * NH]))
            link(dve.tensor_tensor(csv[:, 3 * NH:4 * NH], csv[:, 2 * NH:3 * NH], csv[:, 0:NH], ALU.subtract), cs_ready)
            ada(3)
            for b in range(2):
                conv(b)
            dve.wait_ge(xsT_ps, 1)
            for t in range(TT):
                signal(dve.tensor_tensor(DTX[:, t, :].rearrange("p (h n) -> p h n", h=NH),
                                         bank(t).rearrange("p (h n) -> p h n", h=NH),
                                         dt_[:, t * NH:(t + 1) * NH].unsqueeze(2).to_broadcast([P, NH, HD]),
                                         ALU.mult), dtx_ready)
            for t in range(TT):
                dve.wait_ge(csrow_ps, t + 1)
                for v in ([0] if t == 0 else [1, 2]):
                    for h in range(NH):
                        src = PS[:, h // 4, (h % 4) * P:(h % 4) * P + P]
                        if v < 2:
                            ins = dve.tensor_scalar(E[:, v, h, :], src, csv[:, v * NH + h:v * NH + h + 1], 0.0,
                                                    ALU.subtract, ALU.min)
                        else:
                            ins = dve.tensor_scalar(E[:, v, h, :], src, csv[:, 3 * NH + h:3 * NH + h + 1], 0.0,
                                                    ALU.add, ALU.min)
                        if h < NH - 1:
                            continue
                        signal(ins, decay_in)
                dve.wait_ge(decay_in, 1 + 2 * t)
                signal(dve.memset(small[:, 10:11], 0.0), csrow_used)
            dve.wait_ge(cb_ps, 1)
            for g in range(NG):
                for v in range(3):
                    src = PS[:, g, v * P:(v + 1) * P]
                    if v < 2:
                        ins = dve.tensor_tensor(CBT[:, v, g, :], src, tri[:], ALU.mult)
                    else:
                        ins = dve.tensor_copy(CBT[:, v, g, :], src)
                    signal(ins, cb_used)
            dve.wait_ge(cb_used, 3 * NG)
            dve.wait_ge(decay_ready, 3)
            for v in range(3):
                for g in range(NG):
                    e = E[:, v, HPG * g:HPG * g + HPG, :]
                    signal(dve.tensor_tensor(e, e, CBT[:, v, g, :].unsqueeze(1).to_broadcast([P, HPG, P]),
                                             ALU.mult), wts_ready)
            ada(4)
            dve.wait_ge(y_ps, 1)
            for b in range(CBLK):
                src = PS[:, b // 2, (b % 2) * TOK:(b % 2) * TOK + TOK]
                signal(dve.scalar_tensor_tensor(out=YC[:, CBLK + b, :], in0=XC[:, b, :], scalar=dskip[:, b:b + 1],
                                                in1=src, op0=ALU.mult, op1=ALU.add), y_used)
            dve.wait_ge(y_used, CBLK)
            yb = YC[:, CBLK:2 * CBLK, :]
            link(dve.tensor_tensor(yb, yb, SZ, ALU.mult))
            link(dve.tensor_tensor(SQ, yb, yb, ALU.mult), sq_ready)
            dve.wait_ge(yss_ps, 1)
            link(dve.tensor_scalar(RSB[:, 0, :], PS[:, 7, 0:TOK], 1.0 / DS, EPS, ALU.mult, ALU.add), yms_ready)
            ada(5)
            dve.wait_ge(ystd_ready, 1)
            link(dve.reciprocal(RSB[:, 1, :], RSB[:, 0, :]))
            for b in range(CBLK):
                signal(dve.scalar_tensor_tensor(out=YC[:, CBLK + b, :], in0=YC[:, CBLK + b, :],
                                                scalar=COL[:, R_NG + b:R_NG + b + 1], in1=RSB[:, 1, :],
                                                op0=ALU.mult, op1=ALU.mult), yb_ready)
            for b in (2, 3, 0, 1):
                dve.wait_ge(proj_evac, max(evac[4 + b], evac[8 + b], evac[b]))
                cc = CC[:, b, CK - 1:CK - 1 + TOK]
                link(dve.tensor_tensor(cc, cc, CU[:, b, :], ALU.mult))
                w = [COL[:, R_CA + k * CBLK + b:R_CA + k * CBLK + b + 1] for k in range(CK)]
                link(dve.tensor_scalar(YC[:, b, :], CC[:, b, 0:TOK], w[0], None, ALU.mult))
                for k in range(1, CK):
                    link(dve.scalar_tensor_tensor(out=YC[:, b, :], in0=CC[:, b, k:k + TOK], scalar=w[k],
                                                  in1=YC[:, b, :], op0=ALU.mult, op1=ALU.add))
                signal(dve.tensor_tensor(YC[:, b, :], YC[:, b, :], CB[:, b, :], ALU.mult), ya_ready)
            ada(6)
            ada(7)
            dve.wait_ge(gains_in, 16 * 3)
            dve.wait_ge(modrow_ready, 8)
            link(dve.scalar_tensor_tensor(out=MOD[:, 4 * D:5 * D], in0=MOD[:, 4 * D:5 * D], scalar=1.0, in1=gffn[:],
                                          op0=ALU.add, op1=ALU.mult))
            for t in range(TT):
                for h in range(2):
                    r = 2 * t + h
                    cols = slice(512 * h, 512 * h + 512)
                    dve.wait_ge(mix_ps, r + 1)
                    link(dve.tensor_tensor(T1[:, t, cols], bank(2 + r), MOD[:, 2 * D + 512 * h:2 * D + 512 * h + 512],
                                           ALU.mult))
                    link(dve.tensor_tensor(X[:, t, cols], X[:, t, cols], T1[:, t, cols], ALU.add), x2_ready)
            rstd(8, 2)
            for t in range(TT):
                link(dve.scalar_tensor_tensor(out=T1[:, t, :], in0=X[:, t, :], scalar=small[:, 8 + t:9 + t],
                                              in1=MOD[:, 4 * D:5 * D], op0=ALU.mult, op1=ALU.mult))
                link(dve.tensor_tensor(H2P[:, t, :].rearrange("p (k q) -> p q k", k=KD),
                                       T1[:, t, :].rearrange("p (q k) -> p q k", k=KD),
                                       MOD[:, 3 * D:4 * D].rearrange("p (q k) -> p q k", k=KD), ALU.add), h2_ready)

            dve.wait_ge(score_ready, 1)
            link(dve.tensor_tensor(sel, score, rbias[:].unsqueeze(1).to_broadcast([P, TT, NE]), ALU.add))
            n = 0
            for t in range(TT):
                for g in range(NGR):
                    n = signal(dve.max(top8[:, t, g, :], sel[:, t, 8 * g:8 * g + 8]), dve_step)
            dve.wait_ge(dve_step, n)
            link(dve.tensor_tensor(gs, top8[:, :, :, 0], top8[:, :, :, 1], ALU.add))
            mine = gs.unsqueeze(3).to_broadcast([P, TT, NGR, NGR])
            other = gs.unsqueeze(2).to_broadcast([P, TT, NGR, NGR])
            link(dve.tensor_tensor(gpair, other, mine, ALU.is_equal))
            link(dve.tensor_tensor(gpair, gpair, lower[:].unsqueeze(1).to_broadcast([P, TT, NGR, NGR]), ALU.mult))
            link(dve.tensor_tensor(gpair2, other, mine, ALU.is_gt))
            link(dve.tensor_tensor(gpair, gpair, gpair2, ALU.add))
            link(dve.tensor_reduce(grank, gpair, AX.X, ALU.add))
            link(dve.tensor_scalar(grank, grank, float(TOPG), None, ALU.is_lt))
            gmask = grank.unsqueeze(3).to_broadcast([P, TT, NGR, NE // NGR])
            link(dve.tensor_tensor(msel.rearrange("p t (g j) -> p t g j", g=NGR),
                                   sel.rearrange("p t (g j) -> p t g j", g=NGR), gmask, ALU.mult))
            link(dve.tensor_scalar(gs, grank, 1e30, -1e30, ALU.mult, ALU.add))
            link(dve.tensor_tensor(msel.rearrange("p t (g j) -> p t g j", g=NGR),
                                   msel.rearrange("p t (g j) -> p t g j", g=NGR),
                                   gs.unsqueeze(3).to_broadcast([P, TT, NGR, NE // NGR]), ALU.add))
            for t in range(TT):
                link(dve.max(m8[:, t, :], msel[:, t, :]))
                link(dve.match_replace(out=maskf[:, t, :], in_to_replace=m8[:, t, :], in_values=msel[:, t, :],
                                       imm_value=-3e30))
            link(dve.tensor_scalar(maskf, maskf, -3e30, None, ALU.is_equal))
            link(dve.tensor_copy(maskb[:], maskf), mask_ready)
            link(dve.tensor_tensor(gates, score, maskf, ALU.mult))
            link(dve.tensor_reduce(grank[:, :, 0:1], gates, AX.X, ALU.add))
            link(dve.reciprocal(grank[:, :, 0:1], grank[:, :, 0:1]))
            for t in range(TT):
                link(dve.tensor_scalar(gates[:, t, :], gates[:, t, :], grank[:, t, 0:1], ROUTED_SCALE,
                                       ALU.mult, ALU.mult))
            for part_no in range(3):
                rt = RT[:, :, 0:NE, 2 + part_no]
                link(dve.tensor_copy(rt, gates))
                if part_no < 2:
                    link(dve.tensor_tensor(gates, gates, rt, ALU.subtract))
            link(dve.tensor_copy(RT[:, :, 0:NE, 0], tokid[:].unsqueeze(2).to_broadcast([P, TT, NE])))
            link(dve.memset(cumA, 0.0))
            link(dve.memset(cumB, 0.0))
            link(dve.tensor_copy(cumA[:, :, 33:96], maskf[:, :, 0:63]))
            src_, dst_ = cumA, cumB
            for sh in (1, 2, 4, 8, 16, 32):
                link(dve.tensor_tensor(dst_[:, :, 32:96], src_[:, :, 32:96], src_[:, :, 32 - sh:96 - sh], ALU.add))
                src_, dst_ = dst_, src_
            link(dve.tensor_copy(RT[:, :, 0:NE, 1], src_[:, :, 32:96]))
            dve.wait_ge(rank_ps, 1)
            link(dve.tensor_scalar(rankm[:, :, 0:NE], PS[:, 7, 0:W64].rearrange("p (t e) -> p t e", t=TT), 1.0, None,
                                   ALU.add))
            link(dve.tensor_tensor(rankm[:, :, 0:NE], rankm[:, :, 0:NE], maskf, ALU.mult))
            link(dve.tensor_scalar(rankm[:, :, 0:NE], rankm[:, :, 0:NE], -1.0, None, ALU.add))
            link(dve.tensor_reduce(small[:, 12:13], PS[:, 7, W64:W64 + NE], AX.X, ALU.max))
            link(dve.tensor_scalar(oflag[:], small[:, 12:13], P + 0.5, None, ALU.is_gt), table_ready)
            signal(dve.memset(small[:, 13:14], 0.0), table_ready)

            for t in range(TT):
                dve.wait_ge(ssg_ready, t + 1)
                signal(dve.tensor_tensor(HID[:, t, :].rearrange("p (c q) -> p q c", c=FT),
                                         SG[:, t, :].rearrange("p (q c) -> p q c", c=FT),
                                         PS[:, 2 + t, FE:2 * FE].rearrange("p (q c) -> p q c", c=FT),
                                         ALU.mult), shid_ready)

            def decode(pas, g):
                n = g + PASS_GROUPS * pas
                cols = bass.ds(g * GRP, GRP)
                dve.wait_ge(slot_ps, n + 1)
                ps = PS[:, 7, 0:GRP * NCOL].rearrange("p (e c) -> p e c", e=GRP)
                dve.tensor_copy(dec[:, 0, :], ps[:, :, 1]).then_inc(dec_step, 1)
                dve.tensor_scalar(gidx[:, cols], ps[:, :, 0], float(TOK), None, ALU.add).then_inc(slot_ready, 1)
                dve.wait_ge(dec_step, n * 2 + 1)
                dve.scalar_tensor_tensor(out=dec[:, 1, :], in0=ps[:, :, 0], scalar=float(TOPK), in1=dec[:, 0, :],
                                         op0=ALU.mult, op1=ALU.add).then_inc(dec_step, 1)
                dve.tensor_reduce(gate[:, cols], ps[:, :, 2:5], AX.X, ALU.add).then_inc(slot_ready, 1)
                dve.wait_ge(dec_step, n * 2 + 2)
                dve.tensor_scalar(sidx[:, cols], dec[:, 1, :], float(TOK * TOPK), None, ALU.add).then_inc(slot_ready, 1)

            def one_hots(pas, g):
                n = g + PASS_GROUPS * pas
                dve.wait_ge(cur_copied, n * 2 + 2)
                if not (isinstance(n, int) and n == 0):
                    dve.wait_ge(slot_ps, n)
                for t in range(TT):
                    dve.tensor_tensor(onehot[:, t, :, :], rcur[:, t, :].unsqueeze(2).to_broadcast([P, GRP, P]),
                                      slots[:, pas, :].unsqueeze(1).to_broadcast([P, GRP, P]),
                                      ALU.is_equal).then_inc(onehot_ready, 1)

            def copy_xT(n, u):
                dve.wait_ge(xT_ps, n + 1)
                dve.tensor_copy(XT[:, u % 2, 4:8, :].rearrange("p k n -> p (k n)"), bank(1)).then_inc(xT_ready, 1)

            def hidden(n, i, u):
                dve.wait_ge(sg_ready, n + 1)
                dve.scalar_tensor_tensor(out=HID[:, u % 2, :].rearrange("p (c q) -> p q c", c=FT),
                                         in0=SG[:, u % 2, :].rearrange("p (q c) -> p q c", c=FT),
                                         scalar=gate[:, bass.ds(i * GRP + u, 1)],
                                         in1=PS[:, 2 + u % 2, FE:2 * FE].rearrange("p (q c) -> p q c", c=FT),
                                         op0=ALU.mult, op1=ALU.mult).then_inc(hid_ready, 1)

            def group(pas, i, last=False):
                for u in range(GRP):
                    n = number(pas, i, u)
                    if not (last and u == 3):
                        hidden(n + 1, i, u + 1)
                    if not (last and u >= 2):
                        copy_xT(n + 2, u)
                    if u == 1 and not last:
                        one_hots(pas, i + AHEAD)
                    if u == 2 and not last:
                        decode(pas, i + AHEAD)
                    dve.wait_ge(expert_done, n + 1)
                    if u >= 2:
                        dve.wait_ge(scattered[u % 2], (i * 2 + (32 * pas + 1)) * 16)
                    elif not (isinstance(i, int) and i == 0 and pas == 0):
                        dve.wait_ge(scattered[u % 2], (i * 2 + 32 * pas) * 16)
                    dve.tensor_copy(YS[:, u % 2, 512:1024], bank(5)).then_inc(y_ready, 1)

            def run_pass(pas):
                n = NE * pas
                for g in range(AHEAD):
                    one_hots(pas, g)
                    decode(pas, g)
                dve.wait_ge(slot_ready, (PASS_GROUPS * pas + 2) * 3)
                copy_xT(n, 0)
                hidden(n, 0, 0)
                copy_xT(n + 1, 1)
                group(pas, 0)
                with dve.Fori(1, NGRP - 1) as i:
                    dve.wait_ge(slot_ready, (i + (PASS_GROUPS * pas + 2)) * 3)
                    group(pas, i)
                dve.wait_ge(slot_ready, (NGRP - 1 + PASS_GROUPS * pas + 2) * 3)
                group(pas, NGRP - 1, last=True)

            run_pass(0)
            over = dve.value_load(oflag[0:1, 0:1], min_val=0, max_val=1)
            with dve.If(over > 0):
                run_pass(1)
            with dve.Else():
                dve.nop()

            dve.wait_ge(sh_ready, TT)
            for t in range(TT):
                for h in range(2):
                    s = 2 * t + h
                    dve.wait_ge(y_loaded[s], 16)
                    for j in range(4):
                        link(dve.tensor_tensor(SH[:, t, :], SH[:, t, :], ring[:, s, j * D:(j + 1) * D], ALU.add))
                link(dve.tensor_tensor(SH[:, t, :], SH[:, t, :], MOD[:, 5 * D:6 * D], ALU.mult))
                link(dve.tensor_tensor(X[:, t, :], X[:, t, :], SH[:, t, :], ALU.add), fin_ss)
                dve.wait_ge(ss_ready, 2 * TT + t + 1)
                link(dve.tensor_scalar(small[:, 2 + t:3 + t], small[:, t:t + 1], 1.0 / D, EPS, ALU.mult, ALU.add),
                     fin_ms)
                dve.wait_ge(fin_std, t + 1)
                link(dve.reciprocal(small[:, 8 + t:9 + t], small[:, 4 + t:5 + t]))
                link(dve.scalar_tensor_tensor(out=X[:, t, :], in0=X[:, t, :], scalar=small[:, 8 + t:9 + t],
                                              in1=gfin[:], op0=ALU.mult, op1=ALU.mult), out_ready)

        @block.tensor
        def _(pe):
            pe.wait_ge(consts, 1)
            pe.wait_ge(params_in, 16 * 5)
            pe.transpose(PS[:, 7, 0:R_END], prm[:], ident[0:R_END, 0:R_END]).then_inc(prm_ps, 1)
            pe.wait_ge(xn_ready, TT)
            for k in range(KD):
                for t in range(TT):
                    m = pe.transpose(PS[:, 2 + k // 2, (k % 2) * TOK + t * P:(k % 2) * TOK + t * P + P],
                                     XN[:, t, k * P:(k + 1) * P], ident[:])
            m.then_inc(xnT_ps, 1)
            pe.wait_ge(ada_acc, 3)
            for j in range(2 * KD):
                m = pe.matmul(PS[:, 0, j:j + 1], MOD[:, j * P:(j + 1) * P], ones[:, 0:1], start=True, stop=True)
            m.then_inc(modcol_ps, 1)

            pe.wait_ge(h1_ready, KD)
            pe.wait_ge(col_ready, 1)
            n3 = load_no(I, 3)
            pe.wait_ge(loaded[slot_of(n3)], loaded_count(n3))
            w3 = ring[:, slot_of(n3), 0:KD * LASTP].rearrange("p (k n) -> p k n", k=KD)
            for t in range(TT):
                for k in range(KD):
                    m = pe.matmul(PS[:, 7, t * NH:(t + 1) * NH], hT[:, k, t * P:(t + 1) * P],
                                  w3[:, k, PIECE:PIECE + NH], start=(k == 0), stop=(k == KD - 1))
            m.then_inc(dt_ps, 1)

            def project(q):
                m = ORDER[q]
                n = load_no(I, m // 6)
                if q % 6 == 0:
                    pe.wait_ge(loaded[slot_of(n)], loaded_count(n))
                width = LASTP if m // 6 == 3 else PIECE
                w = ring[:, slot_of(n), 0:KD * width].rearrange("p (k n) -> p k n", k=KD)
                if q >= QB:
                    pe.wait_ge(proj_evac, q - QB + 1)
                for k in range(KD):
                    mm = pe.matmul(PS[:, 2 + q % QB, 0:TOK], w[:, k, (m % 6) * P:(m % 6) * P + P], hT[:, k, :],
                                   start=(k == 0), stop=(k == KD - 1))
                mm.then_inc(proj_mm, 1)

            def cs_cols():
                pe.wait_ge(a_ready, 1)
                for t in range(TT):
                    pe.matmul(PS[:, 7, 32 + t * NH:32 + (t + 1) * NH], tri[:], dtv[:, 9, t * NH:(t + 1) * NH],
                              start=True, stop=True)
                pe.matmul(PS[:, 7, 48:48 + NH], ones[:], dtv[:, 9, 0:NH], start=True, stop=True).then_inc(cs_ps, 1)

            def xs_transposes():
                pe.wait_ge(xbc_ready, XB)
                for t in range(TT):
                    for b in range(CBLK):
                        m = pe.transpose(PS[:, t, b * P:(b + 1) * P], XC[:, b, t * P:(t + 1) * P], ident[:])
                m.then_inc(xsT_ps, 1)

            def cs_rows(t):
                if t == 0:
                    pe.wait_ge(dtx_ready, TT)
                else:
                    pe.wait_ge(csrow_used, t)
                for h in range(NH):
                    m = pe.matmul(PS[:, h // 4, (h % 4) * P:(h % 4) * P + P], AB[:, t, h, :], tri[:],
                                  start=True, stop=True)
                m.then_inc(csrow_ps, 1)

            def c_dot_b():
                pe.wait_ge(csrow_used, TT)
                for g in range(NG):
                    for v, (s, l) in enumerate(((0, 0), (1, 1), (0, 1))):
                        m = pe.matmul(PS[:, g, v * P:(v + 1) * P], XC[:, 4 + g, s * P:(s + 1) * P],
                                      XC[:, 6 + g, l * P:(l + 1) * P], start=True, stop=True)
                m.then_inc(cb_ps, 1)

            def y_heads():
                pe.wait_ge(wts_ready, 3 * NG)
                for h in range(NH):
                    b, r = h // 2, (h % 2) * HD
                    c0 = (b % 2) * TOK
                    lhs = [DTX[:, t, h * HD:(h + 1) * HD] for t in range(TT)]
                    pe.matmul(PS[r:r + HD, b // 2, c0:c0 + P], lhs[0], E[:, 0, h, :], start=True, stop=True)
                    pe.matmul(PS[r:r + HD, b // 2, c0 + P:c0 + TOK], lhs[0], E[:, 2, h, :], start=True, stop=False)
                    m = pe.matmul(PS[r:r + HD, b // 2, c0 + P:c0 + TOK], lhs[1], E[:, 1, h, :], start=False, stop=True)
                m.then_inc(y_ps, 1)

            def y_squares():
                pe.wait_ge(sq_ready, 1)
                for b in range(CBLK):
                    m = pe.matmul(PS[:, 7, 0:TOK], ones[:], SQ[:, b, :], start=(b == 0), stop=(b == CBLK - 1))
                m.then_inc(yss_ps, 1)

            for q in range(NQ):
                project(q)
                if q == 5:
                    cs_cols()
                if q == 13:
                    xs_transposes()
                if q == 14:
                    cs_rows(0)
                if q == 15:
                    cs_rows(1)
                if q == 16:
                    c_dot_b()
                if q == 18:
                    y_heads()
                if q == 21:
                    y_squares()

            def mod_rows(r):
                c0 = 2 * D + 512 * r
                pe.wait_ge(ada_acc, (c0 + 512 + PIECE - 1) // PIECE)
                if r >= 2:
                    pe.wait_ge(modrow_ready, r - 1)
                pe.matmul(bank(r % 2), ones[:], MOD[:, c0:c0 + 512], start=True, stop=True).then_inc(modrow_ps, 1)

            pe.wait_ge(y_used, CBLK)
            for r in range(5):
                mod_rows(r)
            pe.wait_ge(yb_ready, CBLK)
            pe.wait_ge(ya_ready, CBLK)
            pe.wait_ge(proj_evac, NQ)
            for t in range(TT):
                for h in range(2):
                    for k in range(KD):
                        j = 0 if k < OUT_K[0][1] else 1
                        n = load_no(O, j)
                        if t == 0 and h == 0 and k == OUT_K[j][0]:
                            pe.wait_ge(loaded[slot_of(n)], loaded_count(n))
                        w = ring[:, slot_of(n), 0:6 * D].rearrange("p (k n) -> p k n", n=D)
                        m = pe.matmul(bank(2 + 2 * t + h), YC[:, k, t * P:(t + 1) * P],
                                      w[:, k - OUT_K[j][0], 512 * h:512 * h + 512], start=(k == 0), stop=(k == KD - 1))
                        if t == TT - 1 and h == 1 and k == OUT_K[0][1] - 1:
                            m.then_inc(wout_used, 1)
                    m.then_inc(mix_ps, 1)
            for r in range(5, 8):
                mod_rows(r)
            pe.wait_ge(h2_ready, TT)
            for k in range(KD):
                for t in range(TT):
                    m = pe.transpose(PS[:, 2 + k // 2, (k % 2) * TOK + t * P:(k % 2) * TOK + t * P + P],
                                     H2P[:, t, k * P:(k + 1) * P], ident[:])
                if k % 2:
                    m.then_inc(h2T_ps, 1)
            pe.wait_ge(gains_in, 16 * 3)
            for k in range(4):
                pe.wait_ge(h2T_ready, k + 1)
            for t in range(TT):
                for k in range(KD):
                    m = pe.matmul(PS[:, 7, t * NE:(t + 1) * NE], hT[:, k, t * P:(t + 1) * P], WR[:, k, :],
                                  start=(k == 0), stop=(k == KD - 1))
            m.then_inc(logit_ps, 1)

            def gate_up(dst, lhs, w):
                for k in range(KD):
                    m = pe.matmul(bank(dst).rearrange("p (a n) -> p a n", a=2), lhs[k], w[:, :, k, :],
                                  start=(k == 0), stop=(k == KD - 1))
                return m

            def hidden_transposes(b):
                for cc in range(FT):
                    m = pe.transpose(PS[:, 6, cc * P:(cc + 1) * P], HID[:, b, cc * P:(cc + 1) * P], ident[:])
                return m

            def down(s):
                w = down_w(s)
                for h in range(2):
                    for cc in range(FT):
                        m = pe.matmul(bank(4 + h), HTT[:, cc, :], w[:, cc, 512 * h:512 * h + 512],
                                      start=(cc == 0), stop=(cc == FT - 1))
                return m

            ns = load_no(S, 0)
            pe.wait_ge(loaded[slot_of(ns)], loaded_count(ns))
            for t in range(TT):
                gate_up(2 + t, [hT[:, k, t * P:(t + 1) * P] for k in range(KD)], gu_w(slot_of(ns))).then_inc(sgu_ps, 1)
            pe.wait_ge(mask_ready, 1)
            pe.wait_ge(score_ready, 1)
            pe.matmul(PS[:, 7, 0:NE], trib[:], maskb[:, 0, :], start=True, stop=True)
            pe.matmul(PS[:, 7, NE:2 * NE], trib[:], maskb[:, 1, :], start=True, stop=False)
            pe.matmul(PS[:, 7, NE:2 * NE], onesb[:], maskb[:, 0, :], start=False, stop=True)
            pe.matmul(PS[:, 7, 2 * NE:3 * NE], onesb[:], maskb[:, 0, :], start=True, stop=False)
            pe.matmul(PS[:, 7, 2 * NE:3 * NE], onesb[:], maskb[:, 1, :], start=False, stop=True).then_inc(rank_ps, 1)
            for t in range(TT):
                pe.wait_ge(shid_ready, t + 1)
                if t:
                    pe.wait_ge(sh_ready, t)
                hidden_transposes(t).then_inc(shT_ps, 1)
                pe.wait_ge(shT_ready, t + 1)
                down(slot_of(ns)).then_inc(sy_ps, 1)

            def slot_values(pas, g):
                n = g + PASS_GROUPS * pas
                pe.wait_ge(onehot_ready, n * 2 + 2)
                if not (isinstance(n, int) and n == 0):
                    pe.wait_ge(slot_ready, n * 3)
                else:
                    pe.wait_ge(table_ready, 1)
                for e in range(GRP):
                    for t in range(TT):
                        m = pe.matmul(PS[:, 7, e * NCOL:(e + 1) * NCOL], onehot[:, t, e, :], rtcur[:, t, e, :],
                                      start=(t == 0), stop=(t == TT - 1))
                m.then_inc(slot_ps, 1)

            def transposes(pas, i, u):
                n = number(pas, i, u)
                b = u % 2
                pe.wait_ge(gathered[b], (i * 2 + (32 * pas + u // 2 + 1)) * 16)
                if not (isinstance(n, int) and n == 0):
                    pe.wait_ge(xT_ready, n * 2)
                for k in range(KD):
                    m = pe.transpose(PS[:, k // 4, (k % 4) * P:(k % 4) * P + P], HG[:, b, k * P:(k + 1) * P], ident[:])
                m.then_inc(xT_ps, 1)

            def expert_gate_up(pas, i, u):
                n = number(pas, i, u)
                s = e_slot(u % GRP)
                pe.wait_ge(loaded[s], (i + (NGRP * pas + u // GRP + 1)) * 48 + slot_base(s))
                pe.wait_ge(xT_ready, n * 2 + 2)
                gate_up(2 + u % 2, [XT[:, u % 2, k, :] for k in range(KD)], gu_w(s)).then_inc(gu_ps, 1)

            def group(pas, i, last=False):
                for u in range(GRP):
                    n = number(pas, i, u)
                    if not (last and u == 3):
                        if not (isinstance(n, int) and n == 0):
                            pe.wait_ge(hid_ready, n)
                        expert_gate_up(pas, i, u + 1)
                    pe.wait_ge(hid_ready, n + 1)
                    if not (isinstance(n, int) and n == 0):
                        pe.wait_ge(hidT_ready, n)
                    hidden_transposes(u % 2).then_inc(hidT_ps, 1)
                    if not (last and u >= 2):
                        transposes(pas, i, u + 2)
                    if u == 2 and not last:
                        slot_values(pas, i + AHEAD)
                    pe.wait_ge(hidT_ready, n + 1)
                    if isinstance(n, int) and n == 0:
                        pe.wait_ge(sh_ready, TT)
                    else:
                        pe.wait_ge(y_ready, n * 2)
                    down(e_slot(u)).then_inc(expert_done, 1)

            def run_pass(pas):
                slot_values(pas, 0)
                slot_values(pas, 1)
                transposes(pas, 0, 0)
                expert_gate_up(pas, 0, 0)
                transposes(pas, 0, 1)
                group(pas, 0)
                with pe.Fori(1, NGRP - 1) as i:
                    group(pas, i)
                group(pas, NGRP - 1, last=True)

            run_pass(0)
            over = pe.value_load(oflag[0:1, 0:1], min_val=0, max_val=1)
            with pe.If(over > 0):
                run_pass(1)
            with pe.Else():
                pe.nop()


_INS = ["x", "c", "w_ada", "b_ada", "norm_mix_g", "w_in", "conv_a_w", "ssm_conv_w", "ssm_conv_b", "ssm_dt_bias",
        "ssm_a_log", "ssm_d", "ssm_norm_g", "w_out", "norm_ffn_g", "w_router", "router_bias", "we_gate", "we_up",
        "we_down", "ws_gate", "ws_up", "ws_down", "norm_final_g"]
_OUTS = [((1, 256, 1024), "float32")]


def kernel(**inputs):
    import numpy as _np
    import concourse.bacc as _bacc
    from concourse import mybir as _mybir
    from concourse.bass_utils import run_bass_kernel_spmd as _run

    nc = _bacc.Bacc("TRN2", target_bir_lowering=False, num_devices=1)
    arrays, args = {}, []
    for name in _INS:
        a = _np.ascontiguousarray(inputs[name])
        arrays[f"in_{name}_dram"] = a
        args.append(nc.dram_tensor(f"in_{name}_dram", a.shape, _mybir.dt.from_np(a.dtype), kind="ExternalInput").ap())
    for i, (shape, dtype) in enumerate(_OUTS):
        dt = _mybir.dt.from_np(_np.dtype(dtype))
        args.append(nc.dram_tensor(f"out_{i}_dram", shape, dt, kind="ExternalOutput").ap())
    build(nc, *args)
    r = _run(nc, [arrays], core_ids=[0])
    return r.results[0]["out_0_dram"]
```

```python
from contextlib import ExitStack

import concourse.bass as bass
from concourse import mybir

P = 128
F32 = mybir.dt.float32
BF16 = mybir.dt.bfloat16
F32R = mybir.dt.float32r
U32 = mybir.dt.uint32
ALU = mybir.AluOpType
ACT = mybir.ActivationFunctionType
AX = mybir.AxisListType

D = 1024
KD = D // P
TT = 2
TOK = TT * P
DC = 512
DS = 512
NH = 8
HD = 64
NG = 2
HPG = NH // NG
CBLK = DC // P
XB = (DS + 2 * NG * P) // P
CK = 3
SK = 4
EPS = 1e-6
NE = 64
TOPK = 8
NGR = 8
TOPG = 4
FE = 256
FT = FE // P
ROUTED_SCALE = 2.5

NSLOT = 4
PIECE = 768
LASTP = 776
SLOTW = KD * LASTP
GU = 2 * KD * FE
AHEAD = 2
GRP = 4
NGRP = NE // GRP
TG = NGRP + AHEAD
TE = TG * GRP
NCOL = 5
PASS_GROUPS = NGRP - 1 + AHEAD

SPLITS = [(0, 3), (3, 5), (5, 7), (7, 8)]
EARLY = 2
NSP = len(SPLITS)

R_CA, R_CS, R_CB, R_NG, R_NM = 0, CK * CBLK, CK * CBLK + SK * XB, CK * CBLK + SK * XB + XB, 56
R_END = R_NM + KD

A, I, O, S = "ada", "in", "out", "shared"
LOADS = [(A, 0, 0), (A, 1, 1), (A, 2, 2), (I, 3, 3), (A, 3, 1), (I, 2, 0), (A, 4, 2), (I, 1, 1), (A, 5, 2),
         (I, 0, 3), (A, 6, 2), (O, 0, 0), (A, 7, 2), (O, 1, 1), (S, 0, 2)]
FIRST_SLOT = 3
OUT_K = [(0, 6), (6, 8)]
OUT_ORDER = [4, 5, 6, 7, 2, 3, 0, 1]
ORDER = [21, 22, 23, 18, 19, 20, 16, 17, 12, 13, 14, 15, 8, 9, 10, 11, 6, 7, 4, 5, 2, 3, 0, 1]
CONVS = [5, 6, 7, 2, 3, 4, 0, 1]
LATE = 384
NQ = len(ORDER)
QB = 5


def n_dmas(what):
    return 3 if what == S else 1


def slot_of(n):
    return LOADS[n][2]


def loaded_count(n):
    return 16 * sum(n_dmas(what) for what, _, s in LOADS[:n + 1] if s == slot_of(n))


def build(nc, x, c, w_ada, b_ada, norm_mix_g, w_in, conv_a_w, ssm_conv_w, ssm_conv_b, ssm_dt_bias,
          ssm_a_log, ssm_d, ssm_norm_g, w_out, norm_ffn_g, w_router, router_bias, we_gate, we_up,
          we_down, ws_gate, ws_up, ws_down, norm_final_g, out):
    with ExitStack() as ctx:
        def sb(name, shape, dt=F32):
            return ctx.enter_context(nc.sbuf_tensor(name, shape, dt))

        def sem(name):
            return ctx.enter_context(nc.semaphore(name))

        h2_dram = nc.dram_tensor("h2_rows", [TOK, D], F32, kind="Internal").ap()
        y_dram = nc.dram_tensor("expert_rows", [TOK * TOPK, D], F32, kind="Internal").ap()

        ring = sb("ring", [P, NSLOT, SLOTW])
        X = sb("X", [P, TT, D])
        hT_at = nc.sbuf_base
        hT = sb("hT", [P, KD, TOK])
        MOD_at = nc.sbuf_base
        MOD = sb("MOD", [P, 6 * D])
        gffn_at = nc.sbuf_base
        gffn = sb("gffn", [P, D])
        gfin = sb("gfin", [P, D])
        arena_at = nc.sbuf_base
        arena = sb("arena", [P, 13352])
        ident = sb("ident", [P, P])
        tri = sb("tri", [P, P])
        ones = sb("ones", [P, P])
        trib = sb("trib", [P, P], BF16)
        onesb = sb("onesb", [P, P], BF16)
        slots = sb("slots", [P, 2, P])
        WR = sb("WR", [P, KD, NE])
        COL = sb("COL", [P, R_END])
        ccol = sb("ccol", [P, KD])
        rbias = sb("rbias", [P, NE])
        hrow = sb("hrow", [P, 2, NH])
        dskip = sb("dskip", [P, CBLK])
        small = sb("small", [P, 16])
        dtv = sb("dtv", [P, 10, TT * NH])
        csv = sb("csv", [P, 4 * NH])
        AB1 = sb("AB1", [P, 2 * KD])
        lower = sb("lower", [P, NGR, NGR])
        tokid = sb("tokid", [P, TT])
        rankm = sb("rankm", [P, TT, TE])
        RT = sb("RT", [P, TT, TE, NCOL], BF16)
        gidx = sb("gidx", [P, TE], U32)
        counts_u = sb("counts_u", [P, TE], U32)
        sidx = sb("sidx", [P, TE], U32)
        gate = sb("gate", [P, TE])
        gi = sb("gi", [P, 2, 1], U32)
        si = sb("si", [P, 2, 1], U32)
        spare = sb("spare", [P, 2])
        oflag = sb("oflag", [P, 1], U32)
        PS = ctx.enter_context(nc.psum_tensor("PS", [P, 8, 512], F32))

        o = [0]

        def part(n):
            o[0] += n
            return arena[:, o[0] - n:o[0]]

        XPf = part(XB * 260)
        XP = XPf.rearrange("p (b n) -> p b n", b=XB)
        CU = XPf[:, 0:CBLK * TOK].rearrange("p (b n) -> p b n", b=CBLK)
        CB = XPf[:, CBLK * TOK:2 * CBLK * TOK].rearrange("p (b n) -> p b n", b=CBLK)
        XC = part(XB * TOK).rearrange("p (b n) -> p b n", b=XB)
        SZ = part(CBLK * TOK).rearrange("p (b n) -> p b n", b=CBLK)
        CC = part(CBLK * 258).rearrange("p (b n) -> p b n", b=CBLK)
        DTX = part(TT * DS).rearrange("p (t n) -> p t n", t=TT)
        prm = DTX[0:R_END, 0, 0:P]
        Ef = part(3 * NH * P)
        E = Ef.rearrange("p (v h n) -> p v h n", v=3, h=NH)
        YC = part(KD * TOK).rearrange("p (b n) -> p b n", b=KD)
        CBT = part(3 * NG * P).rearrange("p (v g n) -> p v g n", v=3, g=NG)
        XN = YC.rearrange("p b n -> p (b n)").rearrange("p (t n) -> p t n", t=TT)
        T1 = Ef[:, 0:2 * D].rearrange("p (t n) -> p t n", t=TT)
        SQ = Ef[:, 0:CBLK * TOK].rearrange("p (b n) -> p b n", b=CBLK)
        RSB = Ef[:, CBLK * TOK:CBLK * TOK + 2 * TOK].rearrange("p (b n) -> p b n", b=2)
        AB = MOD[:, 0:TT * NH * P].rearrange("p (t h n) -> p t h n", t=TT, h=NH)
        o[0] = 0
        HG = part(2 * D).rearrange("p (b n) -> p b n", b=2)
        XT_at = arena_at + 4 * o[0]
        part(2 * D)
        YS = part(2 * D).rearrange("p (b n) -> p b n", b=2)
        HID = part(2 * FE).rearrange("p (b n) -> p b n", b=2)
        HTT = part(FE).rearrange("p (c n) -> p c n", c=FT)
        SG = part(2 * FE).rearrange("p (b n) -> p b n", b=2)
        o[0] = H2P_AT = 9256
        H2P = part(2 * D).rearrange("p (t n) -> p t n", t=TT)
        SH = part(2 * D).rearrange("p (t n) -> p t n", t=TT)
        XTH = nc.alloc_sbuf_tensor_at("XTH", [P, KD, P], F32R, offset=XT_at)
        XTL = nc.alloc_sbuf_tensor_at("XTL", [P, KD, P], F32R, offset=XT_at + 4 * D)
        WHI, WLO = [], []
        for (k0, k1), at in zip(SPLITS, (MOD_at + 4 * 2 * D, hT_at, arena_at + 4 * H2P_AT, gffn_at)):
            shape = [P, k1 - k0, 2, FE]
            WHI.append(nc.alloc_sbuf_tensor_at(f"WHI{k0}", shape, F32R, offset=at))
            WLO.append(nc.alloc_sbuf_tensor_at(f"WLO{k0}", shape, F32R, offset=at + 4 * (k1 - k0) * 2 * FE))
        o2 = [0]

        def mpart(n):
            o2[0] += n
            return MOD[:, o2[0] - n:o2[0]]

        W64 = TT * NE
        score = mpart(W64).rearrange("p (t e) -> p t e", t=TT)
        sel = mpart(W64).rearrange("p (t e) -> p t e", t=TT)
        msel = mpart(W64).rearrange("p (t e) -> p t e", t=TT)
        maskf = mpart(W64).rearrange("p (t e) -> p t e", t=TT)
        gates = mpart(W64).rearrange("p (t e) -> p t e", t=TT)
        cumA = mpart(TT * 96).rearrange("p (t e) -> p t e", t=TT)
        cumB = mpart(TT * 96).rearrange("p (t e) -> p t e", t=TT)
        top8 = mpart(TT * NGR * 8).rearrange("p (t g j) -> p t g j", t=TT, g=NGR)
        gs = mpart(TT * NGR).rearrange("p (t g) -> p t g", t=TT)
        grank = mpart(TT * NGR).rearrange("p (t g) -> p t g", t=TT)
        gpair = mpart(TT * NGR * NGR).rearrange("p (t g j) -> p t g j", t=TT, g=NGR)
        gpair2 = mpart(TT * NGR * NGR).rearrange("p (t g j) -> p t g j", t=TT, g=NGR)
        m8 = mpart(TT * 8).rearrange("p (t j) -> p t j", t=TT)
        maskb = mpart(W64 // 2).bitcast(BF16).rearrange("p (t e) -> p t e", t=TT)
        rcur = sb("rcur", [P, TT, GRP])
        onehot = mpart(TT * GRP * P // 2).bitcast(BF16).rearrange("p (t e n) -> p t e n", t=TT, e=GRP)
        rtcur = sb("rtcur", [P, TT, GRP, NCOL], BF16)
        dec = sb("dec", [P, 2, GRP])

        loaded = [sem(f"loaded{s}") for s in range(NSLOT)]
        gu_loaded = [sem(f"gu_loaded{s}") for s in range(NSLOT)]
        down_loaded = [sem(f"down_loaded{s}") for s in range(NSLOT)]
        x_in = sem("x_in")
        ada2_half = sem("ada2_half")
        in3_late = sem("in3_late")
        small_issued = sem("small_issued")
        bada_in = sem("bada_in")
        small_in = sem("small_in")
        params_in = sem("params_in")
        gains_in = sem("gains_in")
        mod_zero = sem("mod_zero")
        consts = sem("consts")
        ss_ready = sem("ss_ready")
        ms_ready = sem("ms_ready")
        std_ready = sem("std_ready")
        rstd_ready = sem("rstd_ready")
        xn_ready = sem("xn_ready")
        xnT_ps = sem("xnT_ps")
        xnT_ready = sem("xnT_ready")
        prm_ps = sem("prm_ps")
        col_ready = sem("col_ready")
        ada_acc = sem("ada_acc")
        modcol_ps = sem("modcol_ps")
        modrow_ps = sem("modrow_ps")
        modrow_ready = sem("modrow_ready")
        h1_ready = sem("h1_ready")
        dt_ps = sem("dt_ps")
        exp_in = sem("exp_in")
        exp_out = sem("exp_out")
        a_ready = sem("a_ready")
        cs_ps = sem("cs_ps")
        cs_ready = sem("cs_ready")
        csrow_ps = sem("csrow_ps")
        csrow_used = sem("csrow_used")
        decay_in = sem("decay_in")
        decay_ready = sem("decay_ready")
        proj_mm = sem("proj_mm")
        proj_evac = sem("proj_evac")
        conv_ready = sem("conv_ready")
        xbc_ready = sem("xbc_ready")
        xsT_ps = sem("xsT_ps")
        dtx_ready = sem("dtx_ready")
        cb_ps = sem("cb_ps")
        cb_used = sem("cb_used")
        wts_ready = sem("wts_ready")
        y_ps = sem("y_ps")
        y_used = sem("y_used")
        sq_ready = sem("sq_ready")
        yss_ps = sem("yss_ps")
        yms_ready = sem("yms_ready")
        ystd_ready = sem("ystd_ready")
        yb_ready = sem("yb_ready")
        ya_ready = sem("ya_ready")
        mix_ps = sem("mix_ps")
        x2_ready = sem("x2_ready")
        h2_ready = sem("h2_ready")
        h2_stored = sem("h2_stored")
        h2T_ps = sem("h2T_ps")
        h2T_ready = sem("h2T_ready")
        logit_ps = sem("logit_ps")
        score_ready = sem("score_ready")
        mask_ready = sem("mask_ready")
        rank_ps = sem("rank_ps")
        table_ready = sem("table_ready")
        sgu_ps = sem("sgu_ps")
        ssg_ready = sem("ssg_ready")
        shid_ready = sem("shid_ready")
        shT_ps = sem("shT_ps")
        shT_ready = sem("shT_ready")
        sy_ps = sem("sy_ps")
        sh_ready = sem("sh_ready")
        cur_copied = sem("cur_copied")
        onehot_ready = sem("onehot_ready")
        slot_ps = sem("slot_ps")
        dec_step = sem("dec_step")
        slot_ready = sem("slot_ready")
        gi_ready = sem("gi_ready")
        si_ready = sem("si_ready")
        gathered = [sem(f"gathered{b}") for b in range(2)]
        xT_ps = sem("xT_ps")
        xT_ready = sem("xT_ready")
        xhi_ready = sem("xhi_ready")
        whi_ready = sem("whi_ready")
        wlo_ready = sem("wlo_ready")
        split_used = sem("split_used")
        sg_ready = sem("sg_ready")
        hg_ready = sem("hg_ready")
        hid_ready = sem("hid_ready")
        hidT_ps = sem("hidT_ps")
        hidT_ready = sem("hidT_ready")
        expert_done = sem("expert_done")
        y_ready = sem("y_ready")
        scattered = [sem(f"scattered{b}") for b in range(2)]
        moe_done = sem("moe_done")
        y_loaded = [sem(f"y_loaded{s}") for s in range(4)]
        fin_ss = sem("fin_ss")
        fin_ms = sem("fin_ms")
        fin_std = sem("fin_std")
        out_ready = sem("out_ready")
        stored = sem("stored")
        act_step = sem("act_step")
        dve_step = sem("dve_step")
        pool_step = sem("pool_step")

        block = ctx.enter_context(nc.Block())

        def bank(b):
            return PS[:, b, :]

        def ada_w(n):
            return ring[:, slot_of(n), 0:KD * PIECE].rearrange("p (k n) -> p k n", k=KD)

        def load_no(what, j):
            return [load[:2] for load in LOADS].index((what, j))

        def gu_w(s):
            return ring[:, s, 0:GU].rearrange("p (a k n) -> p a k n", a=2, k=KD)

        def down_w(s):
            return ring[:, s, GU:GU + FT * D].rearrange("p (c n) -> p c n", c=FT)

        def e_slot(u):
            return (FIRST_SLOT + u) % NSLOT

        def number(pas, i, u):
            return i * GRP + (NE * pas + u)

        def gu_count(n, u):
            return (n - u % GRP) * (32 // GRP) + 32

        def down_count(n, u):
            return (n - u % GRP) * (16 // GRP) + 16

        @block.sync
        def _(sp):
            def load_gate_up(s, wg, wu, done):
                sp.dma_start(ring[:, s, 0:GU // 2], wg.rearrange("(p k) n -> p (k n)", p=P)).then_inc(done, 16)
                sp.dma_start(ring[:, s, GU // 2:GU], wu.rearrange("(p k) n -> p (k n)", p=P)).then_inc(done, 16)

            def load_down(s, wd, done):
                sp.dma_start(ring[:, s, GU:GU + FT * D], wd.rearrange("(p c) n -> p (c n)", p=P)).then_inc(done, 16)

            sp.dma_start(X[:], x[0].rearrange("(t p) d -> p t d", p=P)).then_inc(x_in, 16)
            sp.wait_ge(small_issued, 1)
            user = {}
            nada = nin = 0
            for n, (what, j, s) in enumerate(LOADS):
                if s in user:
                    sp.wait_ge(*user[s])
                if what == A:
                    nada += 1
                    user[s] = (ada_acc, nada)
                    src = w_ada[0, :, PIECE * j:PIECE * j + PIECE].rearrange("(p k) n -> p k n", p=P)
                    if j == 2:
                        sp.dma_start(ada_w(n)[:, 0:KD // 2, :], src[:, 0:KD // 2, :]).then_inc(ada2_half, 16)
                        sp.dma_start(ada_w(n)[:, KD // 2:KD, :], src[:, KD // 2:KD, :]).then_inc(loaded[s], 16)
                    else:
                        sp.dma_start(ada_w(n), src).then_inc(loaded[s], 16)
                elif what == I:
                    nin += 1
                    user[s] = (proj_mm, 6 * nin)
                    w = LASTP if j == 3 else PIECE
                    dst = ring[:, s, 0:KD * w].rearrange("p (k n) -> p k n", k=KD)
                    src = w_in[0, :, PIECE * j:PIECE * j + w].rearrange("(k p) n -> p k n", p=P)
                    if j == 3:
                        sp.dma_start(dst[:, :, LATE:w], src[:, :, LATE:w]).then_inc(in3_late, 16)
                        sp.dma_start(dst[:, :, 0:LATE], src[:, :, 0:LATE]).then_inc(loaded[s], 16)
                    else:
                        sp.dma_start(dst, src).then_inc(loaded[s], 16)
                elif what == O:
                    user[s] = (mix_ps, 2 * TT)
                    k0, k1 = OUT_K[j]
                    sp.dma_start(ring[:, s, 0:(k1 - k0) * D].rearrange("p (k n) -> p k n", n=D),
                                 w_out[0, k0 * P:k1 * P, :].rearrange("(k p) n -> p k n", p=P)
                                 ).then_inc(loaded[s], 16)
                else:
                    user[s] = (sy_ps, TT)
                    load_gate_up(s, ws_gate[0], ws_up[0], loaded[s])
                    load_down(s, ws_down[0], loaded[s])
            for u in range(GRP):
                sp.wait_ge(*user[e_slot(u)])
                load_gate_up(e_slot(u), we_gate[0, u], we_up[0, u], gu_loaded[e_slot(u)])
                load_down(e_slot(u), we_down[0, u], down_loaded[e_slot(u)])

            def expert_gate_up(pas, i, u):
                sp.wait_ge(wlo_ready, number(pas, i, u) * NSP - (NSLOT - 1) * NSP)
                e, s = i * GRP + u, e_slot(u % GRP)
                load_gate_up(s, we_gate[0, e], we_up[0, e], gu_loaded[s])

            def expert_down(pas, i, u):
                sp.wait_ge(expert_done, number(pas, i, u) - (NSLOT - 1))
                load_down(e_slot(u), we_down[0, i * GRP + u], down_loaded[e_slot(u)])

            def load_groups(pas, first):
                expert_gate_up(pas, first, 0)
                with sp.Fori(first, NGRP - 1) as i:
                    for u in range(GRP):
                        expert_gate_up(pas, i, u + 1)
                        expert_down(pas, i, u)
                for u in range(GRP):
                    if u < GRP - 1:
                        expert_gate_up(pas, NGRP - 1, u + 1)
                    expert_down(pas, NGRP - 1, u)

            load_groups(0, 1)
            sp.wait_ge(table_ready, 1)
            over = sp.value_load(oflag[0:1, 0:1], min_val=0, max_val=1)
            with sp.If(over > 0):
                load_groups(1, 0)
            with sp.Else():
                sp.nop()
            sp.wait_ge(moe_done, 1)
            for t in range(TT):
                for h in range(2):
                    s = 2 * t + h
                    sp.dma_start(ring[:, s, 0:4 * D],
                                 y_dram.rearrange("(t p j) d -> t p j d", t=TT, p=P)[t, :, 4 * h:4 * h + 4, :]
                                 .rearrange("p j d -> p (j d)")).then_inc(y_loaded[s], 16)
            for t in range(TT):
                sp.wait_ge(out_ready, t + 1)
                sp.dma_start(out[0, t * P:(t + 1) * P, :], X[:, t, :]).then_inc(stored, 16)
            sp.wait_ge(stored, 16 * TT)

        @block.gpsimd
        def _(pool):
            count = [0]

            def link(ins):
                count[0] += 1
                ins.then_inc(pool_step, 1)
                pool.wait_ge(pool_step, count[0])

            pool.memset(MOD[:], 0.0).then_inc(mod_zero, 1)
            link(pool.memset(ident[:], 0.0))
            link(pool.affine_select(out=ident[:], in_=ident[:], compare_op=ALU.not_equal, fill=1.0, base=0,
                                    pattern=[[-1, P]], channel_multiplier=1))
            link(pool.memset(ones[:], 1.0))
            link(pool.affine_select(out=tri[:], in_=ones[:], compare_op=ALU.is_ge, fill=0.0, base=0,
                                    pattern=[[1, P]], channel_multiplier=-1))
            link(pool.memset(onesb[:], 1.0))
            link(pool.affine_select(out=trib[:], in_=onesb[:], compare_op=ALU.is_ge, fill=0.0, base=-1,
                                    pattern=[[1, P]], channel_multiplier=-1))
            link(pool.memset(lower[:], 1.0))
            link(pool.affine_select(out=lower[:], in_=lower[:], compare_op=ALU.is_ge, fill=0.0, base=-1,
                                    pattern=[[1, NGR], [-1, NGR]], channel_multiplier=0))
            link(pool.iota(slots[:], pattern=[[P, 2], [1, P]], base=0, channel_multiplier=0,
                           allow_small_or_imprecise_dtypes=True))
            link(pool.iota(tokid[:], pattern=[[P, TT]], base=-TOK, channel_multiplier=1,
                           allow_small_or_imprecise_dtypes=True))
            link(pool.memset(spare[:], 0.0))
            link(pool.memset(rankm[:], -1.0))
            link(pool.memset(RT[:], 0.0))
            link(pool.memset(counts_u[:], 0.0))
            link(pool.memset(XPf, 0.0))
            pool.memset(CC, 0.0).then_inc(consts, 1)

            pool.wait_ge(ya_ready, CBLK)
            link(pool.memset(HG, 0.0))
            pool.wait_ge(table_ready, 2)
            pool.wait_ge(h2_stored, 16 * TT)

            last_token = pool.to_reg(TOK - 1)
            last_row = pool.to_reg(TOK * TOPK - 1)

            def carry_wait():
                pool.tensor_tensor(spare[:, 1:2], spare[:, 0:1], spare[:, 0:1], ALU.add)

            def sized(pas, e, issue):
                if pas:
                    issue(P)
                    return
                tokens = pool.value_load(counts_u[0:1, bass.ds(e, 1)], min_val=0, max_val=TOK)
                with pool.If(tokens > P // 2):
                    with pool.If(tokens > 3 * P // 4):
                        issue(P)
                    with pool.Else():
                        issue(3 * P // 4)
                    pool.nop()
                with pool.Else():
                    with pool.If(tokens > P // 4):
                        issue(P // 2)
                    with pool.Else():
                        issue(P // 4)
                    pool.nop()

            def stage_group(pas, g, first):
                n = g + PASS_GROUPS * pas
                if not first:
                    pool.wait_ge(slot_ps, n)
                cols = bass.ds(g * GRP, GRP)
                pool.tensor_copy(rcur[:], rankm[:, :, cols]).then_inc(cur_copied, 1)
                pool.tensor_copy(rtcur[:], RT[:, :, cols, :]).then_inc(cur_copied, 1)

            def gather(pas, i, u, first=False):
                n = number(pas, i, u)
                b = u % 2
                if u % GRP == 0 or first:
                    pool.wait_ge(slot_ready, (i + (PASS_GROUPS * pas + u // GRP + 1)) * 3)
                if not first:
                    pool.wait_ge(xT_ps, n - 1)
                pool.tensor_copy(gi[:, b, :], gidx[:, bass.ds(i * GRP + u, 1)]).then_inc(gi_ready, 1)
                pool.wait_ge(gi_ready, n + 1)
                carry_wait()
                sized(pas, i * GRP + u, lambda rows: pool.indirect_dma_start(
                    out=HG[0:rows, b, :], out_offset=None, in_=h2_dram[:],
                    in_offset=bass.IndirectOffsetOnAxis(ap=gi[0:rows, b, :], axis=0),
                    bounds_check=last_token, oob_is_err=False).then_inc(gathered[b], 16))

            def scatter(pas, i, u):
                n = number(pas, i, u)
                b = u % 2
                pool.wait_ge(y_ready, n * 2 + 2)
                pool.tensor_copy(si[:, b, :], sidx[:, bass.ds(i * GRP + u, 1)]).then_inc(si_ready, 1)
                pool.wait_ge(si_ready, n + 1)
                carry_wait()
                sized(pas, i * GRP + u, lambda rows: pool.indirect_dma_start(
                    out=y_dram[:], out_offset=bass.IndirectOffsetOnAxis(ap=si[0:rows, b, :], axis=0),
                    in_=YS[0:rows, b, :], in_offset=None, bounds_check=last_row,
                    oob_is_err=False).then_inc(scattered[b], 16))

            def group(pas, i, last=False):
                for u in range(GRP):
                    if u == 1 and not last:
                        stage_group(pas, i + AHEAD, False)
                    if not (last and u + 3 >= GRP):
                        gather(pas, i, u + 3)
                    if u < 2:
                        if pas == 0 and isinstance(i, int) and i == 0:
                            pass
                        else:
                            pool.wait_ge(scattered[u % 2], (i * 2 + 32 * pas) * 16)
                    else:
                        pool.wait_ge(scattered[u % 2], (i * 2 + (32 * pas + 1)) * 16)
                    scatter(pas, i, u)

            def run_pass(pas):
                stage_group(pas, 0, pas == 0)
                stage_group(pas, 1, False)
                for u in range(2):
                    gather(pas, 0, u, first=True)
                gather(pas, 0, 2)
                group(pas, 0)
                with pool.Fori(1, NGRP - 1) as i:
                    group(pas, i)
                group(pas, NGRP - 1, last=True)
                for b in range(2):
                    pool.wait_ge(scattered[b], 16 * 32 * (pas + 1))

            run_pass(0)
            over = pool.value_load(oflag[0:1, 0:1], min_val=0, max_val=1)
            with pool.If(over > 0):
                run_pass(1)
            with pool.Else():
                pool.nop()
            pool.memset(rcur[:], 0.0).then_inc(moe_done, 1)

        @block.scalar
        def _(act):
            count = [0]

            def link(ins):
                count[0] += 1
                ins.then_inc(act_step, 1)
                act.wait_ge(act_step, count[0])

            act.dma_start(ccol[:], c[0].rearrange("(p k) -> p k", p=P)).then_inc(small_in, 16)
            act.dma_start(prm[R_CA:R_CS, :], conv_a_w[0].rearrange("k (b q) -> (k b) q", q=P)).then_inc(params_in, 16)
            act.dma_start(prm[R_CS:R_CB, :], ssm_conv_w[0].rearrange("k (b q) -> (k b) q", q=P)).then_inc(params_in, 16)
            act.dma_start(prm[R_CB:R_NG, :], ssm_conv_b[0].rearrange("(b q) -> b q", q=P)).then_inc(params_in, 16)
            act.dma_start(prm[R_NG:R_NM, :], ssm_norm_g[0].rearrange("(b q) -> b q", q=P)).then_inc(params_in, 16)
            act.dma_start(prm[R_NM:R_END, :], norm_mix_g[0].rearrange("(b q) -> b q", q=P)).then_inc(params_in, 16)
            act.dma_start(hrow[:, 0, :], ssm_dt_bias[0].partition_broadcast(P)).then_inc(small_in, 16)
            act.dma_start(hrow[:, 1, :], ssm_a_log[0].partition_broadcast(P)).then_inc(small_in, 16)
            for half in range(2):
                act.dma_start(dskip[HD * half:HD * half + HD, :],
                              ssm_d[0].rearrange("(b q) -> q b", q=2)[half].partition_broadcast(HD),
                              allow_slow_non_contiguous=True).then_inc(small_in, 16)
            act.dma_start(rbias[:], router_bias[0].partition_broadcast(P)).then_inc(small_in, 16)
            act.wait_ge(mod_zero, 1)
            act.dma_start(MOD[0:1, :], b_ada[0:1, :]).then_inc(bada_in, 16)
            act.nop().then_inc(small_issued, 1)
            act.dma_start(WR[:], w_router[0].rearrange("(p k) n -> p k n", p=P)).then_inc(gains_in, 16)
            act.dma_start(gffn[:], norm_ffn_g[0].partition_broadcast(P)).then_inc(gains_in, 16)
            act.dma_start(gfin[:], norm_final_g.partition_broadcast(P)).then_inc(gains_in, 16)

            act.wait_ge(x_in, 16)
            for t in range(TT):
                act.activation(XN[:, t, :], X[:, t, :], ACT.Square, accum_out=small[:, t:t + 1]).then_inc(ss_ready, 1)
            act.wait_ge(ms_ready, 1)
            act.activation(small[:, 4:6], small[:, 2:4], ACT.Sqrt).then_inc(std_ready, 1)
            act.wait_ge(rstd_ready, 1)
            act.wait_ge(ss_ready, TT)
            for t in range(TT):
                act.activation(XN[:, t, :], X[:, t, :], ACT.Copy, scale=small[:, 6 + t:7 + t]).then_inc(xn_ready, 1)
            act.wait_ge(prm_ps, 1)
            act.copy(COL[:], PS[:, 7, 0:R_END]).then_inc(col_ready, 1)
            act.wait_ge(xnT_ps, 1)
            for b in range(4):
                act.copy(hT[:, 2 * b:2 * b + 2, :].rearrange("p k n -> p (k n)"), bank(2 + b)).then_inc(xnT_ready, 1)

            def exp_step(n, dst, src):
                act.wait_ge(exp_in, n)
                act.activation(dst, src, ACT.Exp).then_inc(exp_out, 1)

            act.wait_ge(small_in, 16 * 6)
            act.activation(dtv[:, 8, 0:NH], hrow[:, 1, :], ACT.Exp).then_inc(exp_out, 1)
            exp_step(1, dtv[:, 2, :], dtv[:, 1, :])

            nconv = [0]

            def silu_conv(b):
                nconv[0] += 1
                act.wait_ge(conv_ready, nconv[0])
                act.activation(XC[:, b, :], XC[:, b, :], ACT.Silu,
                               bias=COL[:, R_CB + b:R_CB + b + 1]).then_inc(xbc_ready, 1)

            act.wait_ge(consts, 1)
            for q, m in enumerate(ORDER):
                if m < 4 or (8 <= m < 12):
                    act.wait_ge(conv_ready, XB)
                act.wait_ge(proj_mm, q + 1)
                src = PS[:, 2 + q % QB, 0:TOK]
                if m >= 16:
                    act.copy(XP[:, m - 16, SK - 1:SK - 1 + TOK], src).then_inc(proj_evac, 1)
                elif m >= 12:
                    act.activation(SZ[:, m - 12, :], src, ACT.Silu).then_inc(proj_evac, 1)
                elif m >= 8:
                    act.copy(CU[:, m - 8, :], src).then_inc(proj_evac, 1)
                elif m >= 4:
                    act.copy(CC[:, m - 4, CK - 1:CK - 1 + TOK], src).then_inc(proj_evac, 1)
                else:
                    act.copy(CB[:, m, :], src).then_inc(proj_evac, 1)
                if q == 11:
                    for b in CONVS:
                        silu_conv(b)
                if q in (15, 16):
                    for v in ((0,) if q == 15 else (1, 2)):
                        act.wait_ge(decay_in, v + 1)
                        act.activation(E[:, v, :, :], E[:, v, :, :], ACT.Exp).then_inc(decay_ready, 1)
            act.wait_ge(yms_ready, 1)
            act.activation(RSB[:, 0, :], RSB[:, 0, :], ACT.Sqrt).then_inc(ystd_ready, 1)

            def copy_mod_rows(rows):
                for r in rows:
                    act.wait_ge(modrow_ps, r + 1)
                    act.copy(MOD[:, 2 * D + 512 * r:2 * D + 512 * r + 512], bank(r % 2)).then_inc(modrow_ready, 1)

            copy_mod_rows(range(6))
            for t in range(TT):
                act.wait_ge(x2_ready, 2 * t + 2)
                act.activation(T1[:, t, :], X[:, t, :], ACT.Square,
                               accum_out=small[:, t:t + 1]).then_inc(ss_ready, 1)
                act.wait_ge(ms_ready, t + 2)
                act.activation(small[:, 4 + t:5 + t], small[:, 2 + t:3 + t], ACT.Sqrt).then_inc(std_ready, 1)
                act.wait_ge(h2_ready, t + 1)
                act.dma_start(h2_dram[t * P:(t + 1) * P, :], H2P[:, t, :]).then_inc(h2_stored, 16)
            copy_mod_rows(range(6, 8))
            for b in range(4):
                act.wait_ge(h2T_ps, b + 1)
                act.copy(hT[:, 2 * b:2 * b + 2, :].rearrange("p k n -> p (k n)"), bank(2 + b)).then_inc(h2T_ready, 1)
            act.wait_ge(logit_ps, 1)
            act.activation(score, PS[:, 7, 0:TT * NE].rearrange("p (t e) -> p t e", t=TT),
                           ACT.Sigmoid).then_inc(score_ready, 1)
            for t in range(TT):
                act.wait_ge(sgu_ps, t + 1)
                act.activation(SG[:, t, :], PS[:, 2 + t, 0:FE], ACT.Silu).then_inc(ssg_ready, 1)
            for t in range(TT):
                act.wait_ge(shT_ps, t + 1)
                act.copy(HTT.rearrange("p c n -> p (c n)"), PS[:, 6, 0:FE]).then_inc(shT_ready, 1)
                act.wait_ge(sy_ps, t + 1)
                act.copy(SH[:, t, :].rearrange("p (a n) -> p a n", a=2), PS[:, 4:6, :]).then_inc(sh_ready, 1)

            def copy_xT(n):
                act.wait_ge(xT_ps, n + 1)
                act.copy(XTH[:, 0:4, :].rearrange("p k n -> p (k n)"), bank(0)).then_inc(xhi_ready, 1)

            def split_hi(n, u, g):
                k0, k1 = SPLITS[g]
                s = e_slot(u % GRP)
                if g == 0:
                    act.wait_ge(gu_loaded[s], gu_count(n, u))
                if not (isinstance(n, int) and n == 0):
                    act.wait_ge(split_used, n * NSP + (g + 1 - NSP))
                act.copy(WHI[g][:], gu_w(s)[:, :, k0:k1, :].rearrange("p a k n -> p k a n")).then_inc(whi_ready, 1)

            def silu_gate(n, u):
                act.wait_ge(split_used, n * NSP + NSP)
                act.activation(SG[:, u % 2, :], PS[:, 2 + u % 2, 0:FE], ACT.Silu).then_inc(sg_ready, 1)

            def group(pas, i, last=False):
                for u in range(GRP):
                    n = number(pas, i, u)
                    if not (last and u >= 2):
                        for g in range(EARLY):
                            split_hi(n + 2, u + 2, g)
                    if not (last and u == 3):
                        act.wait_ge(hid_ready, n)
                        silu_gate(n + 1, u + 1)
                    act.wait_ge(hidT_ps, n + 1)
                    act.copy(HTT.rearrange("p c n -> p (c n)"), PS[:, 6, 0:FE]).then_inc(hidT_ready, 1)
                    if not (last and u >= 2):
                        copy_xT(n + 2)
                        for g in range(EARLY, NSP):
                            split_hi(n + 2, u + 2, g)
                    act.wait_ge(expert_done, n + 1)
                    if u >= 2:
                        act.wait_ge(scattered[u % 2], (i * 2 + (32 * pas + 1)) * 16)
                    elif not (isinstance(i, int) and i == 0 and pas == 0):
                        act.wait_ge(scattered[u % 2], (i * 2 + 32 * pas) * 16)
                    act.copy(YS[:, u % 2, 0:512], bank(4)).then_inc(y_ready, 1)

            def run_pass(pas):
                n = NE * pas
                if pas == 0:
                    act.wait_ge(sgu_ps, TT)
                    act.wait_ge(h2_stored, 16 * TT)
                for g in range(NSP):
                    split_hi(n, 0, g)
                copy_xT(n)
                for g in range(EARLY):
                    split_hi(n + 1, 1, g)
                silu_gate(n, 0)
                copy_xT(n + 1)
                for g in range(EARLY, NSP):
                    split_hi(n + 1, 1, g)
                group(pas, 0)
                with act.Fori(1, NGRP - 1) as i:
                    group(pas, i)
                group(pas, NGRP - 1, last=True)

            run_pass(0)
            over = act.value_load(oflag[0:1, 0:1], min_val=0, max_val=1)
            with act.If(over > 0):
                run_pass(1)
            with act.Else():
                act.nop()
            for t in range(TT):
                act.wait_ge(fin_ss, t + 1)
                act.activation(SH[:, t, :], X[:, t, :], ACT.Square, accum_out=small[:, t:t + 1]).then_inc(ss_ready, 1)
                act.wait_ge(fin_ms, t + 1)
                act.activation(small[:, 4 + t:5 + t], small[:, 2 + t:3 + t], ACT.Sqrt).then_inc(fin_std, 1)

        @block.vector
        def _(dve):
            counts = {}

            def signal(ins, s):
                ins.then_inc(s, 1)
                counts[id(s)] = counts.get(id(s), 0) + 1
                return counts[id(s)]

            def link(ins, s=None):
                s = dve_step if s is None else s
                dve.wait_ge(s, signal(ins, s))

            dve.wait_ge(ss_ready, TT)
            link(dve.tensor_scalar(small[:, 2:4], small[:, 0:2], 1.0 / D, EPS, ALU.mult, ALU.add), ms_ready)
            dve.wait_ge(std_ready, 1)
            link(dve.reciprocal(small[:, 6:8], small[:, 4:6]), rstd_ready)

            def ada(j):
                n = load_no(A, j)
                w = ada_w(n)
                if j == 2:
                    dve.wait_ge(ada2_half, 16)
                else:
                    dve.wait_ge(loaded[slot_of(n)], loaded_count(n))
                dst = MOD[:, PIECE * j:PIECE * j + PIECE]
                for k in range(KD):
                    if j == 2 and k == KD // 2:
                        dve.wait_ge(loaded[slot_of(n)], loaded_count(n))
                    ins = dve.scalar_tensor_tensor(out=dst, in0=w[:, k, :], scalar=ccol[:, k:k + 1], in1=dst,
                                                   op0=ALU.mult, op1=ALU.add)
                    link(ins, ada_acc if k == KD - 1 else None)

            dve.wait_ge(bada_in, 16)
            dve.wait_ge(small_in, 16 * 6)
            for j in range(3):
                ada(j)
            dve.wait_ge(modcol_ps, 1)
            dve.wait_ge(col_ready, 1)
            link(dve.scalar_tensor_tensor(out=AB1[:, 0:KD], in0=PS[:, 0, KD:2 * KD], scalar=1.0,
                                          in1=COL[:, R_NM:R_END], op0=ALU.add, op1=ALU.mult))
            link(dve.tensor_copy(AB1[:, KD:2 * KD], PS[:, 0, 0:KD]))
            dve.wait_ge(xnT_ready, 4)
            for k in range(KD):
                signal(dve.tensor_scalar(hT[:, k, :], hT[:, k, :], AB1[:, k:k + 1], AB1[:, KD + k:KD + k + 1],
                                         ALU.mult, ALU.add), h1_ready)

            s_, n_, u_, w_, z_, z2_, p_, dt_, a_ = (dtv[:, i, :] for i in (0, 1, 2, 3, 4, 5, 6, 7, 9))
            dve.wait_ge(dt_ps, 1)
            link(dve.tensor_tensor(s_.rearrange("p (t h) -> p t h", t=TT),
                                   PS[:, 7, 0:TT * NH].rearrange("p (t h) -> p t h", t=TT),
                                   hrow[:, 0, :].unsqueeze(1).to_broadcast([P, TT, NH]), ALU.add))
            link(dve.tensor_scalar(n_, s_, -1.0, None, ALU.mult))
            link(dve.tensor_tensor(n_, n_, s_, ALU.min), exp_in)
            link(dve.tensor_scalar(s_, s_, 0.0, None, ALU.max))
            dve.wait_ge(exp_out, 2)
            link(dve.tensor_scalar(w_, u_, 2.0, None, ALU.add))
            link(dve.reciprocal(w_, w_))
            link(dve.tensor_tensor(z_, u_, w_, ALU.mult))
            link(dve.tensor_tensor(z2_, z_, z_, ALU.mult))
            link(dve.tensor_scalar(p_, z2_, 1.0 / 17, None, ALU.mult))
            for c_ in (15, 13, 11, 9, 7, 5, 3):
                link(dve.scalar_tensor_tensor(out=p_, in0=p_, scalar=1.0 / c_, in1=z2_, op0=ALU.add, op1=ALU.mult))
            link(dve.scalar_tensor_tensor(out=p_, in0=p_, scalar=1.0, in1=z_, op0=ALU.add, op1=ALU.mult))
            link(dve.scalar_tensor_tensor(out=dt_, in0=p_, scalar=2.0, in1=s_, op0=ALU.mult, op1=ALU.add))
            link(dve.scalar_tensor_tensor(out=a_.rearrange("p (t h) -> p t h", t=TT),
                                          in0=dt_.rearrange("p (t h) -> p t h", t=TT), scalar=-1.0,
                                          in1=dtv[:, 8, 0:NH].unsqueeze(1).to_broadcast([P, TT, NH]),
                                          op0=ALU.mult, op1=ALU.mult))
            link(dve.tensor_copy(AB.rearrange("p t h n -> p (t h) n"),
                                 a_.unsqueeze(2).to_broadcast([P, TT * NH, P])), a_ready)

            evac = {m: q + 1 for q, m in enumerate(ORDER)}

            def conv(b):
                dve.wait_ge(proj_evac, evac[16 + b])
                w = [COL[:, R_CS + k * XB + b:R_CS + k * XB + b + 1] for k in range(SK)]
                link(dve.tensor_scalar(XC[:, b, :], XP[:, b, 0:TOK], w[0], None, ALU.mult))
                for k in range(1, SK):
                    link(dve.scalar_tensor_tensor(out=XC[:, b, :], in0=XP[:, b, k:k + TOK], scalar=w[k],
                                                  in1=XC[:, b, :], op0=ALU.mult, op1=ALU.add),
                         conv_ready if k == SK - 1 else None)

            ada(3)
            for b in CONVS[0:3]:
                conv(b)
            ada(4)
            for b in CONVS[3:6]:
                conv(b)
            dve.wait_ge(cs_ps, 1)
            link(dve.tensor_copy(csv[:, 0:3 * NH], PS[:, 7, 32:32 + 3 * NH]))
            link(dve.tensor_tensor(csv[:, 3 * NH:4 * NH], csv[:, 2 * NH:3 * NH], csv[:, 0:NH], ALU.subtract), cs_ready)
            for b in CONVS[6:8]:
                conv(b)
            ada(5)
            dve.wait_ge(xsT_ps, 1)
            for t in range(TT):
                signal(dve.tensor_tensor(DTX[:, t, :].rearrange("p (h n) -> p h n", h=NH),
                                         bank(t).rearrange("p (h n) -> p h n", h=NH),
                                         dt_[:, t * NH:(t + 1) * NH].unsqueeze(2).to_broadcast([P, NH, HD]),
                                         ALU.mult), dtx_ready)
            for t in range(TT):
                dve.wait_ge(csrow_ps, t + 1)
                for v in ([0] if t == 0 else [1, 2]):
                    for h in range(NH):
                        src = PS[:, h // 4, (h % 4) * P:(h % 4) * P + P]
                        if v < 2:
                            ins = dve.tensor_scalar(E[:, v, h, :], src, csv[:, v * NH + h:v * NH + h + 1], 0.0,
                                                    ALU.subtract, ALU.min)
                        else:
                            ins = dve.tensor_scalar(E[:, v, h, :], src, csv[:, 3 * NH + h:3 * NH + h + 1], 0.0,
                                                    ALU.add, ALU.min)
                        if h < NH - 1:
                            continue
                        signal(ins, decay_in)
                dve.wait_ge(decay_in, 1 + 2 * t)
                signal(dve.memset(small[:, 10:11], 0.0), csrow_used)
            dve.wait_ge(cb_ps, 1)
            for g in range(NG):
                for v in range(3):
                    src = PS[:, g, v * P:(v + 1) * P]
                    if v < 2:
                        ins = dve.tensor_tensor(CBT[:, v, g, :], src, tri[:], ALU.mult)
                    else:
                        ins = dve.tensor_copy(CBT[:, v, g, :], src)
                    signal(ins, cb_used)
            dve.wait_ge(cb_used, 3 * NG)
            dve.wait_ge(decay_ready, 3)
            for v in range(3):
                for g in range(NG):
                    e = E[:, v, HPG * g:HPG * g + HPG, :]
                    signal(dve.tensor_tensor(e, e, CBT[:, v, g, :].unsqueeze(1).to_broadcast([P, HPG, P]),
                                             ALU.mult), wts_ready)
            ada(6)
            dve.wait_ge(y_ps, 1)
            for b in range(CBLK):
                src = PS[:, b // 2, (b % 2) * TOK:(b % 2) * TOK + TOK]
                signal(dve.scalar_tensor_tensor(out=YC[:, CBLK + b, :], in0=XC[:, b, :], scalar=dskip[:, b:b + 1],
                                                in1=src, op0=ALU.mult, op1=ALU.add), y_used)
            dve.wait_ge(y_used, CBLK)
            yb = YC[:, CBLK:2 * CBLK, :]
            link(dve.tensor_tensor(yb, yb, SZ, ALU.mult))
            link(dve.tensor_tensor(SQ, yb, yb, ALU.mult), sq_ready)
            dve.wait_ge(yss_ps, 1)
            link(dve.tensor_scalar(RSB[:, 0, :], PS[:, 7, 0:TOK], 1.0 / DS, EPS, ALU.mult, ALU.add), yms_ready)
            dve.wait_ge(ystd_ready, 1)
            link(dve.reciprocal(RSB[:, 1, :], RSB[:, 0, :]))
            for b in range(CBLK):
                signal(dve.scalar_tensor_tensor(out=YC[:, CBLK + b, :], in0=YC[:, CBLK + b, :],
                                                scalar=COL[:, R_NG + b:R_NG + b + 1], in1=RSB[:, 1, :],
                                                op0=ALU.mult, op1=ALU.mult), yb_ready)
            ada(7)
            for b in (2, 3, 0, 1):
                dve.wait_ge(proj_evac, max(evac[4 + b], evac[8 + b], evac[b]))
                cc = CC[:, b, CK - 1:CK - 1 + TOK]
                link(dve.tensor_tensor(cc, cc, CU[:, b, :], ALU.mult))
                w = [COL[:, R_CA + k * CBLK + b:R_CA + k * CBLK + b + 1] for k in range(CK)]
                link(dve.tensor_scalar(YC[:, b, :], CC[:, b, 0:TOK], w[0], None, ALU.mult))
                for k in range(1, CK):
                    link(dve.scalar_tensor_tensor(out=YC[:, b, :], in0=CC[:, b, k:k + TOK], scalar=w[k],
                                                  in1=YC[:, b, :], op0=ALU.mult, op1=ALU.add))
                signal(dve.tensor_tensor(YC[:, b, :], YC[:, b, :], CB[:, b, :], ALU.mult), ya_ready)
            dve.wait_ge(gains_in, 16 * 3)
            dve.wait_ge(modrow_ready, 6)
            link(dve.scalar_tensor_tensor(out=MOD[:, 4 * D:5 * D], in0=MOD[:, 4 * D:5 * D], scalar=1.0, in1=gffn[:],
                                          op0=ALU.add, op1=ALU.mult))
            for t in range(TT):
                for h in range(2):
                    r = 2 * t + h
                    cols = slice(512 * h, 512 * h + 512)
                    dve.wait_ge(mix_ps, r + 1)
                    link(dve.tensor_tensor(T1[:, t, cols], bank(2 + r), MOD[:, 2 * D + 512 * h:2 * D + 512 * h + 512],
                                           ALU.mult))
                    link(dve.tensor_tensor(X[:, t, cols], X[:, t, cols], T1[:, t, cols], ALU.add), x2_ready)
                dve.wait_ge(ss_ready, TT + t + 1)
                link(dve.tensor_scalar(small[:, 2 + t:3 + t], small[:, t:t + 1], 1.0 / D, EPS, ALU.mult, ALU.add),
                     ms_ready)
                dve.wait_ge(std_ready, t + 2)
                link(dve.reciprocal(small[:, 8 + t:9 + t], small[:, 4 + t:5 + t]))
                link(dve.scalar_tensor_tensor(out=T1[:, t, :], in0=X[:, t, :], scalar=small[:, 8 + t:9 + t],
                                              in1=MOD[:, 4 * D:5 * D], op0=ALU.mult, op1=ALU.mult))
                link(dve.tensor_tensor(H2P[:, t, :].rearrange("p (k q) -> p q k", k=KD),
                                       T1[:, t, :].rearrange("p (q k) -> p q k", k=KD),
                                       MOD[:, 3 * D:4 * D].rearrange("p (q k) -> p q k", k=KD), ALU.add), h2_ready)

            dve.wait_ge(score_ready, 1)
            link(dve.tensor_tensor(sel, score, rbias[:].unsqueeze(1).to_broadcast([P, TT, NE]), ALU.add))
            n = 0
            for t in range(TT):
                for g in range(NGR):
                    n = signal(dve.max(top8[:, t, g, :], sel[:, t, 8 * g:8 * g + 8]), dve_step)
            dve.wait_ge(dve_step, n)
            link(dve.tensor_tensor(gs, top8[:, :, :, 0], top8[:, :, :, 1], ALU.add))
            mine = gs.unsqueeze(3).to_broadcast([P, TT, NGR, NGR])
            other = gs.unsqueeze(2).to_broadcast([P, TT, NGR, NGR])
            link(dve.tensor_tensor(gpair, other, mine, ALU.is_equal))
            link(dve.tensor_tensor(gpair, gpair, lower[:].unsqueeze(1).to_broadcast([P, TT, NGR, NGR]), ALU.mult))
            link(dve.tensor_tensor(gpair2, other, mine, ALU.is_gt))
            link(dve.tensor_tensor(gpair, gpair, gpair2, ALU.add))
            link(dve.tensor_reduce(grank, gpair, AX.X, ALU.add))
            link(dve.tensor_scalar(grank, grank, float(TOPG), None, ALU.is_lt))
            gmask = grank.unsqueeze(3).to_broadcast([P, TT, NGR, NE // NGR])
            link(dve.tensor_tensor(msel.rearrange("p t (g j) -> p t g j", g=NGR),
                                   sel.rearrange("p t (g j) -> p t g j", g=NGR), gmask, ALU.mult))
            link(dve.tensor_scalar(gs, grank, 1e30, -1e30, ALU.mult, ALU.add))
            link(dve.tensor_tensor(msel.rearrange("p t (g j) -> p t g j", g=NGR),
                                   msel.rearrange("p t (g j) -> p t g j", g=NGR),
                                   gs.unsqueeze(3).to_broadcast([P, TT, NGR, NE // NGR]), ALU.add))
            for t in range(TT):
                link(dve.max(m8[:, t, :], msel[:, t, :]))
                link(dve.match_replace(out=maskf[:, t, :], in_to_replace=m8[:, t, :], in_values=msel[:, t, :],
                                       imm_value=-3e30))
            link(dve.tensor_scalar(maskf, maskf, -3e30, None, ALU.is_equal))
            link(dve.tensor_copy(maskb, maskf), mask_ready)
            link(dve.tensor_tensor(gates, score, maskf, ALU.mult))
            link(dve.tensor_reduce(grank[:, :, 0:1], gates, AX.X, ALU.add))
            link(dve.reciprocal(grank[:, :, 0:1], grank[:, :, 0:1]))
            for t in range(TT):
                link(dve.tensor_scalar(gates[:, t, :], gates[:, t, :], grank[:, t, 0:1], ROUTED_SCALE,
                                       ALU.mult, ALU.mult))
            for part_no in range(3):
                rt = RT[:, :, 0:NE, 2 + part_no]
                link(dve.tensor_copy(rt, gates))
                if part_no < 2:
                    link(dve.tensor_tensor(gates, gates, rt, ALU.subtract))
            link(dve.tensor_copy(RT[:, :, 0:NE, 0], tokid[:].unsqueeze(2).to_broadcast([P, TT, NE])))
            link(dve.memset(cumA, 0.0))
            link(dve.memset(cumB, 0.0))
            link(dve.tensor_copy(cumA[:, :, 33:96], maskf[:, :, 0:63]))
            src_, dst_ = cumA, cumB
            for sh in (1, 2, 4, 8, 16, 32):
                link(dve.tensor_tensor(dst_[:, :, 32:96], src_[:, :, 32:96], src_[:, :, 32 - sh:96 - sh], ALU.add))
                src_, dst_ = dst_, src_
            link(dve.tensor_copy(RT[:, :, 0:NE, 1], src_[:, :, 32:96]))
            dve.wait_ge(rank_ps, 1)
            link(dve.tensor_scalar(rankm[:, :, 0:NE], PS[:, 7, 0:W64].rearrange("p (t e) -> p t e", t=TT), 1.0, None,
                                   ALU.add))
            link(dve.tensor_tensor(rankm[:, :, 0:NE], rankm[:, :, 0:NE], maskf, ALU.mult))
            link(dve.tensor_scalar(rankm[:, :, 0:NE], rankm[:, :, 0:NE], -1.0, None, ALU.add))
            link(dve.tensor_copy(counts_u[:, 0:NE], PS[:, 7, W64:W64 + NE]))
            link(dve.tensor_reduce(small[:, 12:13], PS[:, 7, W64:W64 + NE], AX.X, ALU.max))
            link(dve.tensor_scalar(oflag[:], small[:, 12:13], P + 0.5, None, ALU.is_gt), table_ready)
            signal(dve.memset(small[:, 13:14], 0.0), table_ready)

            def decode(pas, g):
                n = g + PASS_GROUPS * pas
                cols = bass.ds(g * GRP, GRP)
                dve.wait_ge(slot_ps, n + 1)
                ps = PS[:, 7, 0:GRP * NCOL].rearrange("p (e c) -> p e c", e=GRP)
                dve.tensor_copy(dec[:, 0, :], ps[:, :, 1]).then_inc(dec_step, 1)
                dve.tensor_scalar(gidx[:, cols], ps[:, :, 0], float(TOK), None, ALU.add).then_inc(slot_ready, 1)
                dve.wait_ge(dec_step, n * 2 + 1)
                dve.scalar_tensor_tensor(out=dec[:, 1, :], in0=ps[:, :, 0], scalar=float(TOPK), in1=dec[:, 0, :],
                                         op0=ALU.mult, op1=ALU.add).then_inc(dec_step, 1)
                dve.tensor_reduce(gate[:, cols], ps[:, :, 2:5], AX.X, ALU.add).then_inc(slot_ready, 1)
                dve.wait_ge(dec_step, n * 2 + 2)
                dve.tensor_scalar(sidx[:, cols], dec[:, 1, :], float(TOK * TOPK), None, ALU.add).then_inc(slot_ready, 1)

            def one_hots(pas, g):
                n = g + PASS_GROUPS * pas
                dve.wait_ge(cur_copied, n * 2 + 2)
                if not (isinstance(n, int) and n == 0):
                    dve.wait_ge(slot_ps, n)
                for t in range(TT):
                    dve.tensor_tensor(onehot[:, t, :, :], rcur[:, t, :].unsqueeze(2).to_broadcast([P, GRP, P]),
                                      slots[:, pas, :].unsqueeze(1).to_broadcast([P, GRP, P]),
                                      ALU.is_equal).then_inc(onehot_ready, 1)

            def copy_xT(n):
                dve.wait_ge(xT_ps, n + 1)
                dve.tensor_copy(XTH[:, 4:8, :].rearrange("p k n -> p (k n)"), bank(1)).then_inc(xT_ready, 1)
                dve.wait_ge(xT_ready, n * 3 + 1)
                for h, b in ((1, 1), (0, 0)):
                    if h == 0:
                        dve.wait_ge(xhi_ready, n + 1)
                    dve.tensor_tensor(XTL[:, 4 * h:4 * h + 4, :].rearrange("p k n -> p (k n)"), bank(b),
                                      XTH[:, 4 * h:4 * h + 4, :].rearrange("p k n -> p (k n)").bitcast(F32),
                                      ALU.subtract).then_inc(xT_ready, 1)

            def split_lo(n, u, g):
                k0, k1 = SPLITS[g]
                dve.wait_ge(whi_ready, n * NSP + (g + 1))
                dve.tensor_tensor(WLO[g][:], gu_w(e_slot(u % GRP))[:, :, k0:k1, :].rearrange("p a k n -> p k a n"),
                                  WHI[g][:].bitcast(F32), ALU.subtract).then_inc(wlo_ready, 1)

            def hidden(n, i, u):
                dve.wait_ge(sg_ready, n + 1)
                dve.scalar_tensor_tensor(out=HID[:, u % 2, :].rearrange("p (c q) -> p q c", c=FT),
                                         in0=SG[:, u % 2, :].rearrange("p (q c) -> p q c", c=FT),
                                         scalar=gate[:, bass.ds(i * GRP + u, 1)],
                                         in1=PS[:, 2 + u % 2, FE:2 * FE].rearrange("p (q c) -> p q c", c=FT),
                                         op0=ALU.mult, op1=ALU.mult).then_inc(hid_ready, 1)

            def shared_hidden():
                for t in range(TT):
                    dve.wait_ge(ssg_ready, t + 1)
                    signal(dve.tensor_tensor(HID[:, t, :].rearrange("p (c q) -> p q c", c=FT),
                                             SG[:, t, :].rearrange("p (q c) -> p q c", c=FT),
                                             PS[:, 2 + t, FE:2 * FE].rearrange("p (q c) -> p q c", c=FT),
                                             ALU.mult), shid_ready)

            def group(pas, i, last=False):
                for u in range(GRP):
                    n = number(pas, i, u)
                    if not (last and u >= 2):
                        for g in range(EARLY):
                            split_lo(n + 2, u + 2, g)
                    if not (last and u == 3):
                        hidden(n + 1, i, u + 1)
                    if not (last and u >= 2):
                        copy_xT(n + 2)
                        for g in range(EARLY, NSP):
                            split_lo(n + 2, u + 2, g)
                    if u == 1 and not last:
                        one_hots(pas, i + AHEAD)
                    if u == 2 and not last:
                        decode(pas, i + AHEAD)
                    dve.wait_ge(expert_done, n + 1)
                    if u >= 2:
                        dve.wait_ge(scattered[u % 2], (i * 2 + (32 * pas + 1)) * 16)
                    elif not (isinstance(i, int) and i == 0 and pas == 0):
                        dve.wait_ge(scattered[u % 2], (i * 2 + 32 * pas) * 16)
                    dve.tensor_copy(YS[:, u % 2, 512:1024], bank(5)).then_inc(y_ready, 1)

            def run_pass(pas):
                n = NE * pas
                for g in range(AHEAD):
                    one_hots(pas, g)
                    decode(pas, g)
                if pas == 0:
                    shared_hidden()
                dve.wait_ge(slot_ready, (PASS_GROUPS * pas + 2) * 3)
                for g in range(NSP):
                    split_lo(n, 0, g)
                copy_xT(n)
                for g in range(EARLY):
                    split_lo(n + 1, 1, g)
                hidden(n, 0, 0)
                copy_xT(n + 1)
                for g in range(EARLY, NSP):
                    split_lo(n + 1, 1, g)
                group(pas, 0)
                with dve.Fori(1, NGRP - 1) as i:
                    dve.wait_ge(slot_ready, (i + (PASS_GROUPS * pas + 2)) * 3)
                    group(pas, i)
                dve.wait_ge(slot_ready, (NGRP - 1 + PASS_GROUPS * pas + 2) * 3)
                group(pas, NGRP - 1, last=True)

            run_pass(0)
            over = dve.value_load(oflag[0:1, 0:1], min_val=0, max_val=1)
            with dve.If(over > 0):
                run_pass(1)
            with dve.Else():
                dve.nop()

            dve.wait_ge(sh_ready, TT)
            dve.wait_ge(modrow_ready, 8)
            for t in range(TT):
                for h in range(2):
                    s = 2 * t + h
                    dve.wait_ge(y_loaded[s], 16)
                    for j in range(4):
                        link(dve.tensor_tensor(SH[:, t, :], SH[:, t, :], ring[:, s, j * D:(j + 1) * D], ALU.add))
                link(dve.tensor_tensor(SH[:, t, :], SH[:, t, :], MOD[:, 5 * D:6 * D], ALU.mult))
                link(dve.tensor_tensor(X[:, t, :], X[:, t, :], SH[:, t, :], ALU.add), fin_ss)
                dve.wait_ge(ss_ready, 2 * TT + t + 1)
                link(dve.tensor_scalar(small[:, 2 + t:3 + t], small[:, t:t + 1], 1.0 / D, EPS, ALU.mult, ALU.add),
                     fin_ms)
                dve.wait_ge(fin_std, t + 1)
                link(dve.reciprocal(small[:, 8 + t:9 + t], small[:, 4 + t:5 + t]))
                link(dve.scalar_tensor_tensor(out=X[:, t, :], in0=X[:, t, :], scalar=small[:, 8 + t:9 + t],
                                              in1=gfin[:], op0=ALU.mult, op1=ALU.mult), out_ready)

        @block.tensor
        def _(pe):
            pe.wait_ge(consts, 1)
            pe.wait_ge(params_in, 16 * 5)
            pe.transpose(PS[:, 7, 0:R_END], prm, ident[0:R_END, 0:R_END]).then_inc(prm_ps, 1)
            pe.wait_ge(xn_ready, TT)
            for k in range(KD):
                for t in range(TT):
                    m = pe.transpose(PS[:, 2 + k // 2, (k % 2) * TOK + t * P:(k % 2) * TOK + t * P + P],
                                     XN[:, t, k * P:(k + 1) * P], ident[:])
            m.then_inc(xnT_ps, 1)
            for j in range(2 * KD):
                pe.wait_ge(ada_acc, j * P // PIECE + 1)
                m = pe.matmul(PS[:, 0, j:j + 1], MOD[:, j * P:(j + 1) * P], ones[:, 0:1], start=True, stop=True)
            m.then_inc(modcol_ps, 1)

            pe.wait_ge(h1_ready, KD)
            pe.wait_ge(col_ready, 1)
            n3 = load_no(I, 3)
            pe.wait_ge(in3_late, 16)
            w3 = ring[:, slot_of(n3), 0:KD * LASTP].rearrange("p (k n) -> p k n", k=KD)
            for t in range(TT):
                for k in range(KD):
                    m = pe.matmul(PS[:, 7, t * NH:(t + 1) * NH], hT[:, k, t * P:(t + 1) * P],
                                  w3[:, k, PIECE:PIECE + NH], start=(k == 0), stop=(k == KD - 1))
            m.then_inc(dt_ps, 1)

            def project(q):
                m = ORDER[q]
                n = load_no(I, m // 6)
                if q % 6 == 0 and q or q == 3:
                    pe.wait_ge(loaded[slot_of(n)], loaded_count(n))
                width = LASTP if m // 6 == 3 else PIECE
                w = ring[:, slot_of(n), 0:KD * width].rearrange("p (k n) -> p k n", k=KD)
                if q >= QB:
                    pe.wait_ge(proj_evac, q - QB + 1)
                for k in range(KD):
                    mm = pe.matmul(PS[:, 2 + q % QB, 0:TOK], w[:, k, (m % 6) * P:(m % 6) * P + P], hT[:, k, :],
                                   start=(k == 0), stop=(k == KD - 1))
                mm.then_inc(proj_mm, 1)

            def cs_cols():
                pe.wait_ge(a_ready, 1)
                for t in range(TT):
                    pe.matmul(PS[:, 7, 32 + t * NH:32 + (t + 1) * NH], tri[:], dtv[:, 9, t * NH:(t + 1) * NH],
                              start=True, stop=True)
                pe.matmul(PS[:, 7, 48:48 + NH], ones[:], dtv[:, 9, 0:NH], start=True, stop=True).then_inc(cs_ps, 1)

            def xs_transposes():
                pe.wait_ge(xbc_ready, XB)
                for t in range(TT):
                    for b in range(CBLK):
                        m = pe.transpose(PS[:, t, b * P:(b + 1) * P], XC[:, b, t * P:(t + 1) * P], ident[:])
                m.then_inc(xsT_ps, 1)

            def cs_rows(t):
                if t == 0:
                    pe.wait_ge(dtx_ready, TT)
                else:
                    pe.wait_ge(csrow_used, t)
                for h in range(NH):
                    m = pe.matmul(PS[:, h // 4, (h % 4) * P:(h % 4) * P + P], AB[:, t, h, :], tri[:],
                                  start=True, stop=True)
                m.then_inc(csrow_ps, 1)

            def c_dot_b():
                pe.wait_ge(csrow_used, TT)
                for g in range(NG):
                    for v, (s, l) in enumerate(((0, 0), (1, 1), (0, 1))):
                        m = pe.matmul(PS[:, g, v * P:(v + 1) * P], XC[:, 4 + g, s * P:(s + 1) * P],
                                      XC[:, 6 + g, l * P:(l + 1) * P], start=True, stop=True)
                m.then_inc(cb_ps, 1)

            def y_heads():
                pe.wait_ge(wts_ready, 3 * NG)
                for h in range(NH):
                    b, r = h // 2, (h % 2) * HD
                    c0 = (b % 2) * TOK
                    lhs = [DTX[:, t, h * HD:(h + 1) * HD] for t in range(TT)]
                    pe.matmul(PS[r:r + HD, b // 2, c0:c0 + P], lhs[0], E[:, 0, h, :], start=True, stop=True)
                    pe.matmul(PS[r:r + HD, b // 2, c0 + P:c0 + TOK], lhs[0], E[:, 2, h, :], start=True, stop=False)
                    m = pe.matmul(PS[r:r + HD, b // 2, c0 + P:c0 + TOK], lhs[1], E[:, 1, h, :], start=False, stop=True)
                m.then_inc(y_ps, 1)

            def y_squares():
                pe.wait_ge(sq_ready, 1)
                for b in range(CBLK):
                    m = pe.matmul(PS[:, 7, 0:TOK], ones[:], SQ[:, b, :], start=(b == 0), stop=(b == CBLK - 1))
                m.then_inc(yss_ps, 1)

            for q in range(NQ):
                project(q)
                if q == 5:
                    cs_cols()
                if q == 13:
                    xs_transposes()
                if q == 14:
                    cs_rows(0)
                if q == 15:
                    cs_rows(1)
                if q == 16:
                    c_dot_b()
                if q == 18:
                    y_heads()
                if q == 21:
                    y_squares()

            def mod_rows(r):
                c0 = 2 * D + 512 * r
                pe.wait_ge(ada_acc, (c0 + 512 + PIECE - 1) // PIECE)
                if r >= 2:
                    pe.wait_ge(modrow_ready, r - 1)
                pe.matmul(bank(r % 2), ones[:], MOD[:, c0:c0 + 512], start=True, stop=True).then_inc(modrow_ps, 1)

            pe.wait_ge(y_used, CBLK)
            for r in range(2):
                mod_rows(r)
            pe.wait_ge(yb_ready, CBLK)
            pe.wait_ge(proj_evac, NQ)
            for j in range(2):
                n = load_no(O, j)
                pe.wait_ge(loaded[slot_of(n)], loaded_count(n))
            for t in range(TT):
                for h in range(2):
                    for place, k in enumerate(OUT_ORDER):
                        j = 0 if k < OUT_K[0][1] else 1
                        n = load_no(O, j)
                        if t == 0 and h == 0 and k < CBLK:
                            pe.wait_ge(ya_ready, place - CBLK + 1)
                        w = ring[:, slot_of(n), 0:6 * D].rearrange("p (k n) -> p k n", n=D)
                        m = pe.matmul(bank(2 + 2 * t + h), YC[:, k, t * P:(t + 1) * P],
                                      w[:, k - OUT_K[j][0], 512 * h:512 * h + 512],
                                      start=(place == 0), stop=(place == KD - 1))
                    m.then_inc(mix_ps, 1)
                if t == 0:
                    for r in range(2, 6):
                        mod_rows(r)
            for t in range(TT):
                pe.wait_ge(h2_ready, t + 1)
                if t == 0:
                    pe.wait_ge(x2_ready, 2 * TT)
                for k in range(KD):
                    m = pe.transpose(PS[:, 2 + k // 2, (k % 2) * TOK + t * P:(k % 2) * TOK + t * P + P],
                                     H2P[:, t, k * P:(k + 1) * P], ident[:])
                    if t == TT - 1 and k % 2:
                        m.then_inc(h2T_ps, 1)
                if t == 0:
                    for r in range(6, 8):
                        mod_rows(r)
            pe.wait_ge(gains_in, 16 * 3)
            for k in range(4):
                pe.wait_ge(h2T_ready, k + 1)
            for t in range(TT):
                for k in range(KD):
                    m = pe.matmul(PS[:, 7, t * NE:(t + 1) * NE], hT[:, k, t * P:(t + 1) * P], WR[:, k, :],
                                  start=(k == 0), stop=(k == KD - 1))
            m.then_inc(logit_ps, 1)

            def gate_up(dst, lhs, w):
                for k in range(KD):
                    m = pe.matmul(bank(dst).rearrange("p (a n) -> p a n", a=2), lhs[k], w[:, :, k, :],
                                  start=(k == 0), stop=(k == KD - 1))
                return m

            def hidden_transposes(b):
                for cc in range(FT):
                    m = pe.transpose(PS[:, 6, cc * P:(cc + 1) * P], HID[:, b, cc * P:(cc + 1) * P], ident[:])
                return m

            def down(s):
                w = down_w(s)
                for h in range(2):
                    for cc in range(FT):
                        m = pe.matmul(bank(4 + h), HTT[:, cc, :], w[:, cc, 512 * h:512 * h + 512],
                                      start=(cc == 0), stop=(cc == FT - 1))
                return m

            def slot_values(pas, g):
                n = g + PASS_GROUPS * pas
                pe.wait_ge(onehot_ready, n * 2 + 2)
                if not (isinstance(n, int) and n == 0):
                    pe.wait_ge(slot_ready, n * 3)
                else:
                    pe.wait_ge(table_ready, 1)
                for e in range(GRP):
                    for t in range(TT):
                        m = pe.matmul(PS[:, 7, e * NCOL:(e + 1) * NCOL], onehot[:, t, e, :], rtcur[:, t, e, :],
                                      start=(t == 0), stop=(t == TT - 1))
                m.then_inc(slot_ps, 1)

            ns = load_no(S, 0)
            pe.wait_ge(loaded[slot_of(ns)], loaded_count(ns))
            for t in range(TT):
                gate_up(2 + t, [hT[:, k, t * P:(t + 1) * P] for k in range(KD)], gu_w(slot_of(ns))).then_inc(sgu_ps, 1)
            pe.wait_ge(mask_ready, 1)
            pe.wait_ge(score_ready, 1)
            pe.matmul(PS[:, 7, 0:NE], trib[:], maskb[:, 0, :], start=True, stop=True)
            pe.matmul(PS[:, 7, NE:2 * NE], trib[:], maskb[:, 1, :], start=True, stop=False)
            pe.matmul(PS[:, 7, NE:2 * NE], onesb[:], maskb[:, 0, :], start=False, stop=True)
            pe.matmul(PS[:, 7, 2 * NE:3 * NE], onesb[:], maskb[:, 0, :], start=True, stop=False)
            pe.matmul(PS[:, 7, 2 * NE:3 * NE], onesb[:], maskb[:, 1, :], start=False, stop=True).then_inc(rank_ps, 1)
            for g in range(AHEAD):
                slot_values(0, g)
            for t in range(TT):
                pe.wait_ge(shid_ready, t + 1)
                if t:
                    pe.wait_ge(sh_ready, t)
                hidden_transposes(t).then_inc(shT_ps, 1)
                pe.wait_ge(shT_ready, t + 1)
                down(slot_of(ns)).then_inc(sy_ps, 1)

            def transposes(pas, i, u):
                n = number(pas, i, u)
                b = u % 2
                pe.wait_ge(gathered[b], (i * 2 + (32 * pas + u // 2 + 1)) * 16)
                if not (isinstance(n, int) and n == 0):
                    pe.wait_ge(xT_ready, n * 3)
                for k in range(KD):
                    m = pe.transpose(PS[:, k // 4, (k % 4) * P:(k % 4) * P + P], HG[:, b, k * P:(k + 1) * P], ident[:])
                m.then_inc(xT_ps, 1)

            def expert_gate_up(pas, i, u):
                n = number(pas, i, u)
                pe.wait_ge(xT_ready, n * 3 + 3)
                ps = bank(2 + u % 2).rearrange("p (a n) -> p a n", a=2)
                for g, (k0, k1) in enumerate(SPLITS):
                    pe.wait_ge(wlo_ready, n * NSP + (g + 1))
                    for k in range(k0, k1):
                        pe.matmul(ps, XTH[:, k, :], WHI[g][:, k - k0, :, :], start=(k == 0), stop=False)
                        pe.matmul(ps, XTH[:, k, :], WLO[g][:, k - k0, :, :], start=False, stop=False)
                        m = pe.matmul(ps, XTL[:, k, :], WHI[g][:, k - k0, :, :], start=False, stop=(k == KD - 1))
                    m.then_inc(split_used, 1)

            def group(pas, i, last=False):
                for u in range(GRP):
                    n = number(pas, i, u)
                    if not (last and u == 3):
                        if not (isinstance(n, int) and n == 0):
                            pe.wait_ge(hid_ready, n)
                        expert_gate_up(pas, i, u + 1)
                    pe.wait_ge(hid_ready, n + 1)
                    if not (isinstance(n, int) and n == 0):
                        pe.wait_ge(hidT_ready, n)
                    hidden_transposes(u % 2).then_inc(hidT_ps, 1)
                    if not (last and u >= 2):
                        transposes(pas, i, u + 2)
                    if u == 2 and not last:
                        slot_values(pas, i + AHEAD)
                    pe.wait_ge(hidT_ready, n + 1)
                    if isinstance(n, int) and n == 0:
                        pe.wait_ge(sh_ready, TT)
                    else:
                        pe.wait_ge(y_ready, n * 2)
                    pe.wait_ge(down_loaded[e_slot(u)], down_count(n, u))
                    down(e_slot(u)).then_inc(expert_done, 1)

            def run_pass(pas):
                if pas:
                    for g in range(AHEAD):
                        slot_values(pas, g)
                transposes(pas, 0, 0)
                expert_gate_up(pas, 0, 0)
                transposes(pas, 0, 1)
                group(pas, 0)
                with pe.Fori(1, NGRP - 1) as i:
                    group(pas, i)
                group(pas, NGRP - 1, last=True)

            run_pass(0)
            over = pe.value_load(oflag[0:1, 0:1], min_val=0, max_val=1)
            with pe.If(over > 0):
                run_pass(1)
            with pe.Else():
                pe.nop()


_INS = ["x", "c", "w_ada", "b_ada", "norm_mix_g", "w_in", "conv_a_w", "ssm_conv_w", "ssm_conv_b", "ssm_dt_bias",
        "ssm_a_log", "ssm_d", "ssm_norm_g", "w_out", "norm_ffn_g", "w_router", "router_bias", "we_gate", "we_up",
        "we_down", "ws_gate", "ws_up", "ws_down", "norm_final_g"]
_OUTS = [((1, 256, 1024), "float32")]


def kernel(**inputs):
    import numpy as _np
    import concourse.bacc as _bacc
    from concourse import mybir as _mybir
    from concourse.bass_utils import run_bass_kernel_spmd as _run

    nc = _bacc.Bacc("TRN2", target_bir_lowering=False, num_devices=1)
    arrays, args = {}, []
    for name in _INS:
        a = _np.ascontiguousarray(inputs[name])
        arrays[f"in_{name}_dram"] = a
        args.append(nc.dram_tensor(f"in_{name}_dram", a.shape, _mybir.dt.from_np(a.dtype), kind="ExternalInput").ap())
    for i, (shape, dtype) in enumerate(_OUTS):
        dt = _mybir.dt.from_np(_np.dtype(dtype))
        args.append(nc.dram_tensor(f"out_{i}_dram", shape, dt, kind="ExternalOutput").ap())
    build(nc, *args)
    r = _run(nc, [arrays], core_ids=[0])
    return r.results[0]["out_0_dram"]
```

```python
from contextlib import ExitStack

import concourse.bass as bass
from concourse import mybir

P = 128
F32 = mybir.dt.float32
BF16 = mybir.dt.bfloat16
F32R = mybir.dt.float32r
U32 = mybir.dt.uint32
ALU = mybir.AluOpType
ACT = mybir.ActivationFunctionType
AX = mybir.AxisListType

D = 1024
KD = D // P
TT = 2
TOK = TT * P
DC = 512
DS = 512
NH = 8
HD = 64
NG = 2
HPG = NH // NG
CBLK = DC // P
XB = (DS + 2 * NG * P) // P
CK = 3
SK = 4
EPS = 1e-6
NE = 64
NGR = 8
TOPG = 4
FE = 256
FT = FE // P
ROUTED_SCALE = 2.5

NSLOT = 4
PIECE = 768
LASTP = 776
SLOTW = KD * LASTP
GU = 2 * KD * FE
AHEAD = 2
GRP = 4
NGRP = NE // GRP
TG = NGRP + AHEAD
TE = TG * GRP
NCOL = 5
PASS_GROUPS = NGRP - 1 + AHEAD

SPLITS = [(0, 3), (3, 5), (5, 6), (6, 8)]
EARLY = 2
NSP = len(SPLITS)

HEIGHTS = [16, 32, 48, 64, 96, P]

R_CA, R_CS, R_CB, R_NG, R_NM = 0, CK * CBLK, CK * CBLK + SK * XB, CK * CBLK + SK * XB + XB, 56
R_END = R_NM + KD

A, I, O, S = "ada", "in", "out", "shared"
LOADS = [(A, 0, 0), (A, 1, 1), (A, 2, 2), (I, 3, 3), (A, 3, 1), (I, 2, 0), (A, 4, 2), (I, 1, 1), (A, 5, 2),
         (I, 0, 3), (A, 6, 2), (O, 0, 0), (S, 0, 1), (A, 7, 2), (O, 1, 3)]
FIRST_SLOT = 2
OUT_K = [(0, 6), (6, 8)]
OUT_ORDER = [4, 5, 6, 7, 2, 3, 0, 1]
ORDER = [21, 22, 23, 18, 19, 20, 16, 17, 12, 13, 14, 15, 8, 9, 10, 11, 6, 7, 4, 5, 2, 3, 0, 1]
FIRST = 2 * D - 2 * PIECE
CONVS = [5, 6, 7, 2, 3, 4, 0, 1]
LATE = 384
NQ = len(ORDER)
QB = 5


def n_dmas(what):
    return 3 if what == S else 1


def slot_of(n):
    return LOADS[n][2]


def loaded_count(n):
    return 16 * sum(n_dmas(what) for what, _, s in LOADS[:n + 1] if s == slot_of(n))


def build(nc, x, c, w_ada, b_ada, norm_mix_g, w_in, conv_a_w, ssm_conv_w, ssm_conv_b, ssm_dt_bias,
          ssm_a_log, ssm_d, ssm_norm_g, w_out, norm_ffn_g, w_router, router_bias, we_gate, we_up,
          we_down, ws_gate, ws_up, ws_down, norm_final_g, out):
    with ExitStack() as ctx:
        def sb(name, shape, dt=F32):
            return ctx.enter_context(nc.sbuf_tensor(name, shape, dt))

        def sem(name):
            return ctx.enter_context(nc.semaphore(name))

        h2_dram = nc.dram_tensor("h2_rows", [TOK, D], F32, kind="Internal").ap()
        y_dram = nc.dram_tensor("expert_sums", [TOK + P, D], F32, kind="Internal").ap()

        ring = sb("ring", [P, NSLOT, SLOTW])
        ring_at = nc.sbuf_base - 4 * NSLOT * SLOTW
        X = sb("X", [P, TT, D])
        hT_at = nc.sbuf_base
        hT = sb("hT", [P, KD, TOK])
        MOD_at = nc.sbuf_base
        MOD = sb("MOD", [P, 6 * D])
        gffn_at = nc.sbuf_base
        gffn = sb("gffn", [P, D])
        gfin = sb("gfin", [P, D])
        arena_at = nc.sbuf_base
        arena = sb("arena", [P, 13352])
        ident = sb("ident", [P, P])
        tri = sb("tri", [P, P])
        ones = sb("ones", [P, P])
        trib = sb("trib", [P, P], BF16)
        onesb = sb("onesb", [P, P], BF16)
        slots = sb("slots", [P, 2, P])
        WR = sb("WR", [P, KD, NE])
        COL = sb("COL", [P, R_END])
        ccol = sb("ccol", [P, KD])
        rbias = sb("rbias", [P, NE])
        hrow = sb("hrow", [P, 2, NH])
        dskip = sb("dskip", [P, CBLK])
        small = sb("small", [P, 16])
        dtv = sb("dtv", [P, 10, TT * NH])
        csv = sb("csv", [P, 4 * NH])
        AB1 = sb("AB1", [P, 2 * KD])
        lower = sb("lower", [P, NGR, NGR])
        minus_slot = sb("minus_slot", [P, 1])
        spare_row = sb("spare_row", [P, 1])
        tokid = sb("tokid", [P, TT])
        rankm = sb("rankm", [P, TT, TE])
        RT = sb("RT", [P, TT, TE, NCOL], BF16)
        gidx = sb("gidx", [P, TE], U32)
        counts_u = sb("counts_u", [P, TE], U32)
        sidx = sb("sidx", [P, TE], U32)
        gate = sb("gate", [P, TE])
        gi = sb("gi", [P, 2, 1], U32)
        si = sb("si", [P, 2, 1], U32)
        spare = sb("spare", [P, 2])
        oflag = sb("oflag", [P, 1], U32)
        PS = ctx.enter_context(nc.psum_tensor("PS", [P, 8, 512], F32))

        o = [0]

        def part(n):
            o[0] += n
            return arena[:, o[0] - n:o[0]]

        XPf = part(XB * 260)
        XP = XPf.rearrange("p (b n) -> p b n", b=XB)
        CU = XPf[:, 0:CBLK * TOK].rearrange("p (b n) -> p b n", b=CBLK)
        CB = XPf[:, CBLK * TOK:2 * CBLK * TOK].rearrange("p (b n) -> p b n", b=CBLK)
        XC = part(XB * TOK).rearrange("p (b n) -> p b n", b=XB)
        SZ = part(CBLK * TOK).rearrange("p (b n) -> p b n", b=CBLK)
        CC = part(CBLK * 258).rearrange("p (b n) -> p b n", b=CBLK)
        DTX = part(TT * DS).rearrange("p (t n) -> p t n", t=TT)
        prm = DTX[0:R_END, 0, 0:P]
        Ef = part(3 * NH * P)
        E = Ef.rearrange("p (h v n) -> p v h n", v=3, h=NH)
        YC = part(KD * TOK).rearrange("p (b n) -> p b n", b=KD)
        CBT = part(3 * NG * P).rearrange("p (v g n) -> p v g n", v=3, g=NG)
        XN = YC.rearrange("p b n -> p (b n)").rearrange("p (t n) -> p t n", t=TT)
        T1 = Ef[:, 0:2 * D].rearrange("p (t n) -> p t n", t=TT)
        SQ = Ef[:, 0:CBLK * TOK].rearrange("p (b n) -> p b n", b=CBLK)
        RSB = Ef[:, CBLK * TOK:CBLK * TOK + 2 * TOK].rearrange("p (b n) -> p b n", b=2)
        DTROW = Ef[0:NH, 0:TOK]
        AB = MOD[:, 0:TT * NH * P].rearrange("p (t h n) -> p t h n", t=TT, h=NH)
        brow = ring[0:1, 3, 0:6 * D]
        o[0] = 0
        HG = part(2 * D).rearrange("p (b n) -> p b n", b=2)
        XT_at = arena_at + 4 * o[0]
        part(2 * D)
        YS = part(2 * D).rearrange("p (b n) -> p b n", b=2)
        HID = part(2 * FE).rearrange("p (b n) -> p b n", b=2)
        HTT = part(FE).rearrange("p (c n) -> p c n", c=FT)
        SG = part(2 * FE).rearrange("p (b n) -> p b n", b=2)
        HT_at = arena_at + 4 * o[0]
        o[0] = H2P_AT = 9256
        H2P = part(2 * D).rearrange("p (t n) -> p t n", t=TT)
        SH_at = arena_at + 4 * o[0]
        SH = part(2 * D).rearrange("p (t n) -> p t n", t=TT)
        XTH = nc.alloc_sbuf_tensor_at("XTH", [P, KD, P], F32R, offset=XT_at)
        XTL = nc.alloc_sbuf_tensor_at("XTL", [P, KD, P], F32R, offset=XT_at + 4 * D)
        WHI, WLO = [], []
        for (k0, k1), at in zip(SPLITS, (MOD_at + 4 * 2 * D, arena_at + 4 * H2P_AT, gffn_at, hT_at)):
            shape = [P, k1 - k0, 2, FE]
            WHI.append(nc.alloc_sbuf_tensor_at(f"WHI{k0}", shape, F32R, offset=at))
            WLO.append(nc.alloc_sbuf_tensor_at(f"WLO{k0}", shape, F32R, offset=at + 4 * (k1 - k0) * 2 * FE))
        HTH = nc.alloc_sbuf_tensor_at("HTH", [P, FT, P], F32R, offset=HT_at)
        HTL = nc.alloc_sbuf_tensor_at("HTL", [P, FT, P], F32R, offset=HT_at + 4 * FE)
        DHI = nc.alloc_sbuf_tensor_at("DHI", [P, FT, 512], F32R, offset=SH_at)
        ringr = nc.alloc_sbuf_tensor_at("ring_low", [P, NSLOT, SLOTW], F32R, offset=ring_at)
        o2 = [0]

        def mpart(n):
            o2[0] += n
            return MOD[:, o2[0] - n:o2[0]]

        W64 = TT * NE
        score = mpart(W64).rearrange("p (t e) -> p t e", t=TT)
        sel = mpart(W64).rearrange("p (t e) -> p t e", t=TT)
        msel = mpart(W64).rearrange("p (t e) -> p t e", t=TT)
        maskf = mpart(W64).rearrange("p (t e) -> p t e", t=TT)
        gates = mpart(W64).rearrange("p (t e) -> p t e", t=TT)
        top8 = mpart(TT * NGR * 8).rearrange("p (t g j) -> p t g j", t=TT, g=NGR)
        gs = mpart(TT * NGR).rearrange("p (t g) -> p t g", t=TT)
        grank = mpart(TT * NGR).rearrange("p (t g) -> p t g", t=TT)
        gpair = mpart(TT * NGR * NGR).rearrange("p (t g j) -> p t g j", t=TT, g=NGR)
        gpair2 = mpart(TT * NGR * NGR).rearrange("p (t g j) -> p t g j", t=TT, g=NGR)
        m8 = mpart(TT * 8).rearrange("p (t j) -> p t j", t=TT)
        maskb = mpart(W64 // 2).bitcast(BF16).rearrange("p (t e) -> p t e", t=TT)
        rcur = sb("rcur", [P, TT, GRP])
        onehot = mpart(TT * GRP * P // 2).bitcast(BF16).rearrange("p (t e n) -> p t e n", t=TT, e=GRP)
        rtcur = sb("rtcur", [P, TT, GRP, NCOL], BF16)
        dec = sb("dec", [P, 2, GRP])

        loaded = [sem(f"loaded{s}") for s in range(NSLOT)]
        gu_loaded = [sem(f"gu_loaded{s}") for s in range(NSLOT)]
        down_loaded = [sem(f"down_loaded{s}") for s in range(NSLOT)]
        x_in = sem("x_in")
        ada_half = [sem(f"ada{j}_half") for j in range(2)]
        ada2_first = sem("ada2_first")
        ada2_used = sem("ada2_used")
        in3_late = sem("in3_late")
        small_issued = sem("small_issued")
        bada_in = sem("bada_in")
        bias_in_mod = sem("bias_in_mod")
        ccol_in = sem("ccol_in")
        small_in = sem("small_in")
        params_in = sem("params_in")
        gains_in = sem("gains_in")
        mod_zero = sem("mod_zero")
        consts = sem("consts")
        ss_ready = sem("ss_ready")
        ms_ready = sem("ms_ready")
        std_ready = sem("std_ready")
        rstd_ready = sem("rstd_ready")
        xn_ready = sem("xn_ready")
        xnT_ps = sem("xnT_ps")
        xnT_ready = sem("xnT_ready")
        prm_ps = sem("prm_ps")
        col_ready = sem("col_ready")
        ada_acc = sem("ada_acc")
        modcol_ps = sem("modcol_ps")
        modrow_ps = sem("modrow_ps")
        modrow_ready = sem("modrow_ready")
        h1_ready = sem("h1_ready")
        dtrow_ps = sem("dtrow_ps")
        dtrow_ready = sem("dtrow_ready")
        dt_ps = sem("dt_ps")
        exp_in = sem("exp_in")
        exp_out = sem("exp_out")
        a_ready = sem("a_ready")
        cs_ps = sem("cs_ps")
        cs_ready = sem("cs_ready")
        csrow_ps = sem("csrow_ps")
        csrow_used = sem("csrow_used")
        decay_in = sem("decay_in")
        decay_ready = sem("decay_ready")
        proj_mm = sem("proj_mm")
        proj_evac = sem("proj_evac")
        conv_ready = sem("conv_ready")
        xbc_ready = sem("xbc_ready")
        xsT_ps = sem("xsT_ps")
        dtx_ready = sem("dtx_ready")
        cb_ps = sem("cb_ps")
        cb_used = sem("cb_used")
        wts_ready = sem("wts_ready")
        y_ps = sem("y_ps")
        y_used = sem("y_used")
        sq_ready = sem("sq_ready")
        yss_ps = sem("yss_ps")
        yms_ready = sem("yms_ready")
        ystd_ready = sem("ystd_ready")
        yb_ready = sem("yb_ready")
        ya_ready = sem("ya_ready")
        mix_ps = sem("mix_ps")
        x2_ready = sem("x2_ready")
        h2_ready = sem("h2_ready")
        h2_stored = sem("h2_stored")
        h2T_ps = sem("h2T_ps")
        h2T_ready = sem("h2T_ready")
        logit_ps = sem("logit_ps")
        score_ready = sem("score_ready")
        mask_ready = sem("mask_ready")
        rank_ps = sem("rank_ps")
        table_ready = sem("table_ready")
        sgu_ps = sem("sgu_ps")
        ssg_ready = sem("ssg_ready")
        shid_ready = sem("shid_ready")
        shT_ps = sem("shT_ps")
        shT_ready = sem("shT_ready")
        sy_ps = sem("sy_ps")
        sh_ready = sem("sh_ready")
        cur_copied = sem("cur_copied")
        onehot_ready = sem("onehot_ready")
        slot_ps = sem("slot_ps")
        dec_step = sem("dec_step")
        slot_ready = sem("slot_ready")
        gi_ready = sem("gi_ready")
        si_ready = sem("si_ready")
        gathered = [sem(f"gathered{b}") for b in range(2)]
        xT_ps = sem("xT_ps")
        xT_ready = sem("xT_ready")
        xhi_ready = sem("xhi_ready")
        whi_ready = sem("whi_ready")
        wlo_ready = sem("wlo_ready")
        split_used = sem("split_used")
        sg_ready = sem("sg_ready")
        hid_ready = sem("hid_ready")
        hidT_ps = sem("hidT_ps")
        hidT_ready = sem("hidT_ready")
        hidT_high = sem("hidT_high")
        hidT_low = sem("hidT_low")
        dhi_ready = sem("dhi_ready")
        dlo_ready = sem("dlo_ready")
        expert_done = sem("expert_done")
        y_ready = sem("y_ready")
        scattered = [sem(f"scattered{b}") for b in range(2)]
        sums_set = sem("sums_set")
        spare_set = sem("spare_set")
        moe_done = sem("moe_done")
        y_loaded = [sem(f"y_loaded{t}") for t in range(TT)]
        fin_ss = sem("fin_ss")
        fin_ms = sem("fin_ms")
        fin_std = sem("fin_std")
        out_ready = sem("out_ready")
        stored = sem("stored")
        act_step = sem("act_step")
        dve_step = sem("dve_step")
        pool_step = sem("pool_step")

        block = ctx.enter_context(nc.Block())

        def bank(b):
            return PS[:, b, :]

        def ada_w(n):
            return ring[:, slot_of(n), 0:KD * PIECE].rearrange("p (k n) -> p k n", k=KD)

        def load_no(what, j):
            return [load[:2] for load in LOADS].index((what, j))

        def gu_w(s):
            return ring[:, s, 0:GU].rearrange("p (a k n) -> p a k n", a=2, k=KD)

        def down_w(s):
            return ring[:, s, GU:GU + FT * D].rearrange("p (c n) -> p c n", c=FT)

        def down_half(tensor, s):
            return tensor[:, s, GU:GU + FT * D].rearrange("p (c n) -> p c n", c=FT)[:, :, 512:1024]

        def e_slot(u):
            return (FIRST_SLOT + u) % NSLOT

        def number(pas, i, u):
            return i * GRP + (NE * pas + u)

        def gu_count(n, u):
            return (n - u % GRP) * (32 // GRP) + 32

        def down_count(n, u):
            return (n - u % GRP) * (16 // GRP) + 16

        @block.sync
        def _(sp):
            def load_gate_up(s, wg, wu, done):
                sp.dma_start(ring[:, s, 0:GU // 2], wg.rearrange("(p k) n -> p (k n)", p=P)).then_inc(done, 16)
                sp.dma_start(ring[:, s, GU // 2:GU], wu.rearrange("(p k) n -> p (k n)", p=P)).then_inc(done, 16)

            def load_down(s, wd, done):
                sp.dma_start(ring[:, s, GU:GU + FT * D], wd.rearrange("(p c) n -> p (c n)", p=P)).then_inc(done, 16)

            sp.dma_start(ccol[:], c[0].rearrange("(p k) -> p k", p=P)).then_inc(ccol_in, 16)
            sp.dma_start(brow, b_ada[0:1, :]).then_inc(bada_in, 16)
            user = {3: (bias_in_mod, 2)}
            nada = nin = 0
            for n, (what, j, s) in enumerate(LOADS):
                if s in user:
                    sp.wait_ge(*user[s])
                if what == A:
                    nada += 1
                    user[s] = (ada_acc, nada)
                    src = w_ada[0, :, PIECE * j:PIECE * j + PIECE].rearrange("(p k) n -> p k n", p=P)
                    if j < 2:
                        sp.dma_start(ada_w(n)[:, 0:KD // 2, :], src[:, 0:KD // 2, :]).then_inc(ada_half[j], 16)
                        sp.dma_start(ada_w(n)[:, KD // 2:KD, :], src[:, KD // 2:KD, :]).then_inc(loaded[s], 16)
                    elif j == 2:
                        sp.dma_start(ada_w(n)[:, :, 0:FIRST], src[:, :, 0:FIRST]).then_inc(ada2_first, 16)
                    else:
                        sp.dma_start(ada_w(n), src).then_inc(loaded[s], 16)
                    if j == 0:
                        sp.dma_start(X[:], x[0].rearrange("(t p) d -> p t d", p=P)).then_inc(x_in, 16)
                        sp.wait_ge(small_issued, 1)
                elif what == I:
                    nin += 1
                    user[s] = (proj_mm, 6 * nin)
                    w = LASTP if j == 3 else PIECE
                    dst = ring[:, s, 0:KD * w].rearrange("p (k n) -> p k n", k=KD)
                    src = w_in[0, :, PIECE * j:PIECE * j + w].rearrange("(k p) n -> p k n", p=P)
                    if j == 3:
                        sp.dma_start(dst[:, :, LATE:w], src[:, :, LATE:w]).then_inc(in3_late, 16)
                        n2 = load_no(A, 2)
                        sp.dma_start(ada_w(n2)[:, :, FIRST:PIECE],
                                     w_ada[0, :, PIECE * 2 + FIRST:PIECE * 3].rearrange("(p k) n -> p k n", p=P)
                                     ).then_inc(loaded[slot_of(n2)], 16)
                        sp.dma_start(dst[:, :, 0:LATE], src[:, :, 0:LATE]).then_inc(loaded[s], 16)
                    else:
                        sp.dma_start(dst, src).then_inc(loaded[s], 16)
                elif what == O:
                    user[s] = (mix_ps, 2 * TT)
                    k0, k1 = OUT_K[j]
                    sp.dma_start(ring[:, s, 0:(k1 - k0) * D].rearrange("p (k n) -> p k n", n=D),
                                 w_out[0, k0 * P:k1 * P, :].rearrange("(k p) n -> p k n", p=P)
                                 ).then_inc(loaded[s], 16)
                else:
                    user[s] = (sy_ps, TT)
                    load_gate_up(s, ws_gate[0], ws_up[0], loaded[s])
                    load_down(s, ws_down[0], loaded[s])
            for u in range(GRP):
                sp.wait_ge(*user[e_slot(u)])
                if u == 2:
                    sp.wait_ge(h2_ready, TT)
                if u == 3:
                    sp.wait_ge(gathered[1], 16)
                load_gate_up(e_slot(u), we_gate[0, u], we_up[0, u], gu_loaded[e_slot(u)])
                load_down(e_slot(u), we_down[0, u], down_loaded[e_slot(u)])

            def expert_gate_up(pas, i, u):
                sp.wait_ge(wlo_ready, number(pas, i, u) * NSP - (NSLOT - 1) * NSP)
                e, s = i * GRP + u, e_slot(u % GRP)
                load_gate_up(s, we_gate[0, e], we_up[0, e], gu_loaded[s])

            def expert_down(pas, i, u):
                sp.wait_ge(expert_done, number(pas, i, u) - (NSLOT - 1))
                load_down(e_slot(u), we_down[0, i * GRP + u], down_loaded[e_slot(u)])

            def load_groups(pas, first):
                expert_gate_up(pas, first, 0)
                with sp.Fori(first, NGRP - 1) as i:
                    for u in range(GRP):
                        expert_gate_up(pas, i, u + 1)
                        expert_down(pas, i, u)
                for u in range(GRP):
                    if u < GRP - 1:
                        expert_gate_up(pas, NGRP - 1, u + 1)
                    expert_down(pas, NGRP - 1, u)

            load_groups(0, 1)
            sp.wait_ge(table_ready, 1)
            over = sp.value_load(oflag[0:1, 0:1], min_val=0, max_val=1)
            with sp.If(over > 0):
                load_groups(1, 0)
            with sp.Else():
                sp.nop()
            sp.wait_ge(moe_done, 1)
            for t in range(TT):
                sp.dma_start(ring[:, t, 0:D], y_dram[t * P:(t + 1) * P, :]).then_inc(y_loaded[t], 16)
            for t in range(TT):
                sp.wait_ge(out_ready, t + 1)
                sp.dma_start(out[0, t * P:(t + 1) * P, :], X[:, t, :]).then_inc(stored, 16)
            sp.wait_ge(stored, 16 * TT)

        @block.gpsimd
        def _(pool):
            count = [0]

            def link(ins):
                count[0] += 1
                ins.then_inc(pool_step, 1)
                pool.wait_ge(pool_step, count[0])

            pool.memset(MOD[:, 2 * D:6 * D], 0.0).then_inc(mod_zero, 1)
            link(pool.memset(ident[:], 0.0))
            link(pool.affine_select(out=ident[:], in_=ident[:], compare_op=ALU.not_equal, fill=1.0, base=0,
                                    pattern=[[-1, P]], channel_multiplier=1))
            link(pool.memset(ones[:], 1.0))
            link(pool.affine_select(out=tri[:], in_=ones[:], compare_op=ALU.is_ge, fill=0.0, base=0,
                                    pattern=[[1, P]], channel_multiplier=-1))
            link(pool.memset(onesb[:], 1.0))
            link(pool.affine_select(out=trib[:], in_=onesb[:], compare_op=ALU.is_ge, fill=0.0, base=-1,
                                    pattern=[[1, P]], channel_multiplier=-1))
            link(pool.memset(lower[:], 1.0))
            link(pool.affine_select(out=lower[:], in_=lower[:], compare_op=ALU.is_ge, fill=0.0, base=-1,
                                    pattern=[[1, NGR], [-1, NGR]], channel_multiplier=0))
            link(pool.iota(slots[:], pattern=[[P, 2], [1, P]], base=0, channel_multiplier=0,
                           allow_small_or_imprecise_dtypes=True))
            link(pool.iota(tokid[:], pattern=[[P, TT]], base=-TOK, channel_multiplier=1,
                           allow_small_or_imprecise_dtypes=True))
            link(pool.memset(spare[:], 0.0))
            link(pool.memset(rankm[:], -1.0))
            link(pool.memset(RT[:], 0.0))
            link(pool.tensor_copy(RT[:, :, 0:NE, 0], tokid[:].unsqueeze(2).to_broadcast([P, TT, NE])))
            link(pool.memset(RT[:, :, 0:NE, 1], 1.0))
            link(pool.iota(minus_slot[:], pattern=[[0, 1]], base=0, channel_multiplier=-1,
                           allow_small_or_imprecise_dtypes=True))
            link(pool.iota(spare_row[:], pattern=[[0, 1]], base=TOK, channel_multiplier=1,
                           allow_small_or_imprecise_dtypes=True))
            link(pool.memset(counts_u[:], 0.0))
            link(pool.memset(XPf, 0.0))
            pool.memset(CC, 0.0).then_inc(consts, 1)

            pool.wait_ge(ya_ready, CBLK)
            link(pool.memset(HG, 0.0))
            pool.dma_start(y_dram[TOK:TOK + P, :], HG[:, 0, :]).then_inc(spare_set, 16)
            pool.wait_ge(spare_set, 16)

            pool.wait_ge(table_ready, 2)
            pool.wait_ge(h2_stored, 16 * TT)

            last_token = pool.to_reg(TOK - 1)
            last_row = pool.to_reg(TOK + P - 1)

            def carry_wait():
                pool.tensor_tensor(spare[:, 1:2], spare[:, 0:1], spare[:, 0:1], ALU.add)

            def sized(pas, e, issue):
                if pas:
                    issue(P)
                    return
                tokens = pool.value_load(counts_u[0:1, bass.ds(e, 1)], min_val=0, max_val=TOK)

                def choose(heights):
                    if len(heights) == 1:
                        issue(heights[0])
                        return
                    low, high = heights[:len(heights) // 2], heights[len(heights) // 2:]
                    with pool.If(tokens > low[-1]):
                        choose(high)
                        pool.nop()
                    with pool.Else():
                        choose(low)
                        pool.nop()

                choose(HEIGHTS)

            def stage_group(pas, g, first):
                n = g + PASS_GROUPS * pas
                if not first:
                    pool.wait_ge(slot_ps, n)
                cols = bass.ds(g * GRP, GRP)
                pool.tensor_copy(rcur[:], rankm[:, :, cols]).then_inc(cur_copied, 1)
                pool.tensor_copy(rtcur[:], RT[:, :, cols, :]).then_inc(cur_copied, 1)

            def gather(pas, i, u, first=False):
                n = number(pas, i, u)
                b = u % 2
                if u % GRP == 0 or first:
                    pool.wait_ge(slot_ready, (i + (PASS_GROUPS * pas + u // GRP + 1)) * 3)
                if not first:
                    pool.wait_ge(xT_ps, n - 1)
                pool.tensor_copy(gi[:, b, :], gidx[:, bass.ds(i * GRP + u, 1)]).then_inc(gi_ready, 1)
                pool.wait_ge(gi_ready, n + 1)
                carry_wait()
                sized(pas, i * GRP + u, lambda rows: pool.indirect_dma_start(
                    out=HG[0:rows, b, :], out_offset=None, in_=h2_dram[:],
                    in_offset=bass.IndirectOffsetOnAxis(ap=gi[0:rows, b, :], axis=0),
                    bounds_check=last_token, oob_is_err=False).then_inc(gathered[b], 16))

            def scatter(pas, i, u):
                n = number(pas, i, u)
                b = u % 2
                pool.wait_ge(y_ready, n * 2 + 2)
                pool.tensor_copy(si[:, b, :], sidx[:, bass.ds(i * GRP + u, 1)]).then_inc(si_ready, 1)
                pool.wait_ge(si_ready, n + 1)
                carry_wait()
                sized(pas, i * GRP + u, lambda rows: pool.indirect_dma_start(
                    out=y_dram[:], out_offset=bass.IndirectOffsetOnAxis(ap=si[0:rows, b, :], axis=0),
                    in_=YS[0:rows, b, :], in_offset=None, bounds_check=last_row,
                    compute_op=ALU.add).then_inc(scattered[b], 16))

            def split_down_lo(pas, i, u):
                n = number(pas, i, u)
                s = e_slot(u)
                pool.wait_ge(dhi_ready, n + 1)
                pool.tensor_tensor(down_half(ringr, s), down_half(ring, s), DHI[:].bitcast(F32),
                                   ALU.subtract).then_inc(dlo_ready, 1)

            def group(pas, i, last=False):
                for u in range(GRP):
                    split_down_lo(pas, i, u)
                    if not (last and u + 3 >= GRP):
                        gather(pas, i, u + 3)
                    if u == 1 and not last:
                        stage_group(pas, i + AHEAD, False)
                    if u:
                        pool.wait_ge(scattered[(u - 1) % 2], (i * 2 + (32 * pas + (u + 1) // 2)) * 16)
                    elif pas == 0 and isinstance(i, int) and i == 0:
                        pool.wait_ge(sums_set, 16 * TT)
                    else:
                        pool.wait_ge(scattered[1], (i * 2 + 32 * pas) * 16)
                    scatter(pas, i, u)

            def run_pass(pas):
                stage_group(pas, 0, pas == 0)
                stage_group(pas, 1, False)
                for u in range(2):
                    gather(pas, 0, u, first=True)
                gather(pas, 0, 2)
                group(pas, 0)
                with pool.Fori(1, NGRP - 1) as i:
                    group(pas, i)
                group(pas, NGRP - 1, last=True)
                for b in range(2):
                    pool.wait_ge(scattered[b], 16 * 32 * (pas + 1))

            run_pass(0)
            over = pool.value_load(oflag[0:1, 0:1], min_val=0, max_val=1)
            with pool.If(over > 0):
                run_pass(1)
            with pool.Else():
                pool.nop()
            pool.memset(rcur[:], 0.0).then_inc(moe_done, 1)

        @block.scalar
        def _(act):
            count = [0]

            def link(ins):
                count[0] += 1
                ins.then_inc(act_step, 1)
                act.wait_ge(act_step, count[0])

            act.dma_start(prm[R_CA:R_CS, :], conv_a_w[0].rearrange("k (b q) -> (k b) q", q=P)).then_inc(params_in, 16)
            act.dma_start(prm[R_CS:R_CB, :], ssm_conv_w[0].rearrange("k (b q) -> (k b) q", q=P)).then_inc(params_in, 16)
            act.dma_start(prm[R_CB:R_NG, :], ssm_conv_b[0].rearrange("(b q) -> b q", q=P)).then_inc(params_in, 16)
            act.dma_start(prm[R_NG:R_NM, :], ssm_norm_g[0].rearrange("(b q) -> b q", q=P)).then_inc(params_in, 16)
            act.dma_start(prm[R_NM:R_END, :], norm_mix_g[0].rearrange("(b q) -> b q", q=P)).then_inc(params_in, 16)
            act.dma_start(hrow[:, 0, :], ssm_dt_bias[0].partition_broadcast(P)).then_inc(small_in, 16)
            act.dma_start(hrow[:, 1, :], ssm_a_log[0].partition_broadcast(P)).then_inc(small_in, 16)
            for half in range(2):
                act.dma_start(dskip[HD * half:HD * half + HD, :],
                              ssm_d[0].rearrange("(b q) -> q b", q=2)[half].partition_broadcast(HD),
                              allow_slow_non_contiguous=True).then_inc(small_in, 16)
            act.dma_start(rbias[:], router_bias[0].partition_broadcast(P)).then_inc(small_in, 16)
            act.nop().then_inc(small_issued, 1)
            act.wait_ge(bada_in, 16)
            act.wait_ge(mod_zero, 2)
            act.copy(MOD[0:1, 0:2 * D], brow[:, 0:2 * D]).then_inc(bias_in_mod, 1)
            act.copy(MOD[0:1, 2 * D:6 * D], brow[:, 2 * D:6 * D]).then_inc(bias_in_mod, 1)

            act.wait_ge(x_in, 16)
            for t in range(TT):
                act.activation(XN[:, t, :], X[:, t, :], ACT.Square, accum_out=small[:, t:t + 1]).then_inc(ss_ready, 1)
            act.wait_ge(ms_ready, 1)
            act.activation(small[:, 4:6], small[:, 2:4], ACT.Sqrt).then_inc(std_ready, 1)
            act.wait_ge(rstd_ready, 1)
            act.wait_ge(ss_ready, TT)
            for t in range(TT):
                act.activation(XN[:, t, :], X[:, t, :], ACT.Copy, scale=small[:, 6 + t:7 + t]).then_inc(xn_ready, 1)
            act.wait_ge(prm_ps, 1)
            act.copy(COL[:], PS[:, 7, 0:R_END]).then_inc(col_ready, 1)
            act.wait_ge(xnT_ps, 1)
            for b in range(4):
                act.copy(hT[:, 2 * b:2 * b + 2, :].rearrange("p k n -> p (k n)"), bank(2 + b)).then_inc(xnT_ready, 1)
            act.dma_start(WR[:], w_router[0].rearrange("(p k) n -> p k n", p=P)).then_inc(gains_in, 16)
            act.dma_start(gffn[:], norm_ffn_g[0].partition_broadcast(P)).then_inc(gains_in, 16)
            act.dma_start(gfin[:], norm_final_g.partition_broadcast(P)).then_inc(gains_in, 16)

            def exp_step(n, dst, src):
                act.wait_ge(exp_in, n)
                act.activation(dst, src, ACT.Exp).then_inc(exp_out, 1)

            act.wait_ge(small_in, 16 * 5)
            act.activation(dtv[:, 8, 0:NH], hrow[:, 1, :], ACT.Exp).then_inc(exp_out, 1)
            act.wait_ge(dtrow_ps, 1)
            act.copy(DTROW, PS[0:NH, 7, 128:128 + TOK]).then_inc(dtrow_ready, 1)
            exp_step(1, dtv[:, 2, :], dtv[:, 1, :])

            nconv = [0]

            def silu_conv(b):
                nconv[0] += 1
                act.wait_ge(conv_ready, nconv[0])
                act.activation(XC[:, b, :], XC[:, b, :], ACT.Silu,
                               bias=COL[:, R_CB + b:R_CB + b + 1]).then_inc(xbc_ready, 1)

            act.wait_ge(consts, 1)
            for q, m in enumerate(ORDER):
                if m < 4 or (8 <= m < 12):
                    act.wait_ge(conv_ready, XB)
                act.wait_ge(proj_mm, q + 1)
                src = PS[:, 2 + q % QB, 0:TOK]
                if m >= 16:
                    act.copy(XP[:, m - 16, SK - 1:SK - 1 + TOK], src).then_inc(proj_evac, 1)
                elif m >= 12:
                    act.activation(SZ[:, m - 12, :], src, ACT.Silu).then_inc(proj_evac, 1)
                elif m >= 8:
                    act.copy(CU[:, m - 8, :], src).then_inc(proj_evac, 1)
                elif m >= 4:
                    act.copy(CC[:, m - 4, CK - 1:CK - 1 + TOK], src).then_inc(proj_evac, 1)
                else:
                    act.copy(CB[:, m, :], src).then_inc(proj_evac, 1)
                if q == 11:
                    for b in CONVS:
                        silu_conv(b)
                if q in (16, 17):
                    for n, v in ([(1, 0)] if q == 16 else [(2, 2), (3, 1)]):
                        act.wait_ge(decay_in, n)
                        act.activation(E[:, v, :, :], E[:, v, :, :], ACT.Exp).then_inc(decay_ready, 1)
                if q == 22:
                    act.wait_ge(yms_ready, 1)
                    act.activation(RSB[:, 0, :], RSB[:, 0, :], ACT.Sqrt).then_inc(ystd_ready, 1)

            def copy_mod_rows(rows):
                for r in rows:
                    act.wait_ge(modrow_ps, r + 1)
                    act.copy(MOD[:, 2 * D + 512 * r:2 * D + 512 * r + 512],
                             bank(r % 2 if r < 6 else 2 + r % 2)).then_inc(modrow_ready, 1)

            copy_mod_rows(range(6))
            for t in range(TT):
                act.wait_ge(x2_ready, 2 * t + 2)
                act.activation(T1[:, t, :], X[:, t, :], ACT.Square,
                               accum_out=small[:, t:t + 1]).then_inc(ss_ready, 1)
                act.wait_ge(ms_ready, t + 2)
                act.activation(small[:, 4 + t:5 + t], small[:, 2 + t:3 + t], ACT.Sqrt).then_inc(std_ready, 1)
                act.wait_ge(h2_ready, t + 1)
                act.dma_start(h2_dram[t * P:(t + 1) * P, :], H2P[:, t, :]).then_inc(h2_stored, 16)
                act.wait_ge(h2T_ps, t + 1)
                act.copy(hT[:, 0:4, t * P:(t + 1) * P], PS[:, 2 + 2 * t, :].rearrange("p (k n) -> p k n", k=4))
                act.copy(hT[:, 4:8, t * P:(t + 1) * P],
                         PS[:, 3 + 2 * t, :].rearrange("p (k n) -> p k n", k=4)).then_inc(h2T_ready, 1)

            def shared_silu(t):
                act.wait_ge(sgu_ps, t + 1)
                act.activation(SG[:, t, :], PS[:, t, 0:FE], ACT.Silu).then_inc(ssg_ready, 1)

            def split_hi(n, u, g):
                k0, k1 = SPLITS[g]
                s = e_slot(u % GRP)
                if g == 0:
                    act.wait_ge(gu_loaded[s], gu_count(n, u))
                if not (isinstance(n, int) and n == 0):
                    act.wait_ge(split_used, n * NSP + (g + 1 - NSP))
                act.copy(WHI[g][:], gu_w(s)[:, :, k0:k1, :].rearrange("p a k n -> p k a n")).then_inc(whi_ready, 1)

            split_hi(0, 0, 0)
            shared_silu(0)
            copy_mod_rows(range(6, 8))
            act.wait_ge(logit_ps, TT)
            act.activation(score, PS[:, 7, 0:TT * NE].rearrange("p (t e) -> p t e", t=TT),
                           ACT.Sigmoid).then_inc(score_ready, 1)
            def copy_xT(n):
                act.wait_ge(xT_ps, n + 1)
                act.copy(XTH[:, 0:4, :].rearrange("p k n -> p (k n)"), bank(0)).then_inc(xhi_ready, 1)

            def silu_gate(n, u):
                act.wait_ge(split_used, n * NSP + NSP)
                act.activation(SG[:, u % 2, :], PS[:, 2 + u % 2, 0:FE], ACT.Silu).then_inc(sg_ready, 1)

            def group(pas, i, last=False):
                for u in range(GRP):
                    n = number(pas, i, u)
                    if not (last and u >= 2):
                        for g in range(EARLY):
                            split_hi(n + 2, u + 2, g)
                    if not (last and u == 3):
                        act.wait_ge(hid_ready, n)
                        silu_gate(n + 1, u + 1)
                    act.wait_ge(hidT_ps, n + 1)
                    act.copy(HTT.rearrange("p c n -> p (c n)"), PS[:, 6, 0:FE]).then_inc(hidT_ready, 1)
                    act.copy(HTH[:].rearrange("p c n -> p (c n)"), PS[:, 6, 0:FE]).then_inc(hidT_high, 1)
                    if not (last and u >= 2):
                        copy_xT(n + 2)
                        for g in range(EARLY, NSP):
                            split_hi(n + 2, u + 2, g)
                    act.wait_ge(expert_done, n + 1)
                    if u >= 2:
                        act.wait_ge(scattered[u % 2], (i * 2 + (32 * pas + 1)) * 16)
                    elif not (isinstance(i, int) and i == 0 and pas == 0):
                        act.wait_ge(scattered[u % 2], (i * 2 + 32 * pas) * 16)
                    act.copy(YS[:, u % 2, 0:512], bank(4)).then_inc(y_ready, 1)
                    if not (last and u == 3):
                        split_down_hi(n + 1, u + 1)

            def split_down_hi(n, u):
                s = e_slot(u % GRP)
                act.wait_ge(down_loaded[s], down_count(n, u))
                act.copy(DHI[:], down_half(ring, s)).then_inc(dhi_ready, 1)

            def shared_hT(t):
                act.wait_ge(shT_ps, t + 1)
                if t:
                    act.wait_ge(sy_ps, t)
                act.copy(HTT.rearrange("p c n -> p (c n)"), PS[:, 6, 0:FE]).then_inc(shT_ready, 1)

            def shared_out(t):
                act.wait_ge(sy_ps, t + 1)
                act.copy(SH[:, t, :].rearrange("p (a n) -> p a n", a=2), PS[:, 4:6, :]).then_inc(sh_ready, 1)
                act.wait_ge(sh_ready, t + 1)
                act.dma_start(y_dram[t * P:(t + 1) * P, :], SH[:, t, :]).then_inc(sums_set, 16)

            def run_pass(pas):
                n = NE * pas
                if pas == 0:
                    shared_hT(0)
                    act.wait_ge(h2_stored, 16 * TT)
                    split_hi(n, 0, 1)
                    split_hi(n, 0, 2)
                    shared_silu(1)
                    shared_hT(1)
                    shared_out(0)
                    split_hi(n, 0, 3)
                    shared_out(1)
                    act.wait_ge(sums_set, 16 * TT)
                else:
                    for g in range(NSP):
                        split_hi(n, 0, g)
                copy_xT(n)
                for g in range(EARLY):
                    split_hi(n + 1, 1, g)
                silu_gate(n, 0)
                split_down_hi(n, 0)
                copy_xT(n + 1)
                for g in range(EARLY, NSP):
                    split_hi(n + 1, 1, g)
                group(pas, 0)
                with act.Fori(1, NGRP - 1) as i:
                    group(pas, i)
                group(pas, NGRP - 1, last=True)

            run_pass(0)
            over = act.value_load(oflag[0:1, 0:1], min_val=0, max_val=1)
            with act.If(over > 0):
                run_pass(1)
            with act.Else():
                act.nop()
            for t in range(TT):
                act.wait_ge(fin_ss, t + 1)
                act.activation(SH[:, t, :], X[:, t, :], ACT.Square, accum_out=small[:, t:t + 1]).then_inc(ss_ready, 1)
                act.wait_ge(fin_ms, t + 1)
                act.activation(small[:, 4 + t:5 + t], small[:, 2 + t:3 + t], ACT.Sqrt).then_inc(fin_std, 1)

        @block.vector
        def _(dve):
            counts = {}

            def signal(ins, s):
                ins.then_inc(s, 1)
                counts[id(s)] = counts.get(id(s), 0) + 1
                return counts[id(s)]

            def link(ins, s=None):
                s = dve_step if s is None else s
                dve.wait_ge(s, signal(ins, s))

            dve.memset(MOD[:, 0:2 * D], 0.0).then_inc(mod_zero, 1)
            def ada(j, first_columns=False):
                n = load_no(A, j)
                w = ada_w(n)
                c0, c1 = 0, PIECE
                if j < 2:
                    dve.wait_ge(ada_half[j], 16)
                elif first_columns:
                    dve.wait_ge(ada2_first, 16)
                    c1 = FIRST
                else:
                    dve.wait_ge(loaded[slot_of(n)], loaded_count(n))
                    if j == 2:
                        c0 = FIRST
                dst = MOD[:, PIECE * j + c0:PIECE * j + c1]
                for k in range(KD):
                    if j < 2 and k == KD // 2:
                        dve.wait_ge(loaded[slot_of(n)], loaded_count(n))
                    ins = dve.scalar_tensor_tensor(out=dst, in0=w[:, k, c0:c1], scalar=ccol[:, k:k + 1], in1=dst,
                                                   op0=ALU.mult, op1=ALU.add)
                    done = ada2_used if first_columns else ada_acc
                    link(ins, done if k == KD - 1 else None)

            dve.wait_ge(ccol_in, 16)
            dve.wait_ge(bias_in_mod, 1)
            ada(0)
            dve.wait_ge(ss_ready, TT)
            link(dve.tensor_scalar(small[:, 2:4], small[:, 0:2], 1.0 / D, EPS, ALU.mult, ALU.add), ms_ready)
            dve.wait_ge(std_ready, 1)
            link(dve.reciprocal(small[:, 6:8], small[:, 4:6]), rstd_ready)
            dve.wait_ge(small_in, 16 * 5)
            ada(1)
            ada(2, first_columns=True)
            dve.wait_ge(modcol_ps, 1)
            dve.wait_ge(col_ready, 1)
            link(dve.scalar_tensor_tensor(out=AB1[:, 0:KD], in0=PS[:, 0, KD:2 * KD], scalar=1.0,
                                          in1=COL[:, R_NM:R_END], op0=ALU.add, op1=ALU.mult))
            link(dve.tensor_copy(AB1[:, KD:2 * KD], PS[:, 0, 0:KD]))
            dve.wait_ge(xnT_ready, 4)
            for k in range(KD):
                signal(dve.tensor_scalar(hT[:, k, :], hT[:, k, :], AB1[:, k:k + 1], AB1[:, KD + k:KD + k + 1],
                                         ALU.mult, ALU.add), h1_ready)

            s_, n_, u_, w_, z_, z2_, p_, dt_, a_ = (dtv[:, i, :] for i in (0, 1, 2, 3, 4, 5, 6, 7, 9))
            dve.wait_ge(dt_ps, 1)
            link(dve.tensor_tensor(s_.rearrange("p (t h) -> p t h", t=TT),
                                   PS[:, 7, 0:TT * NH].rearrange("p (t h) -> p t h", t=TT),
                                   hrow[:, 0, :].unsqueeze(1).to_broadcast([P, TT, NH]), ALU.add))
            link(dve.tensor_scalar(n_, s_, -1.0, None, ALU.mult))
            link(dve.tensor_tensor(n_, n_, s_, ALU.min), exp_in)
            link(dve.tensor_scalar(s_, s_, 0.0, None, ALU.max))
            dve.wait_ge(exp_out, 2)
            link(dve.tensor_scalar(w_, u_, 2.0, None, ALU.add))
            link(dve.reciprocal(w_, w_))
            link(dve.tensor_tensor(z_, u_, w_, ALU.mult))
            link(dve.tensor_tensor(z2_, z_, z_, ALU.mult))
            link(dve.tensor_scalar(p_, z2_, 1.0 / 17, None, ALU.mult))
            for c_ in (15, 13, 11, 9, 7, 5, 3):
                link(dve.scalar_tensor_tensor(out=p_, in0=p_, scalar=1.0 / c_, in1=z2_, op0=ALU.add, op1=ALU.mult))
            link(dve.scalar_tensor_tensor(out=p_, in0=p_, scalar=1.0, in1=z_, op0=ALU.add, op1=ALU.mult))
            link(dve.scalar_tensor_tensor(out=dt_, in0=p_, scalar=2.0, in1=s_, op0=ALU.mult, op1=ALU.add))
            link(dve.scalar_tensor_tensor(out=a_.rearrange("p (t h) -> p t h", t=TT),
                                          in0=dt_.rearrange("p (t h) -> p t h", t=TT), scalar=-1.0,
                                          in1=dtv[:, 8, 0:NH].unsqueeze(1).to_broadcast([P, TT, NH]),
                                          op0=ALU.mult, op1=ALU.mult))
            dve.wait_ge(consts, 1)
            link(dve.tensor_tensor(AB.rearrange("p t h n -> p (t h) n"), a_.unsqueeze(2).to_broadcast([P, TT * NH, P]),
                                   tri[:].unsqueeze(1).to_broadcast([P, TT * NH, P]), ALU.mult), a_ready)

            evac = {m: q + 1 for q, m in enumerate(ORDER)}

            def conv(b):
                dve.wait_ge(proj_evac, evac[16 + b])
                w = [COL[:, R_CS + k * XB + b:R_CS + k * XB + b + 1] for k in range(SK)]
                link(dve.tensor_scalar(XC[:, b, :], XP[:, b, 0:TOK], w[0], None, ALU.mult))
                for k in range(1, SK):
                    link(dve.scalar_tensor_tensor(out=XC[:, b, :], in0=XP[:, b, k:k + TOK], scalar=w[k],
                                                  in1=XC[:, b, :], op0=ALU.mult, op1=ALU.add),
                         conv_ready if k == SK - 1 else None)

            dve.wait_ge(bias_in_mod, 2)
            ada(2)
            ada(3)
            for b in CONVS[0:3]:
                conv(b)
            ada(4)
            for b in CONVS[3:6]:
                conv(b)
            dve.wait_ge(cs_ps, 1)
            link(dve.tensor_copy(csv[:, 0:3 * NH], PS[:, 7, 32:32 + 3 * NH]))
            link(dve.tensor_tensor(csv[:, 3 * NH:4 * NH], csv[:, 2 * NH:3 * NH], csv[:, 0:NH], ALU.subtract), cs_ready)
            for b in CONVS[6:8]:
                conv(b)
            ada(5)
            dve.wait_ge(xsT_ps, 1)
            for t in range(TT):
                signal(dve.tensor_tensor(DTX[:, t, :].rearrange("p (h n) -> p h n", h=NH),
                                         bank(t).rearrange("p (h n) -> p h n", h=NH),
                                         dt_[:, t * NH:(t + 1) * NH].unsqueeze(2).to_broadcast([P, NH, HD]),
                                         ALU.mult), dtx_ready)
            for t in range(TT):
                dve.wait_ge(csrow_ps, t + 1)
                for v in ([0] if t == 0 else [2, 1]):
                    for h in range(NH):
                        src = PS[:, h // 4, (h % 4) * P:(h % 4) * P + P]
                        if v != 1:
                            ins = dve.tensor_scalar(E[:, v, h, :], src, csv[:, t * NH + h:t * NH + h + 1], 0.0,
                                                    ALU.subtract, ALU.min)
                        else:
                            ins = dve.tensor_scalar(E[:, v, h, :], src, csv[:, 3 * NH + h:3 * NH + h + 1], 0.0,
                                                    ALU.add, ALU.min)
                        if h < NH - 1:
                            continue
                        signal(ins, decay_in)
                dve.wait_ge(decay_in, 1 + 2 * t)
                signal(dve.memset(small[:, 10:11], 0.0), csrow_used)
            dve.wait_ge(cb_ps, 1)
            for g in range(NG):
                for v in range(3):
                    src = PS[:, g, v * P:(v + 1) * P]
                    if v != 1:
                        ins = dve.tensor_tensor(CBT[:, v, g, :], src, tri[:], ALU.mult)
                    else:
                        ins = dve.tensor_copy(CBT[:, v, g, :], src)
                    signal(ins, cb_used)
            dve.wait_ge(cb_used, 3 * NG)
            dve.wait_ge(decay_ready, 3)
            for v in range(3):
                for g in range(NG):
                    e = E[:, v, HPG * g:HPG * g + HPG, :]
                    signal(dve.tensor_tensor(e, e, CBT[:, v, g, :].unsqueeze(1).to_broadcast([P, HPG, P]),
                                             ALU.mult), wts_ready)
            ada(6)
            dve.wait_ge(y_ps, 1)
            for b in range(CBLK):
                src = PS[:, b // 2, (b % 2) * TOK:(b % 2) * TOK + TOK]
                signal(dve.scalar_tensor_tensor(out=YC[:, CBLK + b, :], in0=XC[:, b, :], scalar=dskip[:, b:b + 1],
                                                in1=src, op0=ALU.mult, op1=ALU.add), y_used)
            dve.wait_ge(y_used, CBLK)
            yb = YC[:, CBLK:2 * CBLK, :]
            link(dve.tensor_tensor(yb, yb, SZ, ALU.mult))
            link(dve.tensor_tensor(SQ, yb, yb, ALU.mult), sq_ready)
            dve.wait_ge(yss_ps, 1)
            link(dve.tensor_scalar(RSB[:, 0, :], PS[:, 7, 0:TOK], 1.0 / DS, EPS, ALU.mult, ALU.add), yms_ready)
            dve.wait_ge(ystd_ready, 1)
            link(dve.reciprocal(RSB[:, 1, :], RSB[:, 0, :]))
            for b in range(CBLK):
                signal(dve.scalar_tensor_tensor(out=YC[:, CBLK + b, :], in0=YC[:, CBLK + b, :],
                                                scalar=COL[:, R_NG + b:R_NG + b + 1], in1=RSB[:, 1, :],
                                                op0=ALU.mult, op1=ALU.mult), yb_ready)
            for b in (2, 3, 0, 1):
                dve.wait_ge(proj_evac, max(evac[4 + b], evac[8 + b], evac[b]))
                cc = CC[:, b, CK - 1:CK - 1 + TOK]
                link(dve.tensor_tensor(cc, cc, CU[:, b, :], ALU.mult))
                w = [COL[:, R_CA + k * CBLK + b:R_CA + k * CBLK + b + 1] for k in range(CK)]
                link(dve.tensor_scalar(YC[:, b, :], CC[:, b, 0:TOK], w[0], None, ALU.mult))
                for k in range(1, CK):
                    link(dve.scalar_tensor_tensor(out=YC[:, b, :], in0=CC[:, b, k:k + TOK], scalar=w[k],
                                                  in1=YC[:, b, :], op0=ALU.mult, op1=ALU.add))
                signal(dve.tensor_tensor(YC[:, b, :], YC[:, b, :], CB[:, b, :], ALU.mult), ya_ready)
            ada(7)
            dve.wait_ge(modrow_ready, 2)
            for t in range(TT):
                for h in range(2):
                    r = 2 * t + h
                    cols = slice(512 * h, 512 * h + 512)
                    dve.wait_ge(mix_ps, r + 1)
                    link(dve.tensor_tensor(T1[:, t, cols], bank(2 + r), MOD[:, 2 * D + 512 * h:2 * D + 512 * h + 512],
                                           ALU.mult))
                    link(dve.tensor_tensor(X[:, t, cols], X[:, t, cols], T1[:, t, cols], ALU.add), x2_ready)
                if t == 0:
                    dve.wait_ge(gains_in, 16 * 3)
                    dve.wait_ge(modrow_ready, 6)
                    link(dve.scalar_tensor_tensor(out=MOD[:, 4 * D:5 * D], in0=MOD[:, 4 * D:5 * D], scalar=1.0,
                                                  in1=gffn[:], op0=ALU.add, op1=ALU.mult))
                dve.wait_ge(ss_ready, TT + t + 1)
                link(dve.tensor_scalar(small[:, 2 + t:3 + t], small[:, t:t + 1], 1.0 / D, EPS, ALU.mult, ALU.add),
                     ms_ready)
                dve.wait_ge(std_ready, t + 2)
                link(dve.reciprocal(small[:, 8 + t:9 + t], small[:, 4 + t:5 + t]))
                link(dve.scalar_tensor_tensor(out=T1[:, t, :], in0=X[:, t, :], scalar=small[:, 8 + t:9 + t],
                                              in1=MOD[:, 4 * D:5 * D], op0=ALU.mult, op1=ALU.mult))
                link(dve.tensor_tensor(H2P[:, t, :].rearrange("p (k q) -> p q k", k=KD),
                                       T1[:, t, :].rearrange("p (q k) -> p q k", k=KD),
                                       MOD[:, 3 * D:4 * D].rearrange("p (q k) -> p q k", k=KD), ALU.add), h2_ready)

            def split_lo(n, u, g):
                k0, k1 = SPLITS[g]
                dve.wait_ge(whi_ready, n * NSP + (g + 1))
                dve.tensor_tensor(WLO[g][:], gu_w(e_slot(u % GRP))[:, :, k0:k1, :].rearrange("p a k n -> p k a n"),
                                  WHI[g][:].bitcast(F32), ALU.subtract).then_inc(wlo_ready, 1)

            def shared_hidden(t):
                dve.wait_ge(ssg_ready, t + 1)
                signal(dve.tensor_tensor(HID[:, t, :].rearrange("p (c q) -> p q c", c=FT),
                                         SG[:, t, :].rearrange("p (q c) -> p q c", c=FT),
                                         PS[:, t, FE:2 * FE].rearrange("p (q c) -> p q c", c=FT),
                                         ALU.mult), shid_ready)

            split_lo(0, 0, 0)
            shared_hidden(0)

            dve.wait_ge(score_ready, 1)
            link(dve.tensor_tensor(sel, score, rbias[:].unsqueeze(1).to_broadcast([P, TT, NE]), ALU.add))
            n = 0
            for t in range(TT):
                for g in range(NGR):
                    n = signal(dve.max(top8[:, t, g, :], sel[:, t, 8 * g:8 * g + 8]), dve_step)
            dve.wait_ge(dve_step, n)
            link(dve.tensor_tensor(gs, top8[:, :, :, 0], top8[:, :, :, 1], ALU.add))
            mine = gs.unsqueeze(3).to_broadcast([P, TT, NGR, NGR])
            other = gs.unsqueeze(2).to_broadcast([P, TT, NGR, NGR])
            link(dve.tensor_tensor(gpair, other, mine, ALU.is_equal))
            link(dve.tensor_tensor(gpair, gpair, lower[:].unsqueeze(1).to_broadcast([P, TT, NGR, NGR]), ALU.mult))
            link(dve.tensor_tensor(gpair2, other, mine, ALU.is_gt))
            link(dve.tensor_tensor(gpair, gpair, gpair2, ALU.add))
            link(dve.tensor_reduce(grank, gpair, AX.X, ALU.add))
            link(dve.tensor_scalar(grank, grank, float(TOPG), None, ALU.is_lt))
            gmask = grank.unsqueeze(3).to_broadcast([P, TT, NGR, NE // NGR])
            link(dve.tensor_tensor(msel.rearrange("p t (g j) -> p t g j", g=NGR),
                                   sel.rearrange("p t (g j) -> p t g j", g=NGR), gmask, ALU.mult))
            link(dve.tensor_scalar(gs, grank, 1e30, -1e30, ALU.mult, ALU.add))
            link(dve.tensor_tensor(msel.rearrange("p t (g j) -> p t g j", g=NGR),
                                   msel.rearrange("p t (g j) -> p t g j", g=NGR),
                                   gs.unsqueeze(3).to_broadcast([P, TT, NGR, NE // NGR]), ALU.add))
            for t in range(TT):
                link(dve.max(m8[:, t, :], msel[:, t, :]))
                link(dve.match_replace(out=maskf[:, t, :], in_to_replace=m8[:, t, :], in_values=msel[:, t, :],
                                       imm_value=-3e30))
            link(dve.tensor_scalar(maskf, maskf, -3e30, None, ALU.is_equal))
            link(dve.tensor_copy(maskb, maskf), mask_ready)
            shared_hidden(1)
            link(dve.tensor_tensor(gates, score, maskf, ALU.mult))
            link(dve.tensor_reduce(grank[:, :, 0:1], gates, AX.X, ALU.add))
            link(dve.reciprocal(grank[:, :, 0:1], grank[:, :, 0:1]))
            for t in range(TT):
                link(dve.tensor_scalar(gates[:, t, :], gates[:, t, :], grank[:, t, 0:1], ROUTED_SCALE,
                                       ALU.mult, ALU.mult))
            for part_no in range(3):
                rt = RT[:, :, 0:NE, 2 + part_no]
                link(dve.tensor_copy(rt, gates))
                if part_no < 2:
                    link(dve.tensor_tensor(gates, gates, rt, ALU.subtract))
            dve.wait_ge(rank_ps, 1)
            link(dve.tensor_scalar(rankm[:, :, 0:NE], PS[:, 7, 0:W64].rearrange("p (t e) -> p t e", t=TT), 1.0, None,
                                   ALU.add))
            link(dve.tensor_tensor(rankm[:, :, 0:NE], rankm[:, :, 0:NE], maskf, ALU.mult))
            link(dve.tensor_scalar(rankm[:, :, 0:NE], rankm[:, :, 0:NE], -1.0, None, ALU.add))
            link(dve.tensor_copy(counts_u[:, 0:NE], PS[:, 7, W64:W64 + NE]))
            link(dve.tensor_reduce(small[:, 12:13], PS[:, 7, W64:W64 + NE], AX.X, ALU.max))
            link(dve.tensor_scalar(oflag[:], small[:, 12:13], P + 0.5, None, ALU.is_gt), table_ready)
            signal(dve.memset(small[:, 13:14], 0.0), table_ready)

            def decode(pas, g):
                n = g + PASS_GROUPS * pas
                cols = bass.ds(g * GRP, GRP)
                dve.wait_ge(slot_ps, n + 1)
                ps = PS[:, 7, 0:GRP * NCOL].rearrange("p (e c) -> p e c", e=GRP)
                dve.tensor_copy(dec[:, 0, :], ps[:, :, 1]).then_inc(dec_step, 1)
                dve.tensor_scalar(gidx[:, cols], ps[:, :, 0], float(TOK), None, ALU.add).then_inc(slot_ready, 1)
                dve.wait_ge(dec_step, n * 2 + 1)
                dve.scalar_tensor_tensor(out=dec[:, 1, :], in0=dec[:, 0, :], scalar=minus_slot[:, 0:1], in1=ps[:, :, 0],
                                         op0=ALU.mult, op1=ALU.add).then_inc(dec_step, 1)
                dve.tensor_reduce(gate[:, cols], ps[:, :, 2:5], AX.X, ALU.add).then_inc(slot_ready, 1)
                dve.wait_ge(dec_step, n * 2 + 2)
                dve.tensor_scalar(sidx[:, cols], dec[:, 1, :], spare_row[:, 0:1], None, ALU.add).then_inc(slot_ready, 1)

            def one_hots(pas, g):
                n = g + PASS_GROUPS * pas
                dve.wait_ge(cur_copied, n * 2 + 2)
                if not (isinstance(n, int) and n == 0):
                    dve.wait_ge(slot_ps, n)
                for t in range(TT):
                    dve.tensor_tensor(onehot[:, t, :, :], rcur[:, t, :].unsqueeze(2).to_broadcast([P, GRP, P]),
                                      slots[:, pas, :].unsqueeze(1).to_broadcast([P, GRP, P]),
                                      ALU.is_equal).then_inc(onehot_ready, 1)

            def copy_xT(n):
                dve.wait_ge(xT_ps, n + 1)
                dve.tensor_copy(XTH[:, 4:8, :].rearrange("p k n -> p (k n)"), bank(1)).then_inc(xT_ready, 1)
                dve.wait_ge(xT_ready, n * 3 + 1)
                for h, b in ((1, 1), (0, 0)):
                    if h == 0:
                        dve.wait_ge(xhi_ready, n + 1)
                    dve.tensor_tensor(XTL[:, 4 * h:4 * h + 4, :].rearrange("p k n -> p (k n)"), bank(b),
                                      XTH[:, 4 * h:4 * h + 4, :].rearrange("p k n -> p (k n)").bitcast(F32),
                                      ALU.subtract).then_inc(xT_ready, 1)

            def hidden(n, i, u):
                dve.wait_ge(sg_ready, n + 1)
                dve.scalar_tensor_tensor(out=HID[:, u % 2, :].rearrange("p (c q) -> p q c", c=FT),
                                         in0=SG[:, u % 2, :].rearrange("p (q c) -> p q c", c=FT),
                                         scalar=gate[:, bass.ds(i * GRP + u, 1)],
                                         in1=PS[:, 2 + u % 2, FE:2 * FE].rearrange("p (q c) -> p q c", c=FT),
                                         op0=ALU.mult, op1=ALU.mult).then_inc(hid_ready, 1)

            def hidden_low(n):
                dve.wait_ge(hidT_high, n + 1)
                dve.tensor_tensor(HTL[:].rearrange("p c n -> p (c n)"), PS[:, 6, 0:FE],
                                  HTH[:].rearrange("p c n -> p (c n)").bitcast(F32),
                                  ALU.subtract).then_inc(hidT_low, 1)

            def group(pas, i, last=False):
                for u in range(GRP):
                    n = number(pas, i, u)
                    if not (last and u >= 2):
                        for g in range(EARLY):
                            split_lo(n + 2, u + 2, g)
                    if not (last and u == 3):
                        hidden(n + 1, i, u + 1)
                    hidden_low(n)
                    if not (last and u >= 2):
                        copy_xT(n + 2)
                        for g in range(EARLY, NSP):
                            split_lo(n + 2, u + 2, g)
                    if u == 1 and not last:
                        one_hots(pas, i + AHEAD)
                    if u == 2 and not last:
                        decode(pas, i + AHEAD)
                    dve.wait_ge(expert_done, n + 1)
                    if u >= 2:
                        dve.wait_ge(scattered[u % 2], (i * 2 + (32 * pas + 1)) * 16)
                    elif not (isinstance(i, int) and i == 0 and pas == 0):
                        dve.wait_ge(scattered[u % 2], (i * 2 + 32 * pas) * 16)
                    dve.tensor_copy(YS[:, u % 2, 512:1024], bank(5)).then_inc(y_ready, 1)

            def run_pass(pas):
                n = NE * pas
                for g in range(AHEAD):
                    one_hots(pas, g)
                    decode(pas, g)
                dve.wait_ge(slot_ready, (PASS_GROUPS * pas + 2) * 3)
                for g in range(0 if pas else 1, NSP):
                    split_lo(n, 0, g)
                copy_xT(n)
                for g in range(EARLY):
                    split_lo(n + 1, 1, g)
                hidden(n, 0, 0)
                copy_xT(n + 1)
                for g in range(EARLY, NSP):
                    split_lo(n + 1, 1, g)
                group(pas, 0)
                with dve.Fori(1, NGRP - 1) as i:
                    dve.wait_ge(slot_ready, (i + (PASS_GROUPS * pas + 2)) * 3)
                    group(pas, i)
                dve.wait_ge(slot_ready, (NGRP - 1 + PASS_GROUPS * pas + 2) * 3)
                group(pas, NGRP - 1, last=True)

            run_pass(0)
            over = dve.value_load(oflag[0:1, 0:1], min_val=0, max_val=1)
            with dve.If(over > 0):
                run_pass(1)
            with dve.Else():
                dve.nop()

            dve.wait_ge(modrow_ready, 8)
            for t in range(TT):
                dve.wait_ge(y_loaded[t], 16)
                link(dve.tensor_tensor(SH[:, t, :], ring[:, t, 0:D], MOD[:, 5 * D:6 * D], ALU.mult))
                link(dve.tensor_tensor(X[:, t, :], X[:, t, :], SH[:, t, :], ALU.add), fin_ss)
            for t in range(TT):
                dve.wait_ge(ss_ready, 2 * TT + t + 1)
                link(dve.tensor_scalar(small[:, 2 + t:3 + t], small[:, t:t + 1], 1.0 / D, EPS, ALU.mult, ALU.add),
                     fin_ms)
                dve.wait_ge(fin_std, t + 1)
                link(dve.reciprocal(small[:, 8 + t:9 + t], small[:, 4 + t:5 + t]))
                link(dve.scalar_tensor_tensor(out=X[:, t, :], in0=X[:, t, :], scalar=small[:, 8 + t:9 + t],
                                              in1=gfin[:], op0=ALU.mult, op1=ALU.mult), out_ready)

        @block.tensor
        def _(pe):
            pe.wait_ge(consts, 1)
            pe.wait_ge(params_in, 16 * 5)
            pe.transpose(PS[:, 7, 0:R_END], prm, ident[0:R_END, 0:R_END]).then_inc(prm_ps, 1)
            pe.wait_ge(xn_ready, TT)
            for k in range(KD):
                for t in range(TT):
                    m = pe.transpose(PS[:, 2 + k // 2, (k % 2) * TOK + t * P:(k % 2) * TOK + t * P + P],
                                     XN[:, t, k * P:(k + 1) * P], ident[:])
            m.then_inc(xnT_ps, 1)
            for j in range(2 * KD):
                if j * P < 2 * PIECE:
                    pe.wait_ge(ada_acc, j * P // PIECE + 1)
                else:
                    pe.wait_ge(ada2_used, 1)
                m = pe.matmul(PS[:, 0, j:j + 1], MOD[:, j * P:(j + 1) * P], ones[:, 0:1], start=True, stop=True)
            m.then_inc(modcol_ps, 1)

            n3 = load_no(I, 3)
            pe.wait_ge(in3_late, 16)
            w3 = ring[:, slot_of(n3), 0:KD * LASTP].rearrange("p (k n) -> p k n", k=KD)
            for k in range(KD):
                pe.wait_ge(h1_ready, k + 1)
                m = pe.matmul(PS[0:NH, 7, 128:128 + TOK], w3[:, k, PIECE:PIECE + NH], hT[:, k, :],
                              start=(k == 0), stop=(k == KD - 1))
            m.then_inc(dtrow_ps, 1)

            def dt_transposes():
                pe.wait_ge(dtrow_ready, 1)
                for t in range(TT):
                    m = pe.transpose(PS[:, 7, t * NH:(t + 1) * NH], DTROW[:, t * P:(t + 1) * P], ident[0:NH, 0:NH])
                m.then_inc(dt_ps, 1)

            def project(q):
                m = ORDER[q]
                n = load_no(I, m // 6)
                if q % 6 == 0 and q or q == 3:
                    pe.wait_ge(loaded[slot_of(n)], loaded_count(n))
                width = LASTP if m // 6 == 3 else PIECE
                w = ring[:, slot_of(n), 0:KD * width].rearrange("p (k n) -> p k n", k=KD)
                if q >= QB:
                    pe.wait_ge(proj_evac, q - QB + 1)
                for k in range(KD):
                    mm = pe.matmul(PS[:, 2 + q % QB, 0:TOK], w[:, k, (m % 6) * P:(m % 6) * P + P], hT[:, k, :],
                                   start=(k == 0), stop=(k == KD - 1))
                mm.then_inc(proj_mm, 1)

            def cs_cols():
                pe.wait_ge(a_ready, 1)
                for t in range(TT):
                    pe.matmul(PS[:, 7, 32 + t * NH:32 + (t + 1) * NH], tri[:], dtv[:, 9, t * NH:(t + 1) * NH],
                              start=True, stop=True)
                pe.matmul(PS[:, 7, 48:48 + NH], ones[:], dtv[:, 9, 0:NH], start=True, stop=True).then_inc(cs_ps, 1)

            def xs_transposes():
                pe.wait_ge(xbc_ready, XB)
                for t in range(TT):
                    for b in range(CBLK):
                        m = pe.transpose(PS[:, t, b * P:(b + 1) * P], XC[:, b, t * P:(t + 1) * P], ident[:])
                m.then_inc(xsT_ps, 1)

            def cs_rows(t):
                if t == 0:
                    pe.wait_ge(dtx_ready, TT)
                else:
                    pe.wait_ge(csrow_used, t)
                for half in range(2):
                    m = pe.matmul(bank(half), ones[:], AB[:, t, 4 * half:4 * half + 4, :], start=True, stop=True)
                m.then_inc(csrow_ps, 1)

            def c_dot_b():
                pe.wait_ge(csrow_used, TT)
                for g in range(NG):
                    pe.matmul(PS[:, g, 0:2 * P], XC[:, 4 + g, 0:P], XC[:, 6 + g, 0:2 * P], start=True, stop=True)
                    m = pe.matmul(PS[:, g, 2 * P:3 * P], XC[:, 4 + g, P:2 * P], XC[:, 6 + g, P:2 * P],
                                  start=True, stop=True)
                m.then_inc(cb_ps, 1)

            def y_heads():
                pe.wait_ge(wts_ready, 3 * NG)
                for h in range(NH):
                    b, r = h // 2, (h % 2) * HD
                    c0 = (b % 2) * TOK
                    lhs = [DTX[:, t, h * HD:(h + 1) * HD] for t in range(TT)]
                    pe.matmul(PS[r:r + HD, b // 2, c0:c0 + TOK], lhs[0], E[:, 0:2, h, :], start=True, stop=False)
                    m = pe.matmul(PS[r:r + HD, b // 2, c0 + P:c0 + TOK], lhs[1], E[:, 2, h, :], start=False, stop=True)
                m.then_inc(y_ps, 1)

            def y_squares():
                pe.wait_ge(sq_ready, 1)
                for b in range(CBLK):
                    m = pe.matmul(PS[:, 7, 0:TOK], ones[:], SQ[:, b, :], start=(b == 0), stop=(b == CBLK - 1))
                m.then_inc(yss_ps, 1)

            for q in range(NQ):
                project(q)
                if q == 0:
                    dt_transposes()
                if q == 5:
                    cs_cols()
                if q == 13:
                    xs_transposes()
                if q == 15:
                    cs_rows(0)
                if q == 16:
                    cs_rows(1)
                if q == 17:
                    c_dot_b()
                if q == 19:
                    y_heads()
                if q == 21:
                    y_squares()

            def mod_rows(r):
                c0 = 2 * D + 512 * r
                pe.wait_ge(ada_acc, (c0 + 512 + PIECE - 1) // PIECE)
                if r >= 2:
                    pe.wait_ge(modrow_ready, r - 1)
                dst = bank(r % 2 if r < 6 else 2 + r % 2)
                pe.matmul(dst, ones[:], MOD[:, c0:c0 + 512], start=True, stop=True).then_inc(modrow_ps, 1)

            pe.wait_ge(y_used, CBLK)
            for r in range(6):
                mod_rows(r)

            def h2_transposes(t):
                pe.wait_ge(x2_ready, 2 * t + 2)
                pe.wait_ge(h2_ready, t + 1)
                for k in range(KD):
                    m = pe.transpose(PS[:, 2 + 2 * t + k // 4, (k % 4) * P:(k % 4) * P + P],
                                     H2P[:, t, k * P:(k + 1) * P], ident[:])
                m.then_inc(h2T_ps, 1)

            def logits(t):
                pe.wait_ge(h2T_ready, t + 1)
                for k in range(KD):
                    m = pe.matmul(PS[:, 7, t * NE:(t + 1) * NE], hT[:, k, t * P:(t + 1) * P], WR[:, k, :],
                                  start=(k == 0), stop=(k == KD - 1))
                m.then_inc(logit_ps, 1)

            pe.wait_ge(yb_ready, CBLK)
            pe.wait_ge(proj_evac, NQ)
            for j in range(2):
                n = load_no(O, j)
                pe.wait_ge(loaded[slot_of(n)], loaded_count(n))
            for t in range(TT):
                for h in range(2):
                    for place, k in enumerate(OUT_ORDER):
                        j = 0 if k < OUT_K[0][1] else 1
                        n = load_no(O, j)
                        if t == 0 and h == 0 and k < CBLK:
                            pe.wait_ge(ya_ready, place - CBLK + 1)
                        w = ring[:, slot_of(n), 0:6 * D].rearrange("p (k n) -> p k n", n=D)
                        m = pe.matmul(bank(2 + 2 * t + h), YC[:, k, t * P:(t + 1) * P],
                                      w[:, k - OUT_K[j][0], 512 * h:512 * h + 512],
                                      start=(place == 0), stop=(place == KD - 1))
                    m.then_inc(mix_ps, 1)
                    if (t, h) == (1, 0):
                        h2_transposes(0)

            def shared_gate_up(t, ks):
                for k in ks:
                    m = pe.matmul(bank(t).rearrange("p (a n) -> p a n", a=2), hT[:, k, t * P:(t + 1) * P],
                                  gu_w(slot_of(ns))[:, :, k, :], start=(k == 0), stop=(k == KD - 1))
                if ks[-1] == KD - 1:
                    m.then_inc(sgu_ps, 1)

            def down(n, u):
                s = e_slot(u)
                for cc in range(FT):
                    pe.matmul(bank(4), HTT[:, cc, :], down_w(s)[:, cc, 0:512], start=(cc == 0), stop=(cc == FT - 1))
                pe.wait_ge(dlo_ready, n + 1)
                pe.wait_ge(hidT_low, n + 1)
                for cc in range(FT):
                    pe.matmul(bank(5), HTH[:, cc, :], DHI[:, cc, :], start=(cc == 0), stop=False)
                    pe.matmul(bank(5), HTH[:, cc, :], down_half(ringr, s)[:, cc, :], start=False, stop=False)
                    m = pe.matmul(bank(5), HTL[:, cc, :], DHI[:, cc, :], start=False, stop=(cc == FT - 1))
                return m

            def slot_values(pas, g):
                n = g + PASS_GROUPS * pas
                pe.wait_ge(onehot_ready, n * 2 + 2)
                if not (isinstance(n, int) and n == 0):
                    pe.wait_ge(slot_ready, n * 3)
                else:
                    pe.wait_ge(table_ready, 1)
                for e in range(GRP):
                    for t in range(TT):
                        m = pe.matmul(PS[:, 7, e * NCOL:(e + 1) * NCOL], onehot[:, t, e, :], rtcur[:, t, e, :],
                                      start=(t == 0), stop=(t == TT - 1))
                m.then_inc(slot_ps, 1)

            def hidden_transposes(b):
                for cc in range(FT):
                    m = pe.transpose(PS[:, 6, cc * P:(cc + 1) * P], HID[:, b, cc * P:(cc + 1) * P], ident[:])
                return m

            def shared_hidden_transposes(t):
                pe.wait_ge(shid_ready, t + 1)
                hidden_transposes(t).then_inc(shT_ps, 1)

            def shared_down(t):
                if t:
                    pe.wait_ge(sh_ready, t)
                pe.wait_ge(shT_ready, t + 1)
                w = down_w(slot_of(ns))
                for h in range(2):
                    for cc in range(FT):
                        m = pe.matmul(bank(4 + h), HTT[:, cc, :], w[:, cc, 512 * h:512 * h + 512],
                                      start=(cc == 0), stop=(cc == FT - 1))
                m.then_inc(sy_ps, 1)

            ns = load_no(S, 0)
            pe.wait_ge(gains_in, 16 * 3)
            pe.wait_ge(modrow_ready, 6)
            logits(0)
            pe.wait_ge(loaded[slot_of(ns)], loaded_count(ns))
            shared_gate_up(0, range(0, 5))
            h2_transposes(1)
            shared_gate_up(0, range(5, KD))
            for r in range(6, 8):
                mod_rows(r)
            logits(1)
            shared_hidden_transposes(0)
            shared_gate_up(1, range(KD))
            shared_down(0)
            pe.wait_ge(mask_ready, 1)
            pe.wait_ge(score_ready, 1)
            pe.matmul(PS[:, 7, 0:NE], trib[:], maskb[:, 0, :], start=True, stop=True)
            pe.matmul(PS[:, 7, NE:2 * NE], trib[:], maskb[:, 1, :], start=True, stop=False)
            pe.matmul(PS[:, 7, NE:2 * NE], onesb[:], maskb[:, 0, :], start=False, stop=True)
            pe.matmul(PS[:, 7, 2 * NE:3 * NE], onesb[:], maskb[:, 0, :], start=True, stop=False)
            pe.matmul(PS[:, 7, 2 * NE:3 * NE], onesb[:], maskb[:, 1, :], start=False, stop=True).then_inc(rank_ps, 1)
            shared_hidden_transposes(1)
            shared_down(1)
            for g in range(AHEAD):
                slot_values(0, g)

            def transposes(pas, i, u):
                n = number(pas, i, u)
                b = u % 2
                pe.wait_ge(gathered[b], (i * 2 + (32 * pas + u // 2 + 1)) * 16)
                if not (isinstance(n, int) and n == 0):
                    pe.wait_ge(xT_ready, n * 3)
                else:
                    pe.wait_ge(shid_ready, TT)
                for k in range(KD):
                    m = pe.transpose(PS[:, k // 4, (k % 4) * P:(k % 4) * P + P], HG[:, b, k * P:(k + 1) * P], ident[:])
                m.then_inc(xT_ps, 1)

            def expert_gate_up(pas, i, u):
                n = number(pas, i, u)
                pe.wait_ge(xT_ready, n * 3 + 3)
                ps = bank(2 + u % 2).rearrange("p (a n) -> p a n", a=2)
                for g, (k0, k1) in enumerate(SPLITS):
                    pe.wait_ge(wlo_ready, n * NSP + (g + 1))
                    for k in range(k0, k1):
                        pe.matmul(ps, XTH[:, k, :], WHI[g][:, k - k0, :, :], start=(k == 0), stop=False)
                        pe.matmul(ps, XTH[:, k, :], WLO[g][:, k - k0, :, :], start=False, stop=False)
                        m = pe.matmul(ps, XTL[:, k, :], WHI[g][:, k - k0, :, :], start=False, stop=(k == KD - 1))
                    m.then_inc(split_used, 1)

            def group(pas, i, last=False):
                for u in range(GRP):
                    n = number(pas, i, u)
                    if not (last and u == 3):
                        if not (isinstance(n, int) and n == 0):
                            pe.wait_ge(hid_ready, n)
                        expert_gate_up(pas, i, u + 1)
                    pe.wait_ge(hid_ready, n + 1)
                    if not (isinstance(n, int) and n == 0):
                        pe.wait_ge(hidT_low, n)
                    hidden_transposes(u % 2).then_inc(hidT_ps, 1)
                    if not (last and u >= 2):
                        transposes(pas, i, u + 2)
                    if u == 2 and not last:
                        slot_values(pas, i + AHEAD)
                    pe.wait_ge(hidT_ready, n + 1)
                    if isinstance(n, int) and n == 0:
                        pe.wait_ge(sh_ready, TT)
                    else:
                        pe.wait_ge(y_ready, n * 2)
                    pe.wait_ge(down_loaded[e_slot(u)], down_count(n, u))
                    down(n, u).then_inc(expert_done, 1)

            def run_pass(pas):
                if pas:
                    for g in range(AHEAD):
                        slot_values(pas, g)
                transposes(pas, 0, 0)
                expert_gate_up(pas, 0, 0)
                transposes(pas, 0, 1)
                group(pas, 0)
                with pe.Fori(1, NGRP - 1) as i:
                    group(pas, i)
                group(pas, NGRP - 1, last=True)

            run_pass(0)
            over = pe.value_load(oflag[0:1, 0:1], min_val=0, max_val=1)
            with pe.If(over > 0):
                run_pass(1)
            with pe.Else():
                pe.nop()


_INS = ["x", "c", "w_ada", "b_ada", "norm_mix_g", "w_in", "conv_a_w", "ssm_conv_w", "ssm_conv_b", "ssm_dt_bias",
        "ssm_a_log", "ssm_d", "ssm_norm_g", "w_out", "norm_ffn_g", "w_router", "router_bias", "we_gate", "we_up",
        "we_down", "ws_gate", "ws_up", "ws_down", "norm_final_g"]
_OUTS = [((1, 256, 1024), "float32")]


def kernel(**inputs):
    import numpy as _np
    import concourse.bacc as _bacc
    from concourse import mybir as _mybir
    from concourse.bass_utils import run_bass_kernel_spmd as _run

    nc = _bacc.Bacc("TRN2", target_bir_lowering=False, num_devices=1)
    arrays, args = {}, []
    for name in _INS:
        a = _np.ascontiguousarray(inputs[name])
        arrays[f"in_{name}_dram"] = a
        args.append(nc.dram_tensor(f"in_{name}_dram", a.shape, _mybir.dt.from_np(a.dtype), kind="ExternalInput").ap())
    for i, (shape, dtype) in enumerate(_OUTS):
        dt = _mybir.dt.from_np(_np.dtype(dtype))
        args.append(nc.dram_tensor(f"out_{i}_dram", shape, dt, kind="ExternalOutput").ap())
    build(nc, *args)
    r = _run(nc, [arrays], core_ids=[0])
    return r.results[0]["out_0_dram"]
```
